# Optimizing a Trainium2 kernel written in Bass

```python
import jax, jax.numpy as jnp
from jax import lax
import numpy as np
import math

D_MODEL = 1024
BATCH = 1
SEQ = 512
DEPTH = 2

HG_WIDTH = D_MODEL // 2
HG_DK = 128
HG_HEADS = HG_WIDTH // HG_DK
HG_CHUNK = 64
RW_WIDTH = D_MODEL // 2
RW_HEAD = 64
RW_HEADS = RW_WIDTH // RW_HEAD
RW_DECAY_RANK = 64
RW_ICL_RANK = 64
RW_VRES_RANK = 32
N_BRANCH = 2
HG_COLS = 4 * HG_WIDTH
RW_COLS = 4 * RW_WIDTH + RW_DECAY_RANK + RW_ICL_RANK
GATE_COLS = N_BRANCH * D_MODEL
N_IN = HG_COLS + RW_COLS + GATE_COLS
DN_ALPHA = (2 * DEPTH) ** 0.25
DN_BETA = (8 * DEPTH) ** -0.25
LN_EPS = 1e-5
RMS_EPS = 1e-6
GN_EPS = 64e-5
L2_EPS = 1e-12
LB_FLOOR = 1e-30


def layer_norm(x, g, b):
    xf = x.astype(jnp.float32)
    mu = xf.mean(-1, keepdims=True)
    var = jnp.mean(jnp.square(xf - mu), -1, keepdims=True)
    return ((xf - mu) * lax.rsqrt(var + LN_EPS)).astype(x.dtype) * g + b

def heads(t, n):
    return t.reshape(t.shape[:-1] + (-1, n))

def token_shift(p, mu):
    prev = jnp.pad(p[:, :-1], ((0, 0), (1, 0), (0, 0)))
    return p + (prev - p) * mu

def hgrn2_chunked(q, k, v, log_f):
    B, T, H, K = q.shape
    V = v.shape[-1]
    C = HG_CHUNK
    N = T // C

    def to_chunks(a):
        return a.reshape(B, N, C, H, a.shape[-1]).transpose(1, 0, 3, 2, 4)

    qc, kc, vc, gc = (to_chunks(a) for a in (q, k, v, log_f))
    causal = jnp.tril(jnp.ones((C, C), dtype=bool))[:, :, None]

    def step(S, inp):
        qi, ki, vi, gi = inp
        b = jnp.cumsum(gi, axis=2)
        diff = b[:, :, :, None, :] - b[:, :, None, :, :]
        decay = jnp.where(causal, jnp.exp(jnp.where(causal, diff, 0.0)), 0.0)
        scores = jnp.einsum('bhtk,bhtsk,bhsk->bhts', qi, decay, ki)
        o = (jnp.einsum('bhts,bhsv->bhtv', scores, vi)
             + jnp.einsum('bhtk,bhkv->bhtv', qi * jnp.exp(b), S))
        b_last = b[:, :, -1:, :]
        S = (jnp.exp(b_last[:, :, 0, :])[..., None] * S
             + jnp.einsum('bhsk,bhsv->bhkv', ki * jnp.exp(b_last - b), vi))
        return S, o

    S0 = jnp.zeros((B, H, K, V), q.dtype)
    _, o = lax.scan(step, S0, (qc, kc, vc, gc))
    return o.transpose(1, 0, 3, 2, 4).reshape(B, T, H, V)

def rwkv7_scan(r, w, k, v, kk, a):
    B, T, H, N = r.shape

    def step(S, inp):
        r_t, w_t, k_t, v_t, kk_t, a_t = inp
        sa = jnp.einsum('bhvk,bhk->bhv', S, -kk_t)
        S = (S * w_t[:, :, None, :] + sa[..., None] * (kk_t * a_t)[:, :, None, :]
             + v_t[..., None] * k_t[:, :, None, :])
        y = jnp.einsum('bhvk,bhk->bhv', S, r_t)
        return S, y

    xs = tuple(jnp.moveaxis(t, 1, 0) for t in (r, w, k, v, kk, a))
    S0 = jnp.zeros((B, H, N, N), r.dtype)
    _, y = lax.scan(step, S0, xs)
    return jnp.moveaxis(y, 0, 1)

def first_inputs(seed: int = 0) -> dict:
    key = jax.random.key(seed)
    ks = iter(jax.random.split(key, 32))
    nrm = lambda shape, s: jax.random.normal(next(ks), shape, jnp.float32) * s
    uni = lambda shape, lo, hi: jax.random.uniform(next(ks), shape, jnp.float32, lo, hi)
    return {
        "x": nrm((BATCH, SEQ, D_MODEL), 1.0),
        "c": nrm((BATCH, D_MODEL), 1.0),
        "w_ada": nrm((DEPTH, D_MODEL, 3 * D_MODEL), 0.1 * D_MODEL ** -0.5),
        "b_ada": nrm((DEPTH, 3 * D_MODEL), 0.01),
        "w_in": nrm((DEPTH, D_MODEL, N_IN), D_MODEL ** -0.5),
        "hg_lower_bounds": nrm((DEPTH, HG_WIDTH), 0.5),
        "hg_norm_g": 1.0 + nrm((DEPTH, HG_WIDTH), 0.01),
        "rw_mu": uni((DEPTH, RW_COLS), 0.0, 1.0),
        "rw_w0": uni((DEPTH, RW_WIDTH), -6.0, 0.0),
        "rw_w_up": nrm((DEPTH, RW_DECAY_RANK, RW_WIDTH), 0.1 * RW_DECAY_RANK ** -0.5),
        "rw_a0": nrm((DEPTH, RW_WIDTH), 0.1),
        "rw_a_up": nrm((DEPTH, RW_ICL_RANK, RW_WIDTH), 0.1 * RW_ICL_RANK ** -0.5),
        "rw_k_k": 0.85 + nrm((DEPTH, RW_WIDTH), 0.02),
        "rw_k_a": 1.0 + nrm((DEPTH, RW_WIDTH), 0.02),
        "rw_r_k": nrm((DEPTH, RW_HEADS, RW_HEAD), 0.1),
        "rw_v0": 1.0 + nrm((DEPTH - 1, RW_WIDTH), 0.1),
        "rw_v_down": nrm((DEPTH - 1, D_MODEL, RW_VRES_RANK), D_MODEL ** -0.5),
        "rw_v_up": nrm((DEPTH - 1, RW_VRES_RANK, RW_WIDTH), 0.1 * RW_VRES_RANK ** -0.5),
        "rw_gn_g": 1.0 + nrm((DEPTH, RW_WIDTH), 0.01),
        "rw_gn_b": nrm((DEPTH, RW_WIDTH), 0.01),
        "w_branch_hg": nrm((DEPTH, HG_WIDTH, D_MODEL), DN_BETA * HG_WIDTH ** -0.5),
        "w_branch_rw": nrm((DEPTH, RW_WIDTH, D_MODEL), DN_BETA * RW_WIDTH ** -0.5),
        "w_out": nrm((DEPTH, D_MODEL, D_MODEL), DN_BETA * D_MODEL ** -0.5),
        "ln_g": 1.0 + nrm((DEPTH, D_MODEL), 0.01),
        "ln_b": nrm((DEPTH, D_MODEL), 0.01),
    }

def first_block(x, c, w_ada, b_ada, w_in, hg_lower_bounds, hg_norm_g, rw_mu, rw_w0, rw_w_up,
              rw_a0, rw_a_up, rw_k_k, rw_k_a, rw_r_k, rw_v0, rw_v_down, rw_v_up, rw_gn_g, rw_gn_b,
              w_branch_hg, w_branch_rw, w_out, ln_g, ln_b):
    f32 = jnp.float32
    B, T, _ = x.shape
    lb_soft = jax.nn.softmax(hg_lower_bounds.astype(f32), axis=0)
    lower_bounds = jnp.cumsum(lb_soft, axis=0) - lb_soft[0]
    v_first = None
    for l in range(DEPTH):
        cond = jax.nn.silu(c) @ w_ada[l] + b_ada[l]
        shift, scale, gate_raw = jnp.split(cond, 3, axis=-1)
        h = x * (1.0 + scale[:, None]) + shift[:, None]
        proj = h @ w_in[l]
        p_hg, p_rw, p_gate = jnp.split(proj, [HG_COLS, HG_COLS + RW_COLS], axis=-1)

        p_hg = p_hg.astype(f32)
        q, f_pre, i_val, z_hg = jnp.split(p_hg, 4, axis=-1)
        lb = lower_bounds[l]
        log_f = jnp.logaddexp(jnp.log(jnp.maximum(lb, LB_FLOOR)),
                              jnp.log1p(-lb) + jax.nn.log_sigmoid(f_pre))
        k_hg = (1.0 - lb) * jax.nn.sigmoid(-f_pre)
        o_hg = hgrn2_chunked(heads(q, HG_DK), heads(k_hg, HG_DK), heads(i_val, HG_DK), heads(log_f, HG_DK))
        o_hg = o_hg * lax.rsqrt(jnp.mean(jnp.square(o_hg), -1, keepdims=True) + RMS_EPS)
        o_hg = o_hg.reshape(B, T, HG_WIDTH) * hg_norm_g[l] * jax.nn.silu(z_hg)
        y_hg = o_hg.astype(x.dtype) @ w_branch_hg[l]

        p_rw = token_shift(p_rw.astype(f32), rw_mu[l])
        r, k, v, z_rw, w_down, a_down = jnp.split(
            p_rw, [RW_WIDTH, 2 * RW_WIDTH, 3 * RW_WIDTH, 4 * RW_WIDTH, 4 * RW_WIDTH + RW_DECAY_RANK], axis=-1)
        w_raw = -jax.nn.softplus(-(rw_w0[l] + jnp.tanh(w_down) @ rw_w_up[l])) - 0.5
        decay = jnp.exp(-jnp.exp(w_raw))
        if l == 0:
            v_first = v
        else:
            v_mix = jax.nn.sigmoid(rw_v0[l - 1] + (h.astype(f32) @ rw_v_down[l - 1]) @ rw_v_up[l - 1])
            v = v + (v_first - v) * v_mix
        a = jax.nn.sigmoid(rw_a0[l] + a_down @ rw_a_up[l])
        kk = heads(k * rw_k_k[l], RW_HEAD)
        kk = kk / jnp.maximum(jnp.sqrt(jnp.sum(jnp.square(kk), -1, keepdims=True)), L2_EPS)
        k = k * (1.0 + (a - 1.0) * rw_k_a[l])
        r_h, k_h, v_h = heads(r, RW_HEAD), heads(k, RW_HEAD), heads(v, RW_HEAD)
        y_rw = rwkv7_scan(r_h, heads(decay, RW_HEAD), k_h, v_h, kk, heads(a, RW_HEAD))
        mu = y_rw.mean(-1, keepdims=True)
        var = jnp.mean(jnp.square(y_rw - mu), -1, keepdims=True)
        y_rw = ((y_rw - mu) * lax.rsqrt(var + GN_EPS)).reshape(B, T, RW_WIDTH) * rw_gn_g[l] + rw_gn_b[l]
        bonus = jnp.sum(r_h * k_h * rw_r_k[l], -1, keepdims=True) * v_h
        y_rw = (y_rw + bonus.reshape(B, T, RW_WIDTH)) * jax.nn.silu(z_rw)
        y_rw = y_rw.astype(x.dtype) @ w_branch_rw[l]

        g_hg, g_rw = jnp.split(p_gate, N_BRANCH, axis=-1)
        merged = jax.nn.sigmoid(g_hg) * y_hg + jax.nn.sigmoid(g_rw) * y_rw
        out = merged @ w_out[l]
        x = layer_norm(DN_ALPHA * x + (1.0 + gate_raw[:, None]) * out, ln_g[l], ln_b[l])
    return x


N_MIXERS = 2
N_LRU = (DEPTH + 1) // 2
N_RET = DEPTH // 2

D_RNN = 3 * D_MODEL // 2
N_GATE_BLOCKS = 16
BLOCK_W = D_RNN // N_GATE_BLOCKS
CONV_W = 4
C_RG = 8.0

RET_HEADS = D_MODEL // 256
QK_HEAD = 256
V_HEAD = 2 * QK_HEAD
QK_DIM = RET_HEADS * QK_HEAD
V_DIM = RET_HEADS * V_HEAD
CHUNK = 128
ROPE_BASE = 10000.0

GN_EPS_2 = 1e-5


def rms_norm(x, g):
    xf = x.astype(jnp.float32)
    y = xf * lax.rsqrt(jnp.mean(xf * xf, axis=-1, keepdims=True) + RMS_EPS)
    return (y * g.astype(jnp.float32)).astype(x.dtype)

def causal_depthwise_conv(x, w, b):
    s = x.shape[1]
    xp = jnp.pad(x, ((0, 0), (CONV_W - 1, 0), (0, 0)))
    y = b
    for k in range(CONV_W):
        y = y + xp[:, k:k + s] * w[k]
    return y

def _lin_rec_combine(e1, e2):
    a1, b1 = e1
    a2, b2 = e2
    return a1 * a2, a2 * b1 + b2

def rglru_mixer(h, w_in, conv_w, conv_b, w_a, b_a, w_x, b_x, lam, w_out):
    bsz, s, _ = h.shape
    u = h @ w_in
    xb, gate = u[..., :D_RNN], u[..., D_RNN:]
    xb = causal_depthwise_conv(xb, conv_w, conv_b)
    xblk = xb.reshape(bsz, s, N_GATE_BLOCKS, BLOCK_W)
    r = jax.nn.sigmoid(jnp.einsum('bsnc,ncd->bsnd', xblk, w_a).reshape(bsz, s, D_RNN) + b_a)
    i = jax.nn.sigmoid(jnp.einsum('bsnc,ncd->bsnd', xblk, w_x).reshape(bsz, s, D_RNN) + b_x)
    log_a = -C_RG * r.astype(jnp.float32) * jax.nn.softplus(-lam.astype(jnp.float32))
    a = jnp.exp(log_a)
    bt = jnp.sqrt(-jnp.expm1(2.0 * log_a)) * (i * xb).astype(jnp.float32)
    _, hseq = lax.associative_scan(_lin_rec_combine, (a, bt), axis=1)
    y = hseq.astype(h.dtype) * jax.nn.silu(gate)
    return y @ w_out

def apply_rotary(x, cos, sin):
    half = x.shape[-1] // 2
    x1, x2 = x[..., :half], x[..., half:]
    c = cos[None, :, None, :]
    s_ = sin[None, :, None, :]
    return jnp.concatenate([x1 * c - x2 * s_, x2 * c + x1 * s_], axis=-1)

def retention_mixer(h, w_in, w_out, cos, sin):
    bsz, s, _ = h.shape
    n_chunks = s // CHUNK
    u = h @ w_in
    q = u[..., :QK_DIM].reshape(bsz, s, RET_HEADS, QK_HEAD).astype(jnp.float32)
    k = u[..., QK_DIM:2 * QK_DIM].reshape(bsz, s, RET_HEADS, QK_HEAD).astype(jnp.float32)
    v = u[..., 2 * QK_DIM:2 * QK_DIM + V_DIM].reshape(bsz, s, RET_HEADS, V_HEAD).astype(jnp.float32)
    gate = u[..., 2 * QK_DIM + V_DIM:]
    q = apply_rotary(q, cos, sin)
    k = apply_rotary(k, cos, sin) * (QK_HEAD ** -0.5)

    def to_chunks(t):
        return t.reshape(bsz, n_chunks, CHUNK, RET_HEADS, t.shape[-1]).transpose(1, 0, 3, 2, 4)

    qc, kc, vc = to_chunks(q), to_chunks(k), to_chunks(v)

    log_g = jnp.log(1.0 - jnp.exp2(-5.0 - jnp.arange(RET_HEADS, dtype=jnp.float32)))
    idx = jnp.arange(CHUNK, dtype=jnp.float32)
    diff = idx[:, None] - idx[None, :]
    dmask = jnp.where(diff[None] >= 0, jnp.exp(jnp.maximum(diff, 0.0)[None] * log_g[:, None, None]), 0.0)
    q_decay = jnp.exp((idx[None, :] + 1.0) * log_g[:, None])[..., None]
    k_decay = jnp.exp((CHUNK - 1.0 - idx[None, :]) * log_g[:, None])[..., None]
    chunk_decay = jnp.exp(CHUNK * log_g)[:, None, None]

    def step(state, inp):
        qi, ki, vi = inp
        scores = jnp.einsum('bhqd,bhkd->bhqk', qi, ki) * dmask
        inner = jnp.einsum('bhqk,bhke->bhqe', scores, vi)
        cross = jnp.einsum('bhqd,bhde->bhqe', qi * q_decay, state)
        new_state = state * chunk_decay + jnp.einsum('bhkd,bhke->bhde', ki * k_decay, vi)
        return new_state, inner + cross

    state0 = jnp.zeros((bsz, RET_HEADS, QK_HEAD, V_HEAD), jnp.float32)
    _, out = lax.scan(step, state0, (qc, kc, vc))
    out = out.transpose(1, 0, 3, 2, 4).reshape(bsz, s, RET_HEADS, V_HEAD)
    mu = jnp.mean(out, axis=-1, keepdims=True)
    var = jnp.mean(jnp.square(out - mu), axis=-1, keepdims=True)
    out = ((out - mu) * lax.rsqrt(var + GN_EPS_2)).reshape(bsz, s, V_DIM).astype(h.dtype)
    y = out * jax.nn.silu(gate)
    return y @ w_out

def second_inputs(seed: int = 0) -> dict:
    key = jax.random.key(seed)
    ks = jax.random.split(key, 16)
    f32 = jnp.float32

    def nrm(k, shape, fan_in):
        return jax.random.normal(k, shape, f32) * (fan_in ** -0.5)

    x = jax.random.normal(ks[0], (BATCH, SEQ, D_MODEL), f32)
    norm_pre = 1.0 + 0.05 * jax.random.normal(ks[1], (DEPTH, D_MODEL), f32)
    norm_post = 1.0 + 0.05 * jax.random.normal(ks[2], (DEPTH, D_MODEL), f32)
    lru_w_in = nrm(ks[3], (N_LRU, D_MODEL, 2 * D_RNN), D_MODEL)
    lru_conv_w = nrm(ks[4], (N_LRU, CONV_W, D_RNN), CONV_W)
    lru_conv_b = 0.02 * jax.random.normal(ks[5], (N_LRU, D_RNN), f32)
    lru_w_a = nrm(ks[6], (N_LRU, N_GATE_BLOCKS, BLOCK_W, BLOCK_W), BLOCK_W)
    lru_b_a = 0.02 * jax.random.normal(ks[7], (N_LRU, D_RNN), f32)
    lru_w_x = nrm(ks[8], (N_LRU, N_GATE_BLOCKS, BLOCK_W, BLOCK_W), BLOCK_W)
    lru_b_x = 0.02 * jax.random.normal(ks[9], (N_LRU, D_RNN), f32)
    a_c = jax.random.uniform(ks[10], (N_LRU, D_RNN), f32, minval=0.9, maxval=0.999)
    sig = a_c ** (1.0 / C_RG)
    lru_lambda = jnp.log(sig) - jnp.log1p(-sig)
    lru_w_out = nrm(ks[11], (N_LRU, D_RNN, D_MODEL), D_RNN)
    ret_w_in = nrm(ks[12], (N_RET, D_MODEL, 2 * QK_DIM + 2 * V_DIM), D_MODEL)
    ret_w_out = nrm(ks[13], (N_RET, V_DIM, D_MODEL), V_DIM)
    return {"x": x, "norm_pre": norm_pre, "norm_post": norm_post,
            "lru_w_in": lru_w_in, "lru_conv_w": lru_conv_w, "lru_conv_b": lru_conv_b,
            "lru_w_a": lru_w_a, "lru_b_a": lru_b_a, "lru_w_x": lru_w_x, "lru_b_x": lru_b_x,
            "lru_lambda": lru_lambda, "lru_w_out": lru_w_out,
            "ret_w_in": ret_w_in, "ret_w_out": ret_w_out}

def second_block(x, norm_pre, norm_post, lru_w_in, lru_conv_w, lru_conv_b, lru_w_a, lru_b_a,
              lru_w_x, lru_b_x, lru_lambda, lru_w_out, ret_w_in, ret_w_out):
    s = x.shape[1]
    pos = jnp.arange(s, dtype=jnp.float32)
    inv_freq = ROPE_BASE ** (-jnp.arange(0, QK_HEAD, 2, dtype=jnp.float32) / QK_HEAD)
    ang = pos[:, None] * inv_freq[None, :]
    cos, sin = jnp.cos(ang), jnp.sin(ang)
    for layer in range(DEPTH):
        h = rms_norm(x, norm_pre[layer])
        j = layer // N_MIXERS
        if layer % N_MIXERS == 0:
            o = rglru_mixer(h, lru_w_in[j], lru_conv_w[j], lru_conv_b[j], lru_w_a[j], lru_b_a[j],
                            lru_w_x[j], lru_b_x[j], lru_lambda[j], lru_w_out[j])
        else:
            o = retention_mixer(h, ret_w_in[j], ret_w_out[j], cos, sin)
        x = x + rms_norm(o, norm_post[layer])
    return x


def setup_inputs(seed=0):
    out = dict(first_inputs(seed))
    for name, value in second_inputs(seed + 1).items():
        if name != "x":
            out[name + "_2"] = value
    return out


def reference(
    x, c, w_ada, b_ada, w_in, hg_lower_bounds, hg_norm_g, rw_mu, rw_w0, rw_w_up, rw_a0, rw_a_up,
    rw_k_k, rw_k_a, rw_r_k, rw_v0, rw_v_down, rw_v_up, rw_gn_g, rw_gn_b, w_branch_hg,
    w_branch_rw, w_out, ln_g, ln_b, norm_pre_2, norm_post_2, lru_w_in_2, lru_conv_w_2,
    lru_conv_b_2, lru_w_a_2, lru_b_a_2, lru_w_x_2, lru_b_x_2, lru_lambda_2, lru_w_out_2,
    ret_w_in_2, ret_w_out_2,
):
    x = first_block(
        x, c, w_ada, b_ada, w_in, hg_lower_bounds, hg_norm_g, rw_mu, rw_w0, rw_w_up, rw_a0,
        rw_a_up, rw_k_k, rw_k_a, rw_r_k, rw_v0, rw_v_down, rw_v_up, rw_gn_g, rw_gn_b,
        w_branch_hg, w_branch_rw, w_out, ln_g, ln_b,
    )
    return second_block(
        x, norm_pre_2, norm_post_2, lru_w_in_2, lru_conv_w_2, lru_conv_b_2, lru_w_a_2,
        lru_b_a_2, lru_w_x_2, lru_b_x_2, lru_lambda_2, lru_w_out_2, ret_w_in_2, ret_w_out_2,
    )


_drawn_inputs = setup_inputs


def setup_inputs(seed=0):
    import zlib

    import numpy as np

    out = dict(_drawn_inputs(seed))
    spreads = {}
    factors = {'b_ada': 7.027,
     'hg_norm_g': 37.785,
     'rw_w_up': 8.0,
     'rw_a0': 8.0,
     'rw_a_up': 8.0,
     'rw_k_k': 33.297,
     'rw_k_a': 8.0,
     'rw_v0': 8.0,
     'rw_v_down': 8.0,
     'rw_v_up': 8.0,
     'rw_gn_g': 49.051,
     'rw_gn_b': 32.467,
     'lru_b_a_2': 8.0,
     'lru_b_x_2': 7.596}
    for name, (base, spread) in spreads.items():
        noise = np.random.default_rng([zlib.crc32(name.encode()), seed]).standard_normal(out[name].shape)
        drawn = base * np.exp(spread * noise) if base else spread * noise
        out[name] = __import__('jax').numpy.asarray(drawn.astype(out[name].dtype))
    for name, factor in factors.items():
        out[name] = (out[name] * factor).astype(out[name].dtype)
    return out
```

```python
import math
from contextlib import ExitStack

import numpy as np
import concourse.bass as bass
from concourse import mybir

F32 = mybir.dt.float32
F32R = mybir.dt.float32r
I32 = mybir.dt.int32
ALU = mybir.AluOpType
ACT = mybir.ActivationFunctionType

P = 128
T = 512
D = 1024
KT = D // P
DEPTH = 2
HALF = 512
QT = HALF // P
ADA = 3 * D
RNN = 1536
RT = RNN // P
RET_HEADS = 4
C_RW = 64
C_HG = 128
DN_ALPHA = (2 * DEPTH) ** 0.25
RW_DECAY = math.exp(-0.5)
RET_LOG = [math.log(1.0 - 2.0 ** (-5.0 - h)) for h in range(RET_HEADS)]


def block_plan():
    first, pieces = {}, []

    def full(name, layer, col, rows=D):
        return [(name, layer, P * k, col) for k in range(rows // P)]

    def add(phase, layer, blocks):
        first[phase, layer] = (len(pieces), len(blocks))
        pieces.extend(blocks)

    for l in range(DEPTH):
        rw = [full("w_in", l, 4096)]
        if l:
            rw += [full("v_down", 0, 0)]
        rw += [full("w_in", l, 2048 + P * m) for m in range(16)]
        add("rw", l, rw)
        add("hg", l, [full("w_in", l, P * m) for m in range(16)])
        add("gate", l, [full("w_in", l, 4224 + P * m) for m in range(16)])
        add("branch", l, [full("b_hg", l, P * m, HALF) + full("b_rw", l, P * m, HALF) for m in range(8)])
        add("out", l, [full("w_out", l, P * m) for m in range(8)])
    add("lru_in", 0, [full("lru_in", 0, P * m) for m in range(2 * RT)])
    tiles = [t for m in range(8) for t in full("lru_out", 0, P * m, RNN)]
    add("lru_out", 0, [tiles[8 * b:8 * b + 8] for b in range(len(tiles) // 8)])
    for h in range(RET_HEADS):
        cols = [256 * h, 256 * h + P, 1024 + 256 * h, 1024 + 256 * h + P]
        cols += [2048 + 512 * h + P * m for m in range(4)] + [4096 + 512 * h + P * m for m in range(4)]
        add("ret_in", h, [full("ret_in", 0, c) for c in cols])
    for half in range(2):
        add("ret_out", half, [[("ret_out", 0, D * half + P * k, P * m) for k in range(KT)] for m in range(8)])
    return first, pieces


VECTORS = [("c", 8)]
for _l in range(DEPTH):
    VECTORS += [(f"{n}{_l}", k) for n, k in (
        ("b_ada", 24), ("lb", 4), ("hg_g", 4), ("mu", 17), ("w0", 4), ("a0", 4), ("k_k", 4), ("k_a", 4),
        ("r_k", 4), ("gn_g", 4), ("gn_b", 4), ("ln_g", 8), ("ln_b", 8))]
VECTORS += [("v0", 4), ("pre0", 8), ("pre1", 8), ("post0", 8), ("post1", 8), ("conv_w", 4 * RT), ("conv_b", RT),
            ("b_a", RT), ("b_x", RT), ("lam", RT)]
CONSTANTS = [("ident", 128), ("ones", 128), ("bdones", 128), ("scan64", 512), ("scan128", 512),
             ("mask192", 192), ("level", 6 * 128), ("hgmask", 8 * 128), ("kdec", 4)]
TABLES = [("cos", 512), ("sin", 512), ("dmask", 512), ("qdec", 512)]


def columns(spec):
    at, out = 0, {}
    for name, n in spec:
        out[name] = (at, n)
        at += n
    return out, at


def constants():
    i = np.arange(P)
    s, t = i[:, None], i[None, :]
    head = (s // 64) == (t // 64)
    c = {"ident": s == t, "ones": np.ones((P, P)), "bdones": head}
    k = np.arange(T)
    c["scan64"] = np.broadcast_to(k % C_RW != 0, (P, T))
    c["scan128"] = np.broadcast_to(k % C_HG != 0, (P, T))
    c["mask192"] = np.concatenate([head & (s < t), (s % 64) <= np.arange(64)[None, :]], 1)
    low = lambda m: (s // (2 * m) == t // (2 * m)) & (s % (2 * m) >= m) & (t % (2 * m) < m)
    c["level"] = np.concatenate([low(1).T] + [low(m) for m in (2, 4, 8, 16, 32)], 1)
    c["hgmask"] = np.concatenate([s == t] + [low(m).T for m in (1, 2, 4, 8, 16, 32, 64)], 1)
    c["kdec"] = np.exp((P - 1.0 - i)[:, None] * np.array(RET_LOG)[None, :]) / 16.0
    tables = {}
    inv_freq = 10000.0 ** (-np.arange(0, 256, 2, dtype=np.float32) / np.float32(256))
    angle = (np.arange(T, dtype=np.float32)[None, :] * inv_freq.astype(np.float32)[:, None]).astype(np.float32)
    tables["cos"], tables["sin"] = np.cos(angle), np.sin(angle)
    diff = (t - s).astype(np.float64)
    tables["dmask"] = np.concatenate(
        [np.where(diff >= 0, np.exp(np.maximum(diff, 0) * g), 0.0) / 16.0 for g in RET_LOG], 1)
    tables["qdec"] = np.concatenate([np.broadcast_to(np.exp((i + 1.0) * g), (P, P)) for g in RET_LOG], 1)
    return (np.concatenate([np.asarray(c[n], np.float32) for n, _ in CONSTANTS], 1),
            np.concatenate([np.asarray(tables[n], np.float32) for n, _ in TABLES], 1))


BAND = [(0, 0), (0, 1), (1, 0), (1, 1), (1, 2), (2, 1), (2, 2)]


HG_CHAIN = 4


class Jobs:

    def __init__(self):
        self.table, self.used = {}, [0] * 6

    def add(self, name, bank):
        self.table[name] = (bank, self.used[bank], 0)
        self.used[bank] += 1

    def loop(self, names, turns):
        per = [sum(b == k for _, b in names) for k in range(6)]
        at = list(self.used)
        for name, bank in names:
            self.table[name] = (bank, at[bank], per[bank])
            at[bank] += 1
        self.used = [u + p * turns for u, p in zip(self.used, per)]

    def __call__(self, name, turn=0):
        bank, base, step = self.table[name]
        return bank, turn * step + base


def job_plan():
    jobs = Jobs()
    for l in range(DEPTH):
        jobs.add(("ada", l), 0)
        for j in range(QT):
            jobs.add(("w_up", l, j), j)
        for j in range(QT):
            jobs.add(("a_up", l, j), 4 + j % 2)
        if l:
            for j in range(QT):
                jobs.add(("v_up", l, j), j)
        for name in ("kk_sum", "rk_sum"):
            for j in range(QT):
                jobs.add((name, l, j), j)
        jobs.loop([(("v_turn", l), 0)] + [(("level", l, n), 1 + n % 2) for n in range(8)]
                  + [(("k_turn", l), 3), (("hg_state", l), 4), (("hg_out", l), 5), (("hg_square", l), 0)], QT)
        names = [(("sc", l, 0), 0), (("sc", l, 1), 1), (("sc", l, 2), 2), (("sc", l, 3), 3), (("b_turn", l), 4),
                 (("k_turn_rw", l), 5), (("v_turn_rw", l), 4), (("x_turn", l), 5)]
        for n in range(5):
            names += [(("z", l, n), 0)] + ([(("xz", l, n), 1)] if n < 4 else []) + [(("zx", l, n), 2)]
        names += [(("rhs", l), 3), (("u", l), 4), (("y", l), 5), (("rw_state", l), 3)]
        jobs.loop(names, T // C_RW)
        for j in range(QT):
            jobs.add(("gn_mean", l, j), j)
        for j in range(QT):
            jobs.add(("gn_var", l, j), j)
        for m in range(KT):
            jobs.add(("branch_rw", l, m), m % 2)
        jobs.add(("ln_mean", l), 2)
        jobs.add(("ln_var", l), 3)
    jobs.add("rms_pre0", 2)
    for g in range(4):
        for w in range(6):
            jobs.add(("lru_gate", g, w), w)
    jobs.add("rms_post0", 2)
    jobs.add("rms_pre1", 3)
    for h in range(RET_HEADS):
        for k in range(2):
            jobs.add(("rk_turn", h, k), 4 + k)
        for v in range(4):
            jobs.add(("rv_turn", h, v), v)
        jobs.add(("r_score", h), 4)
        for v in range(4):
            jobs.add(("r_out", h, v), v)
        for c in range(3):
            for k in range(2):
                jobs.add(("r_state", h, c, k), 4 + k)
        jobs.add(("r_mean", h), 4)
        jobs.add(("r_var", h), 5)
    jobs.add("rms_post1", 2)
    return jobs


class Chain:

    def __init__(self, eng, sem):
        self.eng, self.sem, self.n, self.turn, self.per = eng, sem, 0, None, 0

    def done(self, ins):
        ins.then_inc(self.sem, 1)
        self.n += 1
        self.eng.wait_ge(self.sem, self.n if self.turn is None else self.turn * self.per + self.n)

    def enter(self, turn, per):
        self.turn, self.per, self.start = turn, per, self.n

    def leave(self, turns):
        assert self.n - self.start == self.per, (self.n - self.start, self.per)
        self.n = self.start + self.per * turns
        self.turn = None


def build(nc, shapes):
    first, pieces = block_plan()
    jobs = job_plan()
    blocks = len(pieces)

    dram = {k: nc.dram_tensor(k, s, F32, kind="ExternalInput").ap() for k, s in shapes.items()}
    out = nc.dram_tensor("out", (KT, P, T), F32, kind="ExternalOutput").ap()
    gate_scr = nc.dram_tensor("gate_scr", (DEPTH, 16, P, T), F32).ap()
    x_scr = nc.dram_tensor("x_scr", (3, KT, P, T), F32).ap()
    v_scr = nc.dram_tensor("v_scr", (QT, P, T), F32).ap()

    with ExitStack() as ctx:
        def sb(name, shape, dt=F32):
            return ctx.enter_context(nc.sbuf_tensor(f"{name}_sb", shape, dt))

        def sem(name):
            return ctx.enter_context(nc.semaphore(name))

        act_hi, act_lo = sb("act_hi", [P, 12, T], F32R), sb("act_lo", [P, 12, T], F32R)
        w_raw = sb("w_raw", [P, 2, KT * P])
        w_hi, w_lo = sb("w_hi", [P, 2, KT, P], F32R), sb("w_lo", [P, 2, KT, P], F32R)
        slots = sb("slots", [P, 8, 4, T])
        area = sb("area", [P, 24, T])
        xa, hg = area[:, 0:8], area[:, 8:24]
        vec_at, vec_n = columns(VECTORS)
        const_at, const_n = columns(CONSTANTS)
        vec, const = sb("vec", [P, vec_n]), sb("const", [P, const_n])
        stage = sb("stage", [P, 2, 516])
        wa = sb("wa", [P, T])
        cond = sb("cond", [P, DEPTH, 24])
        derived = sb("derived", [P, 160])
        chunk_end = sb("chunk_end", [P, QT, T // C_RW])
        ST = [stage[:, i, 4:516] for i in range(2)]

        def V(name, k=None, n=1):
            at, size = vec_at[name]
            return vec[:, at:at + size] if k is None else vec[:, at + k:at + k + n]

        def C(name, lo=0, n=None):
            at, size = const_at[name]
            return const[:, at + lo:at + (size if n is None else lo + n)]

        derived_at, derived_first, used = {}, {}, 0
        for name, n in [("c", 8), ("lb_t", 12), ("cl", RT), ("cl_t", RT)] + [
                (f"{k}{l}", n) for l in range(DEPTH)
                for k, n in (("mu1", 17), ("omlb", 4), ("lbf", 4), ("ka1", 4))]:
            derived_at[name] = derived[:, used:used + n]
            derived_first[name] = used
            used += n
        assert used <= 160
        DV = derived_at

        proj = [ctx.enter_context(nc.psum_tensor(f"proj{i}", [P, T], F32)) for i in range(2)]
        aux = [ctx.enter_context(nc.psum_tensor(f"aux{i}", [P, T], F32)) for i in range(6)]

        raw_in = [sem(f"raw_in{i}") for i in range(2)]
        hi_ready, lo_ready, block_used = sem("hi_ready"), sem("lo_ready"), sem("block_used")
        proj_read = [sem(f"proj_read{i}") for i in range(2)]
        aux_full = [sem(f"aux_full{i}") for i in range(6)]
        aux_read = [sem(f"aux_read{i}") for i in range(6)]
        split_src, split_hi, split_lo = sem("split_src"), sem("split_hi"), sem("split_lo")
        sq_ready, sq_used = sem("sq_ready"), sem("sq_used")
        made = {}

        def S(name):
            if name not in made:
                made[name] = sem(name)
            return made[name]

        RW_LAST = [first["rw", l][0] + first["rw", l][1] - 1 for l in range(DEPTH)]
        SPLITS = {("h", 0): 0, ("hg", 0): 8, ("rw", 0): 12, ("merged", 0): 16, ("h", 1): 24, ("hg", 1): 32,
                  ("rw", 1): 36, ("merged", 1): 40, "lru_h": 48, "lru_y": 56, "ret_h": 68, "ret_y": 76}
        SQUARES = {("ln", 0): 0, ("ln", 1): 8, "pre0": 16, "post0": 24, "pre1": 32,
                   **{("ret", h): 40 + 4 * h for h in range(RET_HEADS)}, "post1": 56}
        R_, K_, V_, Z_, P1, P2, P3, P4 = (slots[:, i] for i in range(8))
        merged = slots[:, 0:2].rearrange("p a b t -> p (a b) t")
        ada_acc = slots[:, 2:4].rearrange("p a b t -> p (a b t)")[:, 0:ADA]
        ada_in = slots[:, 5:8].rearrange("p a b t -> p (a b t)").rearrange("p (s n) -> p s n", s=2)

        def wait(eng, semaphore, value):
            if not (isinstance(value, int) and value <= 0):
                eng.wait_ge(semaphore, value)

        def use_of(b):
            return b if b < first["lru_out", 0][0] else b - 4

        def projected(eng, b, turn=0, steps=4):
            eng.wait_ge(block_used, b + 1 + steps * turn)
            return proj[use_of(b) % 2][:, :]

        def read(ins, b):
            return ins.then_inc(proj_read[use_of(b) % 2], 1)

        def evacuated(eng, b):
            u = use_of(b)
            eng.wait_ge(proj_read[u % 2], u // 2 + 1)

        def job_open(eng, name, turn=0):
            bank, use = jobs(name, turn)
            wait(eng, aux_read[bank], use)
            return aux[bank][:, :]

        def job_full(ins, name):
            return ins.then_inc(aux_full[jobs(name)[0]], 1)

        def job_ready(eng, name, turn=0):
            bank, use = jobs(name, turn)
            eng.wait_ge(aux_full[bank], use + 1)
            return aux[bank][:, :]

        def job_read(ins, name):
            return ins.then_inc(aux_read[jobs(name)[0]], 1)

        def evacuated_job(eng, name, turn=0):
            bank, use = jobs(name, turn)
            eng.wait_ge(aux_read[bank], use + 1)

        def left(eng, u):
            eng.wait_ge(proj_read[u % 2], u // 2 + 1)

        def lru_out_ready(eng, m):
            if m % 2:
                eng.wait_ge(block_used, first["lru_out", 0][0] + 3 * (m // 2) + 3)
            else:
                eng.wait_ge(S("lru_half"), m // 2 + 1)

        def landed(eng):
            eng.wait_ge(S("const_in"), 32)

        def derived_column(name):
            return derived_first[name]

        def in_chunks(ap, n):
            return ap.rearrange("p (c t) -> p c t", t=n)

        ring = [xa[:, i] for i in range(4)]
        v_tok, k_hg, decay, scores = xa[:, 4], xa[:, 5], xa[:, 6], xa[:, 7]

        flat = area[:, :, :].rearrange("p a t -> p (a t)")
        taken = [0]

        def carve(width):
            at = taken[0]
            taken[0] += QT * width
            return flat[:, at:at + QT * width].rearrange("p (j n) -> p j n", j=QT)

        ar = carve(192)
        b_bd, k_bd, v_bd = carve(P), carve(P), carve(P)
        m1, m2 = carve(192), carve(192)
        x_inv, xt_inv = carve(P), carve(P)
        b_tok, k_tok, v_tok_rw = carve(P), carve(P), carve(P)
        z_sb, rhs_sb, u_sb, state = carve(P), carve(P), carve(P), carve(P)
        assert taken[0] <= 24 * T

        block = ctx.enter_context(nc.Block())

        @block.sync
        def _(sp):
            def load_block(b, turn=0):
                wait(sp, lo_ready, b - 1 + 2 * turn)
                sp.dma_start(w_raw[:, b % 2, :], dram["wall"][b + 2 * turn]).then_inc(raw_in[b % 2], 16)

            at = [0]

            def blocks_to(end):
                end = min(end, blocks)
                while at[0] < min(2, end):
                    load_block(at[0])
                    at[0] += 1
                n = (end - at[0]) // 2
                if n > 1:
                    start = at[0]
                    with sp.Fori(0, n) as turn:
                        for b in (start, start + 1):
                            load_block(b, turn)
                    at[0] += 2 * n
                while at[0] < end:
                    load_block(at[0])
                    at[0] += 1

            sp.dma_start(const[:, :], dram["const"]).then_inc(S("const_in"), 16)
            sp.dma_start(vec[:, :], dram["vec"]).then_inc(S("const_in"), 16)
            sp.dma_start(xa[:, :, :], dram["x_t"].rearrange("k p t -> p k t")).then_inc(S("x_in"), 16)

            def load_ada(l, k):
                n = 8 * l + k
                wait(sp, S("ada_used"), n - 1)
                sp.dma_start(ada_in[:, k % 2], dram["w_ada"][l, k]).then_inc(S(f"ada_in{k % 2}"), 16)

            for k in range(KT):
                load_ada(0, k)
            for l in range(DEPTH):
                b_rw, b_hg, b_gate = first["rw", l][0], first["hg", l][0], first["gate", l][0]
                b_br, b_out = first["branch", l][0], first["out", l][0]
                blocks_to(b_rw + 4)
                if l:
                    sp.wait_ge(S("x_done"), l)
                    sp.dma_start(x_scr[0].rearrange("k p t -> p k t"), xa[:, :, :]).then_inc(S("x_saved"), 16)
                    sp.wait_ge(S("x_saved"), 16)
                sp.wait_ge(split_lo, SPLITS["h", l] + 8)
                sp.dma_start(xa[:, 0, :], dram["up"][l]).then_inc(S("up_in"), 16)
                if l:
                    sp.dma_start(xa[0:32, 2, :], dram["v_up"]).then_inc(S("up_in"), 16)
                    sp.wait_ge(S("v_out"), 16)
                    sp.dma_start(xa[:, 4:8, :], v_scr.rearrange("k p t -> p k t")).then_inc(S("v_in"), 16)
                blocks_to(b_hg + 3)
                if not l:
                    for b in (RW_LAST[0] - 5, RW_LAST[0] - 4):
                        evacuated(sp, b)
                    sp.dma_start(v_scr.rearrange("k p t -> p k t"), V_).then_inc(S("v_out"), 16)
                for m in range(16):
                    blocks_to(b_gate + m + 3)
                    evacuated(sp, b_gate + m)
                    sp.dma_start(gate_scr[l, m], ST[(b_gate + m) % 2]).then_inc(S(f"gate_out{(b_gate + m) % 2}"), 16)
                for m in range(KT):
                    blocks_to(b_br + m + 4)
                    if m == 0:
                        sp.wait_ge(S("state_ready"), (T // C_RW) * (l + 1))
                        for k in range(2):
                            sp.wait_ge(S(f"gate_out{k}"), 128 * (l + 1))
                    if m > 1:
                        sp.wait_ge(split_src, SPLITS["merged", l] + m - 1)
                    for k in range(2):
                        sp.dma_start(P1[:, 2 * (m % 2) + k, :], gate_scr[l, 8 * k + m])\
                            .then_inc(S(f"gate_in{m % 2}"), 16)
                    if m == 1:
                        evacuated_job(sp, ("y", l), T // C_RW - 1)
                        src = x_scr[0] if l else dram["x_t"]
                        sp.dma_start(xa[:, :, :], src.rearrange("k p t -> p k t")).then_inc(S("x_in"), 16)
                if not l:
                    sp.wait_ge(split_lo, SPLITS["rw", 0] + 4)
                    for k in range(KT):
                        load_ada(1, k)
                        blocks_to(b_out + 4 + k)
            lru = first["lru_in", 0][0]
            blocks_to(lru + 4)
            sp.wait_ge(S("x_done"), 2)
            sp.dma_start(x_scr[1].rearrange("k p t -> p k t"), xa[:, :, :]).then_inc(S("x_saved"), 16)
            sp.dma_start(flat[:, 8 * T:8 * T + 4 * 14 * P], dram["lru_gates"].rearrange("p g n -> p (g n)"))\
                .then_inc(S("lru_w"), 16)
            blocks_to(first["lru_out", 0][0] + 3)
            sp.wait_ge(split_lo, SPLITS["lru_y"] + RT)
            sp.wait_ge(S("x_saved"), 32)
            sp.dma_start(xa[:, :, :], x_scr[1].rearrange("k p t -> p k t")).then_inc(S("x_in"), 16)
            ret = first["ret_in", 0][0]
            blocks_to(ret + 4)
            sp.wait_ge(S("x_done"), 3)
            sp.dma_start(x_scr[2].rearrange("k p t -> p k t"), xa[:, :, :]).then_inc(S("x_saved"), 16)
            sp.wait_ge(S("x_saved"), 48)
            sp.wait_ge(split_lo, SPLITS["ret_h"] + 8)
            sp.dma_start(xa[:, 0:4, :].rearrange("p a t -> p (a t)"), dram["tables"]).then_inc(S("tables_in"), 16)
            blocks_to(first["ret_out", 1][0] + 3)
            sp.wait_ge(split_lo, SPLITS["ret_y"] + 16)
            sp.dma_start(xa[:, :, :], x_scr[2].rearrange("k p t -> p k t")).then_inc(S("x_in"), 16)
            blocks_to(blocks)
            for m in range(KT):
                sp.wait_ge(S("x_final"), m + 1)
                sp.dma_start(out[m], xa[:, m, :]).then_inc(S("out_done"), 16)
            sp.wait_ge(S("out_done"), 16 * KT)
            sp.wait_ge(S("x_saved"), 48)

        @block.gpsimd
        def _(pool):
            def low(b, turn=0):
                pool.wait_ge(hi_ready, b + 1 + 2 * turn)
                nc.gpsimd.tensor_tensor(w_lo[:, b % 2, :, :].rearrange("p k n -> p (k n)"), w_raw[:, b % 2, :],
                                        w_hi[:, b % 2, :, :].rearrange("p k n -> p (k n)").bitcast(F32),
                                        ALU.subtract).then_inc(lo_ready, 1)

            with pool.Fori(0, blocks // 2) as turn:
                low(0, turn)
                low(1, turn)
            low(blocks - 1)

        LRU, LRU_OUT, RET, RET_OUT = (first[k, 0][0] for k in ("lru_in", "lru_out", "ret_in", "ret_out"))
        X_C = slots[:, 0:3].rearrange("p a b t -> p (a b) t")
        G_S = slots[:, 3:6].rearrange("p a b t -> p (a b) t")
        OUT = slots[:, 0:2].rearrange("p a b t -> p (a b) t")
        RS = slots[:, 7, 3, :]
        LRU_A, LRU_U = slots[:, 6], slots[:, 7]
        r_ktok = slots[:, 7, 0:2, :].rearrange("p k (c n) -> p k c n", n=P)
        r_vtok = slots[:, 6].rearrange("p a t -> p (a t)").rearrange("p (c n) -> p c n", n=512)
        r_scores = slots[:, 7, 2, :]
        r_qd = xa[:, 4:6]
        r_state = xa[:, 6:8]
        tables = dict(zip(("cos", "sin", "dmask", "qdec"), (xa[:, i] for i in range(4))))

        def ret_tiles(h):
            s = 3 * (h % 2)
            return slots[:, s, 0:2], slots[:, s, 2:4], slots[:, s + 1], slots[:, s + 2]

        def halves(ap, m):
            v = ap.rearrange("p (b h m) -> p b h m", h=2, m=m)
            return v[:, :, 0, :], v[:, :, 1, :]

        @block.scalar
        def _(act):
            chain = Chain(act, S("act_chain"))
            A = nc.scalar.activation

            def weights(b, turn=0):
                if b >= blocks:
                    return
                act.wait_ge(raw_in[b % 2], 16 * (b // 2 + 1) + 32 * turn)
                wait(act, block_used, b - 1 + 4 * turn)
                A(w_hi[:, b % 2, :, :].rearrange("p k n -> p (k n)"), w_raw[:, b % 2, :], ACT.Copy)\
                    .then_inc(hi_ready, 1)

            def high(n, slot, src, turn=0):
                act.wait_ge(split_src, n + 1 + turn)
                if not isinstance(turn, int):
                    landed(act)
                A(act_hi[:, slot, :], src, ACT.Copy).then_inc(split_hi, 1)

            def square(key, m, src):
                if m > 1:
                    act.wait_ge(sq_used, SQUARES[key] - list(SQUARES).index(key) + m - 1)
                A(ST[m % 2], src, ACT.Square).then_inc(sq_ready, 1)

            def inverse_root(dst, job, scale, eps, signal, turn=0):
                x = job_ready(act, job, turn)
                job_read(A(dst, x, ACT.Ln, scale=scale, bias=eps), job)
                evacuated_job(act, job, turn)
                A(dst, dst, ACT.Exp, scale=-0.5).then_inc(signal, 1)

            act.wait_ge(S("const_in"), 32)
            A(DV["c"], V("c"), ACT.Sigmoid).then_inc(S("c_sig"), 1)
            act.wait_ge(S("setup_dve"), 1)
            chain.done(A(DV["lb_t"][:, 4:12], DV["lb_t"][:, 4:12], ACT.Exp))
            chain.done(A(DV["cl_t"], DV["cl_t"], ACT.Exp, scale=-1.0))
            A(DV["cl_t"], DV["cl_t"], ACT.Ln, bias=1.0).then_inc(S("setup_act"), 1)
            weights(0)
            weights(1)
            for l in range(DEPTH):
                b_rw, b_hg, b_gate = first["rw", l][0], first["hg", l][0], first["gate", l][0]
                b_br, b_out = first["branch", l][0], first["out", l][0]
                for m in range(KT):
                    high(SPLITS["h", l] + m, m, ST[m % 2])

                def scaled(b, k, turn=0):
                    weights(b + 2, turn)
                    x = projected(act, b, turn)
                    at = vec_at[f"mu{l}"][0] + k
                    landed(act)
                    A(ST[b % 2], x, ACT.Copy, scale=vec[:, bass.ds(at + 4 * turn, 1)]).then_inc(S("mu_scaled"), 1)

                scaled(b_rw, 0)
                evacuated(act, b_rw)
                A(wa[0:64, :], wa[0:64, :], ACT.Tanh).then_inc(S("tanh_done"), 1)
                b = b_rw + 1
                if l:
                    weights(b + 2)
                    act.wait_ge(S("x_saved"), 16)
                    read(A(xa[:, 1, :], projected(act, b), ACT.Copy), b)
                    b += 1
                with act.Fori(0, 4) as turn:
                    for j in range(4):
                        scaled(b + j, 1 + j, turn)
                for j in range(QT):
                    x = job_ready(act, ("w_up", l, j))
                    job_read(A(P1[:, j, :], x, ACT.Sigmoid, bias=V(f"w0{l}", j)), ("w_up", l, j))
                    x = job_ready(act, ("a_up", l, j))
                    job_read(A(P2[:, j, :], x, ACT.Sigmoid, bias=V(f"a0{l}", j)), ("a_up", l, j))
                if l:
                    for j in range(QT):
                        x = job_ready(act, ("v_up", l, j))
                        job_read(A(P3[:, j, :], x, ACT.Sigmoid, bias=V("v0", j)), ("v_up", l, j))
                evacuated(act, b_hg - 1)
                evacuated(act, b_hg - 2)
                A(P4, Z_, ACT.Sigmoid).then_inc(S("z_sig"), 1)
                for j in range(QT):
                    act.wait_ge(S("kk0_ready"), 4 * l + j + 1)
                    A(xa[:, 4 + j, :], P4[:, j, :], ACT.Square).then_inc(S("kk_squares"), 1)

                def keep(m):
                    weights(b_hg + m + 2)
                    read(A(hg[:, m, :], projected(act, b_hg + m), ACT.Copy), b_hg + m)

                for m in range(4):
                    keep(m)
                for j in range(QT):
                    evacuated_job(act, ("kk_sum", l, j))
                chain.done(A(xa[:, 4:8, :], xa[:, 4:8, :], ACT.Ln, scale=2.0 ** 20))
                A(xa[:, 4:8, :], xa[:, 4:8, :], ACT.Exp, scale=-0.5, bias=10.0 * math.log(2.0))\
                    .then_inc(S("norm_ready"), 1)
                act.wait_ge(S("decay_ex"), l + 1)
                A(P1, P1, ACT.Exp, scale=-RW_DECAY).then_inc(S("decay_exp"), 1)
                for m in range(4, 8):
                    keep(m)
                act.wait_ge(S("bn_ready"), l + 1)
                A(P2, P3, ACT.Exp, scale=RW_DECAY).then_inc(S("decay_in"), 1)
                A(P3, P3, ACT.Exp, scale=-RW_DECAY).then_inc(S("decay_all"), 1)
                for m in range(8, 12):
                    keep(m)
                for m in range(12, 16):
                    b = b_hg + m
                    weights(b + 2)
                    A(ST[b % 2], projected(act, b), ACT.Sigmoid).then_inc(S("sig_staged"), 1)

                act.wait_ge(S("dve_prep"), l + 1)
                for k in (14, 15):
                    evacuated(act, b_hg + k)
                with act.Fori(0, QT) as turn:
                    chain.enter(turn, 0)
                    head = 4 * l + turn
                    act.wait_ge(split_lo, SPLITS["hg", l] + turn)
                    landed(act)
                    A(decay, hg[:, 4 + turn, :], ACT.Sigmoid).then_inc(S("f_sig"), 1)
                    A(k_hg, hg[:, 4 + turn, :], ACT.Sigmoid, scale=-1.0).then_inc(S("f_sig"), 1)
                    A(ring[3], hg[:, 8 + turn, :], ACT.Copy).then_inc(S("i_copied"), 1)
                    act.wait_ge(S("f_mix"), 2 * head + 2)
                    A(decay, decay, ACT.Ln).then_inc(S("f_ln"), 1)
                    A(hg[:, 4 + turn, :], hg[:, 4 + turn, :], ACT.Ln).then_inc(S("f_ln"), 1)

                    def gate(g):
                        b = b_gate + g
                        weights(b + 2, turn)
                        x = projected(act, b, turn)
                        act.wait_ge(S(f"gate_out{b % 2}"), 16 * (8 * l + g // 2) + 32 * turn)
                        read(A(ST[b % 2], x, ACT.Sigmoid), b)

                    def level(n):
                        act.wait_ge(S("diff_ready"), 7 * head + n)
                        r = ring[(n - 1) % 3]
                        lo, hi = halves(r, 1 << (n - 1))
                        A(lo, lo, ACT.Exp, scale=-1.0).then_inc(S("level_exp"), 1)
                        A(hi, hi, ACT.Exp).then_inc(S("level_exp"), 1)

                    gate(0)
                    job_read(A(v_tok, job_ready(act, ("v_turn", l), turn), ACT.Copy), ("v_turn", l))
                    level(1)
                    A(decay, hg[:, 4 + turn, :], ACT.Exp).then_inc(S("exp_ready"), 1)
                    gate(1)
                    for n in (2, 3, 4):
                        level(n)
                    gate(2)
                    for n in (5, 6, 7):
                        level(n)
                    gate(3)
                    act.wait_ge(S("tail_diff"), head + 1)
                    A(ring[1], ring[1], ACT.Exp, scale=-1.0).then_inc(S("tail_exp"), 1)
                    job_read(A(ring[2], job_ready(act, ("k_turn", l), turn), ACT.Copy), ("k_turn", l))
                    x = job_ready(act, ("hg_out", l), turn)
                    A(ring[3], x, ACT.Square).then_inc(S("hg_sq"), 1)
                    inverse_root(scores, ("hg_square", l), 1.0 / P, 1e-6, S("hg_rms"), turn)
                    high(SPLITS["hg", l], 8 + turn, hg[:, 12 + turn, :], turn)
                    chain.leave(QT)

                act.wait_ge(S("zeroed"), l + 1)
                chunks = T // C_RW
                with act.Fori(0, chunks) as c:
                    tokens = bass.ds(c * C_RW, C_RW)
                    act.wait_ge(S("state_ready"), chunks * l + c)
                    landed(act)
                    for src, dst in ((K_, k_bd), (V_, v_bd)):
                        for q in (slice(0, 64), slice(64, 128)):
                            A(dst[q, :, q], src[q, :, tokens], ACT.Copy).then_inc(S("chunk_act"), 1)
                    A(ar[:, :, 128:192], R_[:, :, tokens], ACT.Copy).then_inc(S("chunk_act"), 1)

                    def take(dst, job):
                        x = job_ready(act, job, c)
                        job_read(A(dst, in_chunks(x, P), ACT.Copy), job)

                    take(b_tok, ("b_turn", l))
                    take(k_tok, ("k_turn_rw", l))
                    take(v_tok_rw, ("v_turn_rw", l))
                    take(x_inv, ("x_turn", l))
                    take(rhs_sb, ("rhs", l))
                    take(u_sb, ("u", l))
                    x = job_ready(act, ("y", l), c)
                    landed(act)
                    job_read(A(P3[:, :, tokens], in_chunks(x[:, 0:QT * C_RW], C_RW), ACT.Copy), ("y", l))

                act.wait_ge(S("state_ready"), chunks * (l + 1))
                for j in range(QT):
                    evacuated_job(act, ("gn_mean", l, j))
                    A(R_[:, j, :], P3[:, j, :], ACT.Square).then_inc(S("gn_sq"), 1)
                for j in range(QT):
                    inverse_root(K_[:, j, :], ("gn_var", l, j), 1.0 / 64, 64e-5, S("gn_rs"))
                act.wait_ge(block_used, b_gate + 16)
                for j in range(QT):
                    high(SPLITS["rw", l] + j, j, P3[:, j, :])
                for m in range(KT):
                    weights(b_br + m + 2)
                    if m < 4:
                        high(SPLITS["merged", l] + m, 4 + m, merged[:, m, :])
                for m in range(4, KT):
                    high(SPLITS["merged", l] + m, m - 4, merged[:, m, :])
                for m in range(KT):
                    weights(b_out + m + 2)
                for m in range(KT):
                    if m < 7:
                        act.wait_ge(S("xc_ready"), 7 * l + m + 1)
                    else:
                        evacuated_job(act, ("ln_mean", l))
                    square(("ln", l), m, xa[:, m, :])
                inverse_root(merged[:, 0, :], ("ln_var", l), 1.0 / D, 1e-5, S("ln_rs"))

            def rms(key, job, tiles, ready):
                for m in range(KT):
                    ready(m)
                    square(key, m, tiles[:, m, :])
                inverse_root(RS, job, 1.0 / D, 1e-6, S("rms_rs"))

            act.wait_ge(S("x_done"), 2)
            rms("pre0", "rms_pre0", xa, lambda m: None)
            for m in range(KT):
                high(SPLITS["lru_h"] + m, m, ST[m % 2])
            with act.Fori(0, RT // 4) as turn:
                for j in range(4):
                    b = LRU + j
                    weights(b + 2, turn)
                    x = projected(act, b, turn)
                    act.wait_ge(S("conv_done"), max(j - 1, 0) + 4 * turn)
                    read(A(ST[b % 2], x, ACT.Copy), b)
            act.wait_ge(S("conv_done"), RT)
            with act.Fori(0, RT // 4) as turn:
                for j in range(4):
                    b = LRU + RT + j
                    weights(b + 2, turn)
                    A(ST[b % 2], projected(act, b, turn), ACT.Sigmoid).then_inc(S("sig_staged"), 1)
            for g in range(4):
                if g:
                    act.wait_ge(split_src, SPLITS["lru_y"] + 3 * g)
                if g == 0:
                    act.wait_ge(S("x_saved"), 32)
                for w in range(6):
                    o = w % 3
                    name = ("lru_gate", g, w)
                    x = job_ready(act, name)
                    dst, bias = (LRU_A[:, o, :], V("b_a", 3 * g + o)) if w < 3 else (xa[:, o, :], V("b_x", 3 * g + o))
                    job_read(A(dst, x, ACT.Sigmoid, bias=bias), name)
                for o in range(3):
                    evacuated_job(act, ("lru_gate", g, o))
                    A(LRU_U[:, o, :], LRU_A[:, o, :], ACT.Tanh, scale=DV["cl_t"][:, 3 * g + o:3 * g + o + 1])\
                        .then_inc(S("lru_tanh"), 1)
                for o in range(3):
                    A(LRU_A[:, o, :], LRU_A[:, o, :], ACT.Exp, scale=DV["cl"][:, 3 * g + o:3 * g + o + 1])\
                        .then_inc(S("lru_exp"), 1)
                for o in range(3):
                    act.wait_ge(S("lru_u"), 3 * g + o + 1)
                    chain.done(A(LRU_U[:, o, :], LRU_U[:, o, :], ACT.Ln, scale=2.0 ** 60))
                    A(LRU_U[:, o, :], LRU_U[:, o, :], ACT.Exp, scale=0.5, bias=-30.0 * math.log(2.0))\
                        .then_inc(S("lru_sqrt"), 1)
                act.wait_ge(block_used, LRU + 2 * RT)
                for o in range(3):
                    high(SPLITS["lru_y"] + 3 * g + o, 3 * g + o, xa[:, 4 + o, :])
            for b in range(LRU_OUT, RET):
                weights(b + 2)
            rms("post0", "rms_post0", OUT, lambda m: left(act, LRU_OUT + m))

            act.wait_ge(S("x_done"), 3)
            rms("pre1", "rms_pre1", xa, lambda m: None)
            for m in range(KT):
                high(SPLITS["ret_h"] + m, m, ST[m % 2])

            def ret_blocks(h):
                q, k, v, _ = ret_tiles(h)
                if h > 1:
                    act.wait_ge(split_src, SPLITS["ret_y"] + 4 * (h - 1))
                for j in range(12):
                    b = RET + 12 * h + j
                    weights(b + 2)
                    x = projected(act, b)
                    if j < 8:
                        dst = (q, k, v[:, 0:2], v[:, 2:4])[j // 2][:, j % 2, :]
                        read(A(dst, x, ACT.Copy), b)
                    else:
                        A(ST[b % 2], x, ACT.Sigmoid).then_inc(S("sig_staged"), 1)

            def attend(h):
                for k in range(2):
                    x = job_ready(act, ("rk_turn", h, k))
                    job_read(A(r_ktok[:, k], in_chunks(x, P), ACT.Copy, scale=C("kdec", h, 1)), ("rk_turn", h, k))
                for v in range(4):
                    x = job_ready(act, ("rv_turn", h, v))
                    job_read(A(r_vtok[:, :, v * P:(v + 1) * P], in_chunks(x, P), ACT.Copy), ("rv_turn", h, v))
                for v in range(4):
                    x = job_ready(act, ("r_out", h, v))
                    job_read(A(hg[:, 4 * h + v, :], x, ACT.Copy), ("r_out", h, v))
                for v in range(4):
                    if v < 3:
                        act.wait_ge(S("ret_c"), 3 * h + v + 1)
                    else:
                        evacuated_job(act, ("r_mean", h))
                    square(("ret", h), v, hg[:, 4 * h + v, :])
                inverse_root(RS, ("r_var", h), 1.0 / 512, 1e-5, S("rms_rs"))

            ret_blocks(0)
            ret_blocks(1)
            attend(0)
            ret_blocks(2)
            attend(1)
            ret_blocks(3)
            act.wait_ge(block_used, RET + 48)
            for i in range(8):
                high(SPLITS["ret_y"] + i, i, hg[:, i, :])
            attend(2)
            for i in range(4):
                high(SPLITS["ret_y"] + 8 + i, 8 + i, hg[:, 8 + i, :])
            for m in range(KT):
                weights(RET_OUT + m + 2)
            attend(3)
            for i in range(4):
                high(SPLITS["ret_y"] + 12 + i, i, hg[:, 12 + i, :])
            for m in range(KT):
                weights(RET_OUT + KT + m + 2)
            rms("post1", "rms_post1", OUT, lambda m: evacuated(act, RET_OUT + KT + m))

        @block.vector
        def _(dve):
            chain = Chain(dve, S("dve_chain"))
            TS, TT, STT = nc.vector.tensor_scalar, nc.vector.tensor_tensor, nc.vector.scalar_tensor_tensor

            def tt(out_ap, a, b, op):
                return TT(out_ap, a, b, op)

            def stt(out_ap, in0, scalar, in1, op0, op1):
                return STT(out=out_ap, in0=in0, scalar=scalar, in1=in1, op0=op0, op1=op1)

            def low(n, slot, src, turn=0):
                dve.wait_ge(split_hi, n + 1 + turn)
                tt(act_lo[:, slot, :], src, act_hi[:, slot, :].bitcast(F32), ALU.subtract).then_inc(split_lo, 1)

            def spread(ap, n):
                return ap.unsqueeze(1).to_broadcast([P, n, ap.shape[1]])

            chain.done(nc.vector.memset(stage[:, :, 0:4], 0.0))
            dve.wait_ge(S("const_in"), 32)
            t = DV["lb_t"]
            chain.done(tt(t[:, 0:4], V("lb0"), V("lb1"), ALU.max))
            chain.done(tt(t[:, 4:8], V("lb0"), t[:, 0:4], ALU.subtract))
            chain.done(tt(t[:, 8:12], V("lb1"), t[:, 0:4], ALU.subtract))
            stt(DV["cl_t"], V("lam"), -1.0, V("lam"), ALU.mult, ALU.max).then_inc(S("setup_dve"), 1)
            for l in range(DEPTH):
                chain.done(TS(DV[f"mu1{l}"], V(f"mu{l}"), -1.0, 1.0, ALU.mult, ALU.add))
                chain.done(TS(DV[f"ka1{l}"], V(f"k_a{l}"), -1.0, 1.0, ALU.mult, ALU.add))
            dve.wait_ge(S("c_sig"), 1)
            chain.done(tt(DV["c"], DV["c"], V("c"), ALU.mult))

            def ada_step(l, k):
                n = 8 * l + k
                dve.wait_ge(S(f"ada_in{k % 2}"), 16 * (n // 2 + 1))
                wait(dve, S("ada_used"), n)
                if k == 0:
                    ins = TS(ada_acc, ada_in[:, 0], DV["c"][:, 0:1], None, ALU.mult)
                else:
                    ins = stt(ada_acc, ada_in[:, k % 2], DV["c"][:, k:k + 1], ada_acc, ALU.mult, ALU.add)
                ins.then_inc(S("ada_used"), 1)

            for k in range(KT):
                ada_step(0, k)
            dve.wait_ge(S("setup_act"), 1)
            chain.done(tt(t[:, 0:4], t[:, 4:8], t[:, 8:12], ALU.add))
            chain.done(nc.vector.reciprocal(t[:, 0:4], t[:, 0:4]))
            chain.done(tt(t[:, 4:8], t[:, 4:8], t[:, 0:4], ALU.mult))
            chain.done(tt(t[:, 8:12], t[:, 8:12], t[:, 0:4], ALU.mult))
            chain.done(tt(t[:, 8:12], t[:, 8:12], t[:, 4:8], ALU.add))
            chain.done(tt(t[:, 8:12], t[:, 8:12], t[:, 4:8], ALU.subtract))
            chain.done(tt(t[:, 4:8], t[:, 4:8], t[:, 4:8], ALU.subtract))
            for l in range(DEPTH):
                lb = t[:, 4 + 4 * l:8 + 4 * l]
                chain.done(TS(DV[f"omlb{l}"], lb, -1.0, 1.0, ALU.mult, ALU.add))
                chain.done(TS(DV[f"lbf{l}"], lb, 1e-30, None, ALU.max))
            chain.done(TS(DV["cl"], V("lam"), -1.0, 0.0, ALU.mult, ALU.max))
            chain.done(tt(DV["cl"], DV["cl"], DV["cl_t"], ALU.add))
            chain.done(TS(DV["cl"], DV["cl"], -8.0, None, ALU.mult))
            chain.done(TS(DV["cl_t"], DV["cl"], -1.0, None, ALU.mult))

            for l in range(DEPTH):
                b_rw, b_hg, b_gate = first["rw", l][0], first["hg", l][0], first["gate", l][0]
                b_br, b_out = first["branch", l][0], first["out", l][0]
                x = job_ready(dve, ("ada", l))
                job_read(tt(cond[:, l, :], x[:, 0:24], V(f"b_ada{l}"), ALU.add), ("ada", l))
                evacuated_job(dve, ("ada", l))
                chain.done(TS(cond[:, l, 8:24], cond[:, l, 8:24], 1.0, None, ALU.add))
                if l == 0:
                    dve.wait_ge(S("x_in"), 16)
                n = SPLITS["h", l]
                for m in range(KT):
                    if m > 1:
                        dve.wait_ge(split_lo, n + m - 1)
                    TS(ST[m % 2], xa[:, m, :], cond[:, l, 8 + m:9 + m], cond[:, l, m:m + 1], ALU.mult, ALU.add)\
                        .then_inc(split_src, 1)
                    if m:
                        low(n + m - 1, m - 1, ST[(m - 1) % 2])
                low(n + 7, 7, ST[1])

                def shifted(b, k, dst, turn=0):
                    dve.wait_ge(S("mu_scaled"), 17 * l + k + 1 + 4 * turn)
                    at = derived_column(f"mu1{l}") + k
                    read(stt(dst, proj[b % 2][:, :], derived[:, bass.ds(at + 4 * turn, 1)],
                             stage[:, b % 2, 3:515], ALU.mult, ALU.add), b)

                shifted(b_rw, 0, wa[:, :])
                b = b_rw + 1 + l
                if l:
                    dve.wait_ge(S("v_out"), 16)
                with dve.Fori(0, 4) as turn:
                    for j in range(4):
                        shifted(b + j, 1 + j, slots[:, turn, j, :], turn)
                for b in (b_hg - 2, b_hg - 1):
                    evacuated(dve, b)
                dve.wait_ge(S("z_sig"), l + 1)
                chain.done(tt(Z_, Z_, P4, ALU.mult))
                if l:
                    dve.wait_ge(S("v_in"), 16)
                    vf = xa[:, 4:8, :]
                    chain.done(tt(vf, vf, V_, ALU.subtract))
                    for j in range(QT):
                        evacuated_job(dve, ("v_up", l, j))
                    chain.done(tt(vf, vf, P3, ALU.mult))
                    chain.done(tt(V_, V_, vf, ALU.add))
                for j in range(QT):
                    TS(P4[:, j, :], K_[:, j, :], V(f"k_k{l}", j), None, ALU.mult).then_inc(S("kk0_ready"), 1)
                for j in range(QT):
                    evacuated_job(dve, ("w_up", l, j))
                    chain.done(nc.vector.tensor_tensor_scan(P3[:, j, :], C("scan64"), P1[:, j, :], 0.0,
                                                            ALU.mult, ALU.add))
                tt(P1, P3, P1, ALU.subtract).then_inc(S("decay_ex"), 1)
                for j in range(QT):
                    evacuated_job(dve, ("a_up", l, j))
                for j in range(QT):
                    chain.done(TS(xa[:, 3, :], P2[:, j, :], V(f"k_a{l}", j), DV[f"ka1{l}"][:, j:j + 1],
                                  ALU.mult, ALU.add))
                    chain.done(tt(K_[:, j, :], K_[:, j, :], xa[:, 3, :], ALU.mult))
                for j in range(QT):
                    stt(xa[:, j, :], R_[:, j, :], V(f"r_k{l}", j), K_[:, j, :], ALU.mult, ALU.mult)\
                        .then_inc(S("rk_ready"), 1)
                for j in range(QT):
                    x = job_ready(dve, ("kk_sum", l, j))
                    job_read(TS(xa[:, 4 + j, :], x, 1e-24, None, ALU.max), ("kk_sum", l, j))
                dve.wait_ge(S("norm_ready"), l + 1)
                chain.done(tt(P4, P4, xa[:, 4:8, :], ALU.mult))
                dve.wait_ge(S("decay_exp"), l + 1)
                chain.done(tt(P1, P1, P4, ALU.mult))
                stt(P4, P4, -1.0, P2, ALU.mult, ALU.mult).then_inc(S("bn_ready"), 1)
                dve.wait_ge(S("bn_ready"), l + 1)
                dve.wait_ge(S("decay_in"), l + 1)
                chain.done(tt(P4, P4, P2, ALU.mult))
                chain.done(tt(K_, K_, P2, ALU.mult))
                for j in range(QT):
                    x = job_ready(dve, ("rk_sum", l, j))
                    job_read(tt(P2[:, j, :], x, V_[:, j, :], ALU.mult), ("rk_sum", l, j))
                dve.wait_ge(S("decay_all"), l + 1)
                chain.done(nc.vector.tensor_copy(chunk_end[:, :, :], P3[:, :, C_RW - 1:T:C_RW]))
                tt(R_, R_, P3, ALU.mult).then_inc(S("dve_prep"), 1)
                for k in range(4):
                    b = b_hg + 12 + k
                    dve.wait_ge(S("sig_staged"), 4 * l + k + 1)
                    read(tt(hg[:, 12 + k, :], proj[b % 2][:, :], ST[b % 2], ALU.mult), b)

                with dve.Fori(0, QT) as turn:
                    chain.enter(turn, HG_CHAIN)
                    head = 4 * l + turn
                    b_row, q_row = hg[:, 4 + turn, :], hg[:, turn, :]
                    one = derived[:, bass.ds(derived_column(f"omlb{l}") + turn, 1)]
                    floor = derived[:, bass.ds(derived_column(f"lbf{l}") + turn, 1)]
                    dve.wait_ge(S("f_sig"), 2 * head + 2)
                    chain.done(TS(decay, decay, one, floor, ALU.mult, ALU.add))
                    TS(b_row, decay, 2.0 ** -50, None, ALU.max).then_inc(S("f_mix"), 1)
                    TS(decay, decay, 2.0 ** 50, 1.0, ALU.mult, ALU.min).then_inc(S("f_mix"), 1)
                    TS(k_hg, k_hg, one, None, ALU.mult).then_inc(S("k_scaled"), 1)
                    dve.wait_ge(S("f_ln"), 2 * head + 2)
                    chain.done(tt(decay, decay, b_row, ALU.add))
                    nc.vector.tensor_tensor_scan(b_row, C("scan128"), decay, 0.0, ALU.mult, ALU.add)\
                        .then_inc(S("b_ready"), 1)
                    dve.wait_ge(S("b_ready"), head + 1)
                    dve.wait_ge(S("k_scaled"), head + 1)

                    def diff(n):
                        if n > 3:
                            job_ready(dve, ("level", l, n - 3), turn)
                        m = 1 << (n - 1)
                        rows = b_row.rearrange("p (b t) -> p b t", t=2 * m)
                        mid = rows[:, :, m - 1:m].to_broadcast([P, T // (2 * m), 2 * m])
                        tt(ring[(n - 1) % 3].rearrange("p (b t) -> p b t", t=2 * m), rows, mid, ALU.subtract)\
                            .then_inc(S("diff_ready"), 1)

                    def fill(n):
                        m = 1 << (n - 1)
                        dve.wait_ge(S("level_exp"), 14 * head + 2 * n)
                        lo, hi = halves(ring[(n - 1) % 3], m)
                        tt(lo, lo, halves(k_hg, m)[0], ALU.mult).then_inc(S("qk_ready"), 1)
                        tt(hi, hi, halves(q_row, m)[1], ALU.mult).then_inc(S("qk_ready"), 1)

                    def pick(n):
                        if n == 0:
                            x = job_ready(dve, ("level", l, 0), turn)
                            job_read(tt(in_chunks(scores, P), in_chunks(x, P), spread(C("hgmask", 0, P), 4),
                                        ALU.mult), ("level", l, 0))
                            return
                        bank, use = jobs(("level", l, n), turn)
                        before, use_before = jobs(("level", l, n - 1), turn)
                        full, read_before = dve.snap(use + 1), dve.snap(use_before + 1)
                        landed(dve)
                        dve.wait_ge(aux_full[bank], full)
                        dve.wait_ge(aux_read[before], read_before)
                        dve.sem_inc(S("level_landed"), 1)
                        mask = spread(C("hgmask", P * n, P), 4).bitcast(I32)
                        job_read(nc.vector.copy_predicated(in_chunks(scores, P), mask,
                                                           in_chunks(aux[bank][:, :], P)), ("level", l, n))

                    diff(1), diff(2), fill(1), diff(3), fill(2), pick(0)
                    diff(4), pick(1), fill(3)
                    diff(5), pick(2), fill(4)
                    diff(6), pick(3), fill(5)
                    diff(7), pick(4), fill(6), fill(7)
                    pick(5), pick(6), pick(7)
                    dve.wait_ge(S("exp_ready"), head + 1)
                    tt(ring[0], q_row, decay, ALU.mult).then_inc(S("q_decayed"), 1)
                    b_chunks = in_chunks(b_row, P)
                    tt(in_chunks(ring[1], P), b_chunks, b_chunks[:, :, P - 1:P].to_broadcast([P, 4, P]),
                       ALU.subtract).then_inc(S("tail_diff"), 1)
                    dve.wait_ge(S("tail_exp"), head + 1)
                    tt(ring[1], ring[1], k_hg, ALU.mult).then_inc(S("k_decayed"), 1)
                    x = job_ready(dve, ("hg_state", l), turn)
                    chain.done(nc.vector.tensor_copy(k_hg[:, 0:P], x[:, 0:P]))
                    chain.done(stt(k_hg[:, P:2 * P], k_hg[:, 0:P], decay[:, 255:256], x[:, P:2 * P],
                                   ALU.mult, ALU.add))
                    job_read(stt(k_hg[:, 2 * P:3 * P], k_hg[:, P:2 * P], decay[:, 383:384], x[:, 2 * P:3 * P],
                                 ALU.mult, ALU.add), ("hg_state", l))
                    x = job_ready(dve, ("hg_out", l), turn)
                    dve.wait_ge(S("hg_rms"), head + 1)
                    gain = vec[:, bass.ds(vec_at[f"hg_g{l}"][0] + turn, 1)]
                    job_read(stt(ring[1], x, gain, scores, ALU.mult, ALU.mult), ("hg_out", l))
                    evacuated_job(dve, ("hg_out", l), turn)
                    tt(hg[:, 12 + turn, :], hg[:, 12 + turn, :], ring[1], ALU.mult).then_inc(split_src, 1)
                    low(SPLITS["hg", l], 8 + turn, hg[:, 12 + turn, :], turn)
                    chain.leave(QT)

                chunks = T // C_RW
                dve.wait_ge(split_lo, SPLITS["hg", l] + 4)
                chain.done(nc.vector.memset(flat[:, 0:QT * (192 + 3 * P)], 0.0))
                nc.vector.memset(state, 0.0).then_inc(S("zeroed"), 1)
                dve.wait_ge(S("zeroed"), l + 1)
                with dve.Fori(0, chunks) as c:
                    chain.enter(c, 1)
                    tokens = bass.ds(c * C_RW, C_RW)
                    done = chunks * l + c
                    dve.wait_ge(S("state_ready"), done)
                    for src, dst in ((P1, ar), (P4, b_bd)):
                        for q in (slice(0, 64), slice(64, 128)):
                            nc.vector.tensor_copy(dst[q, :, q], src[q, :, tokens]).then_inc(S("chunk_dve"), 1)
                    for k in range(4):
                        x = job_ready(dve, ("sc", l, k), c)
                        job_read(tt((m1, m2)[k // 2][:, 2 * (k % 2):2 * (k % 2) + 2, :],
                                    x[:, 0:384].rearrange("p (j n) -> p j n", n=192),
                                    spread(C("mask192"), 2), ALU.mult), ("sc", l, k))
                    evacuated_job(dve, ("sc", l, 0), c)
                    evacuated_job(dve, ("sc", l, 1), c)
                    chain.done(tt(xt_inv, m1[:, :, 0:P], spread(C("level", 0, P), QT), ALU.mult))
                    tt(xt_inv, xt_inv, spread(C("ident"), QT), ALU.add).then_inc(S("x0_ready"), 1)
                    dve.wait_ge(S("x0_ready"), done + 1)
                    for n in range(5):
                        x = job_ready(dve, ("z", l, n), c)
                        job_read(tt(z_sb, in_chunks(x, P), spread(C("level", P * (n + 1), P), QT), ALU.mult),
                                 ("z", l, n))
                        if n < 4:
                            evacuated_job(dve, ("x_turn", l), c) if n == 0 else evacuated_job(dve, ("xz", l, n - 1), c)
                            x = job_ready(dve, ("xz", l, n), c)
                            job_read(tt(x_inv, x_inv, in_chunks(x, P), ALU.add), ("xz", l, n))
                        if n:
                            evacuated_job(dve, ("zx", l, n - 1), c)
                        x = job_ready(dve, ("zx", l, n), c)
                        job_read(tt(xt_inv, xt_inv, in_chunks(x, P), ALU.add), ("zx", l, n))
                    x = job_ready(dve, ("rw_state", l), c)
                    job_read(tt(state, state, in_chunks(x, P), ALU.add), ("rw_state", l))
                    evacuated_job(dve, ("rw_state", l), c)
                    end = chunk_end[:, :, bass.ds(c, 1)].to_broadcast([P, QT, P])
                    tt(state, state, end, ALU.mult).then_inc(S("state_ready"), 1)
                    chain.leave(chunks)

                for j in range(QT):
                    x = job_ready(dve, ("gn_mean", l, j))
                    job_read(stt(P3[:, j, :], x, -1.0 / 64, P3[:, j, :], ALU.mult, ALU.add), ("gn_mean", l, j))
                n = SPLITS["rw", l]
                for j in range(QT):
                    dve.wait_ge(S("gn_rs"), 4 * l + j + 1)
                    y = P3[:, j, :]
                    chain.done(tt(y, y, K_[:, j, :], ALU.mult))
                    chain.done(TS(y, y, V(f"gn_g{l}", j), V(f"gn_b{l}", j), ALU.mult, ALU.add))
                    chain.done(tt(y, y, P2[:, j, :], ALU.add))
                    tt(y, y, Z_[:, j, :], ALU.mult).then_inc(split_src, 1)
                    if j:
                        low(n + j - 1, j - 1, P3[:, j - 1, :])
                low(n + 3, 3, P3[:, 3, :])

                n = SPLITS["merged", l]
                for m in range(KT):
                    b = b_br + m
                    dve.wait_ge(S(f"gate_in{m % 2}"), 32 * (4 * l + m // 2 + 1))
                    g = [P1[:, 2 * (m % 2) + k, :] for k in range(2)]
                    read(tt(g[0], g[0], projected(dve, b), ALU.mult), b)
                    x = job_ready(dve, ("branch_rw", l, m))
                    job_read(tt(g[1], g[1], x, ALU.mult), ("branch_rw", l, m))
                    evacuated(dve, b)
                    evacuated_job(dve, ("branch_rw", l, m))
                    tt(merged[:, m, :], g[0], g[1], ALU.add).then_inc(split_src, 1)
                    if 1 <= m <= 4:
                        low(n + m - 1, 4 + m - 1, merged[:, m - 1, :])
                for m in range(4, KT):
                    low(n + m, m - 4, merged[:, m, :])

                dve.wait_ge(S("x_in"), 32 + 16 * l)
                chain.done(TS(xa[:, :, :], xa[:, :, :], DN_ALPHA, None, ALU.mult))
                for m in range(KT):
                    b = b_out + m
                    read(stt(xa[:, m, :], projected(dve, b), cond[:, l, 16 + m:17 + m], xa[:, m, :],
                             ALU.mult, ALU.add), b)
                    if l == 0:
                        ada_step(1, m)
                x = job_ready(dve, ("ln_mean", l))
                for m in range(KT):
                    evacuated(dve, b_out + m)
                    ins = stt(xa[:, m, :], x, -1.0 / D, xa[:, m, :], ALU.mult, ALU.add)
                    job_read(ins, ("ln_mean", l)) if m == 7 else ins.then_inc(S("xc_ready"), 1)
                dve.wait_ge(S("ln_rs"), l + 1)
                for m in range(KT):
                    chain.done(tt(xa[:, m, :], xa[:, m, :], merged[:, 0, :], ALU.mult))
                    ins = TS(xa[:, m, :], xa[:, m, :], V(f"ln_g{l}", m), V(f"ln_b{l}", m), ALU.mult, ALU.add)
                    ins.then_inc(S("x_done"), 1) if m == 7 else chain.done(ins)
                dve.wait_ge(S("x_done"), l + 1)

            def normed(n, pre, count):
                dve.wait_ge(S("rms_rs"), count)
                for m in range(KT):
                    if m > 1:
                        dve.wait_ge(split_lo, n + m - 1)
                    stt(ST[m % 2], xa[:, m, :], V(pre, m), RS, ALU.mult, ALU.mult).then_inc(split_src, 1)
                    if m:
                        low(n + m - 1, m - 1, ST[(m - 1) % 2])
                low(n + 7, 7, ST[1])

            def onto_x(post, count, x_in, signal):
                dve.wait_ge(S("rms_rs"), count)
                dve.wait_ge(S("x_in"), x_in)
                for m in range(KT):
                    chain.done(stt(OUT[:, m, :], OUT[:, m, :], V(post, m), RS, ALU.mult, ALU.mult))
                    ins = tt(xa[:, m, :], xa[:, m, :], OUT[:, m, :], ALU.add)
                    signal(ins, m)

            normed(SPLITS["lru_h"], "pre0", 1)
            with dve.Fori(0, RT // 4) as turn:
                chain.enter(turn, 12)
                for j in range(4):
                    b = LRU + j
                    dve.wait_ge(proj_read[b % 2], b // 2 + 1 + 2 * turn)
                    dst = X_C[:, 4 * turn + j, :]
                    w = [vec[:, bass.ds(vec_at["conv_w"][0] + RT * k + j + 4 * turn, 1)] for k in range(4)]
                    bias = vec[:, bass.ds(vec_at["conv_b"][0] + j + 4 * turn, 1)]
                    chain.done(TS(dst, stage[:, b % 2, 4:516], w[3], bias, ALU.mult, ALU.add))
                    for k in (2, 1):
                        chain.done(stt(dst, stage[:, b % 2, 1 + k:513 + k], w[k], dst, ALU.mult, ALU.add))
                    stt(dst, stage[:, b % 2, 1:513], w[0], dst, ALU.mult, ALU.add).then_inc(S("conv_done"), 1)
                chain.leave(RT // 4)
            with dve.Fori(0, RT // 4) as turn:
                for j in range(4):
                    b = LRU + RT + j
                    dve.wait_ge(S("sig_staged"), 8 + j + 1 + 4 * turn)
                    read(tt(G_S[:, 4 * turn + j, :], proj[b % 2][:, :], ST[b % 2], ALU.mult), b)
            for g in range(4):
                if g:
                    dve.wait_ge(split_lo, SPLITS["lru_y"] + 3 * g)
                for o in range(3):
                    dve.wait_ge(S("lru_exp"), 3 * g + o + 1)
                    a, u, a2 = LRU_A[:, o, :], LRU_U[:, o, :], xa[:, 4 + o, :]
                    chain.done(tt(a2, a, a, ALU.mult))
                    chain.done(stt(u, a2, 1.0, u, ALU.add, ALU.mult))
                    TS(u, u, 1e-37, None, ALU.max).then_inc(S("lru_u"), 1)
                for o in range(3):
                    t = 3 * g + o
                    a, u, i = LRU_A[:, o, :], LRU_U[:, o, :], xa[:, o, :]
                    evacuated_job(dve, ("lru_gate", g, 3 + o))
                    chain.done(tt(i, i, X_C[:, t, :], ALU.mult))
                    dve.wait_ge(S("lru_sqrt"), t + 1)
                    chain.done(tt(i, i, u, ALU.mult))
                    chain.done(nc.vector.tensor_tensor_scan(u, a, i, 0.0, ALU.mult, ALU.add))
                    tt(xa[:, 4 + o, :], u, G_S[:, t, :], ALU.mult).then_inc(split_src, 1)
                for o in range(3):
                    low(SPLITS["lru_y"] + 3 * g + o, 3 * g + o, xa[:, 4 + o, :])
            for m in range(KT):
                u = LRU_OUT + m
                lru_out_ready(dve, m)
                nc.vector.tensor_copy(OUT[:, m, :], proj[u % 2][:, :]).then_inc(proj_read[u % 2], 1)
            for m in (6, 7):
                left(dve, LRU_OUT + m)
            onto_x("post0", 2, 64, lambda ins, m: ins.then_inc(S("x_done"), 1) if m == 7 else chain.done(ins))
            dve.wait_ge(S("x_done"), 3)

            normed(SPLITS["ret_h"], "pre1", 3)

            def ret_blocks(h):
                q, k, _, gate = ret_tiles(h)
                b0 = RET + 12 * h
                if h == 0:
                    dve.wait_ge(S("tables_in"), 16)
                for n, x in enumerate((q, k)):
                    evacuated(dve, b0 + 2 * n)
                    evacuated(dve, b0 + 2 * n + 1)
                    chain.done(tt(r_qd, x, spread(tables["sin"], 2), ALU.mult))
                    chain.done(tt(x, x, spread(tables["cos"], 2), ALU.mult))
                    tt(x[:, 0, :], x[:, 0, :], r_qd[:, 1, :], ALU.subtract).then_inc(S("rotated"), 1)
                    tt(x[:, 1, :], x[:, 1, :], r_qd[:, 0, :], ALU.add).then_inc(S("rotated"), 1)
                    dve.wait_ge(S("rotated"), 4 * h + 2 * n + 2)
                for v in range(4):
                    b = b0 + 8 + v
                    dve.wait_ge(S("sig_staged"), 20 + 4 * h + v + 1)
                    read(tt(gate[:, v, :], proj[use_of(b) % 2][:, :], ST[b % 2], ALU.mult), b)

            def attend(h):
                q, _, _, gate = ret_tiles(h)
                dve.wait_ge(S("rotated"), 4 * (h + 1))
                for k in range(2):
                    tt(in_chunks(r_qd[:, k, :], P), in_chunks(q[:, k, :], P),
                       spread(tables["qdec"][:, P * h:P * h + P], 4), ALU.mult).then_inc(S("rq_ready"), 1)
                x = job_ready(dve, ("r_score", h))
                job_read(tt(in_chunks(r_scores, P), in_chunks(x, P), spread(tables["dmask"][:, P * h:P * h + P], 4),
                            ALU.mult), ("r_score", h))
                for c in range(3):
                    for k in range(2):
                        x = job_ready(dve, ("r_state", h, c, k))
                        if c == 0:
                            ins = nc.vector.tensor_copy(r_state[:, k, :], x)
                        else:
                            evacuated_job(dve, ("r_state", h, c - 1, k))
                            ins = stt(r_state[:, k, :], r_state[:, k, :], math.exp(P * RET_LOG[h]), x,
                                      ALU.mult, ALU.add)
                        job_read(ins, ("r_state", h, c, k))
                x = job_ready(dve, ("r_mean", h))
                for v in range(4):
                    y = hg[:, 4 * h + v, :]
                    ins = stt(y, x, -1.0 / 512, y, ALU.mult, ALU.add)
                    job_read(ins, ("r_mean", h)) if v == 3 else ins.then_inc(S("ret_c"), 1)
                dve.wait_ge(S("rms_rs"), 4 + h)
                for v in range(4):
                    y = hg[:, 4 * h + v, :]
                    chain.done(tt(y, y, RS, ALU.mult))
                    tt(y, y, gate[:, v, :], ALU.mult).then_inc(split_src, 1)

            ret_blocks(0)
            ret_blocks(1)
            attend(0)
            ret_blocks(2)
            attend(1)
            ret_blocks(3)
            for i in range(8):
                low(SPLITS["ret_y"] + i, i, hg[:, i, :])
            attend(2)
            for i in range(4):
                low(SPLITS["ret_y"] + 8 + i, 8 + i, hg[:, 8 + i, :])
            for m in range(KT):
                b = RET_OUT + m
                read(nc.vector.tensor_copy(OUT[:, m, :], projected(dve, b)), b)
            attend(3)
            for i in range(4):
                low(SPLITS["ret_y"] + 12 + i, i, hg[:, 12 + i, :])
            for m in range(KT):
                b = RET_OUT + KT + m
                evacuated(dve, RET_OUT + m)
                read(tt(OUT[:, m, :], OUT[:, m, :], projected(dve, b), ALU.add), b)
            for m in (6, 7):
                evacuated(dve, RET_OUT + KT + m)
            onto_x("post1", 8, 80, lambda ins, m: ins.then_inc(S("x_final"), 1))

        @block.tensor
        def _(pe):
            MM = nc.tensor.matmul

            def project(b, tiles=tuple(range(KT)), turn=0, bank=None, start=True, stop=True, open_bank=True,
                        rows=tuple(range(KT))):
                s = b % 2
                pe.wait_ge(lo_ready, b + 1 + 4 * turn)
                if bank is None:
                    u = use_of(b)
                    bank = proj[u % 2][:, :]
                    if open_bank:
                        pe.wait_ge(proj_read[u % 2], u // 2 + 2 * turn)
                terms = [(w, a, k, t) for k, t in zip(rows, tiles)
                         for w, a in ((w_hi, act_hi), (w_hi, act_lo), (w_lo, act_hi))]
                for i, (w, a, k, t) in enumerate(terms):
                    ins = MM(bank, w[:, s, k, :], a[:, t, :], start=(start and i == 0),
                             stop=(stop and i == len(terms) - 1))
                return ins

            def used(ins):
                ins.then_inc(block_used, 1)

            def turn_over(dst, src):
                return nc.tensor.transpose(dst, src, C("ident"))

            def sum_squares(key, job, tiles=KT):
                x = job_open(pe, job)
                for m in range(tiles):
                    pe.wait_ge(sq_ready, SQUARES[key] + m + 1)
                    ins = MM(x, C("ones"), ST[m % 2], start=(m == 0), stop=(m == tiles - 1))
                    job_full(ins, job) if m == tiles - 1 else ins.then_inc(sq_used, 1)

            pe.wait_ge(S("const_in"), 32)
            for l in range(DEPTH):
                b_rw, b_hg, b_gate = first["rw", l][0], first["hg", l][0], first["gate", l][0]
                b_br, b_out = first["branch", l][0], first["out", l][0]
                pe.wait_ge(S("ada_used"), 8 * (l + 1))
                x = job_open(pe, ("ada", l))
                for j in range(24):
                    ins = MM(x[:, j:j + 1], ada_acc[:, P * j:P * j + P], C("ones", 0, 1), start=True, stop=True)
                job_full(ins, ("ada", l))
                pe.wait_ge(split_lo, SPLITS["h", l] + 8)
                used(project(b_rw))
                b = b_rw + 1
                if l:
                    used(project(b))
                    b += 1
                with pe.Fori(0, 4) as turn:
                    for j in range(4):
                        used(project(b + j, turn=turn))
                pe.wait_ge(S("tanh_done"), l + 1)
                pe.wait_ge(S("up_in"), 16 + 32 * l)
                for j in range(QT):
                    cols = slice(P * j, P * j + P)
                    for name, q in (("w_up", slice(0, 64)), ("a_up", slice(64, 128))):
                        x = job_open(pe, (name, l, j))
                        job_full(MM(x, xa[q, 0, cols], wa[q, :], start=True, stop=True), (name, l, j))
                if l:
                    evacuated(pe, b_rw + 1)
                    for j in range(QT):
                        x = job_open(pe, ("v_up", l, j))
                        job_full(MM(x, xa[0:32, 2, P * j:P * j + P], xa[0:32, 1, :], start=True, stop=True),
                                 ("v_up", l, j))
                for m in range(4):
                    used(project(b_hg + m))
                for j in range(QT):
                    x = job_open(pe, ("kk_sum", l, j))
                    pe.wait_ge(S("kk_squares"), 4 * l + j + 1)
                    job_full(MM(x, C("bdones"), xa[:, 4 + j, :], start=True, stop=True), ("kk_sum", l, j))
                for j in range(QT):
                    x = job_open(pe, ("rk_sum", l, j))
                    pe.wait_ge(S("rk_ready"), 4 * l + j + 1)
                    job_full(MM(x, C("bdones"), xa[:, j, :], start=True, stop=True), ("rk_sum", l, j))
                with pe.Fori(0, 3) as turn:
                    for j in range(4):
                        used(project(b_hg + 4 + j, turn=turn))

                with pe.Fori(0, QT) as turn:
                    head = 4 * l + turn

                    def level(n):
                        x = job_open(pe, ("level", l, n), turn)
                        if n == 0:
                            pe.wait_ge(S("k_scaled"), head + 1)
                        else:
                            pe.wait_ge(S("qk_ready"), 14 * head + 2 * n)
                        for c in range(4):
                            cols = slice(P * c, P * c + P)
                            if n == 0:
                                rhs = hg[:, turn, cols]
                                ins = MM(x[:, cols], k_hg[:, cols], rhs, start=True, stop=True)
                            else:
                                r = ring[(n - 1) % 3][:, cols]
                                ins = MM(x[:, cols], r, r, start=True, stop=True)
                        job_full(ins, ("level", l, n))

                    used(project(b_gate, turn=turn))
                    x = job_open(pe, ("v_turn", l), turn)
                    pe.wait_ge(S("i_copied"), head + 1)
                    for c in range(4):
                        cols = slice(P * c, P * c + P)
                        ins = turn_over(x[:, cols], ring[3][:, cols])
                    job_full(ins, ("v_turn", l))
                    used(project(b_gate + 1, turn=turn))
                    level(0)
                    level(1)
                    used(project(b_gate + 2, turn=turn))
                    for n in (2, 3, 4):
                        level(n)
                    used(project(b_gate + 3, turn=turn))
                    for n in (5, 6, 7):
                        level(n)
                    x = job_open(pe, ("k_turn", l), turn)
                    pe.wait_ge(S("k_decayed"), head + 1)
                    for c in range(3):
                        cols = slice(P * c, P * c + P)
                        turn_over(x[:, cols], ring[1][:, cols])
                    job_full(turn_over(x[:, 3 * P:], ring[1][:, 3 * P:]), ("k_turn", l))
                    x = job_open(pe, ("hg_state", l), turn)
                    evacuated_job(pe, ("k_turn", l), turn)
                    evacuated_job(pe, ("v_turn", l), turn)
                    for c in range(3):
                        cols = slice(P * c, P * c + P)
                        ins = MM(x[:, cols], ring[2][:, cols], v_tok[:, cols], start=True, stop=True)
                    job_full(ins, ("hg_state", l))
                    x = job_open(pe, ("hg_out", l), turn)
                    evacuated_job(pe, ("level", l, 7), turn)
                    evacuated_job(pe, ("hg_state", l), turn)
                    pe.wait_ge(S("q_decayed"), head + 1)
                    for c in range(4):
                        cols = slice(P * c, P * c + P)
                        ins = MM(x[:, cols], v_tok[:, cols], scores[:, cols], start=True, stop=(c == 0))
                        if c:
                            ins = MM(x[:, cols], k_hg[:, P * (c - 1):P * c], ring[0][:, cols], start=False, stop=True)
                    job_full(ins, ("hg_out", l))
                    x = job_open(pe, ("hg_square", l), turn)
                    pe.wait_ge(S("hg_sq"), head + 1)
                    job_full(MM(x, C("ones"), ring[3], start=True, stop=True), ("hg_square", l))

                chunks = T // C_RW
                pe.wait_ge(S("zeroed"), l + 1)
                with pe.Fori(0, chunks) as c:
                    done = chunks * l + c
                    pe.wait_ge(S("chunk_dve"), 4 * done + 4)
                    pe.wait_ge(S("chunk_act"), 5 * done + 5)
                    for k in range(4):
                        x = job_open(pe, ("sc", l, k), c)
                        keys = (b_bd, k_bd)[k // 2]
                        for i in range(2):
                            j = 2 * (k % 2) + i
                            ins = MM(x[:, 192 * i:192 * i + 192], keys[:, j, :], ar[:, j, :], start=True, stop=True)
                        job_full(ins, ("sc", l, k))
                    for name, src in (("b_turn", b_bd), ("k_turn_rw", k_bd), ("v_turn_rw", v_bd)):
                        x = job_open(pe, (name, l), c)
                        for j in range(QT):
                            ins = turn_over(x[:, P * j:P * j + P], src[:, j, :])
                        job_full(ins, (name, l))

                    def pairs(name, *products, width=P):
                        x = job_open(pe, name, c)
                        for j in range(QT):
                            for i, (a, b) in enumerate(products):
                                ins = MM(x[:, width * j:width * j + width], a[:, j, :], b[:, j, :], start=(i == 0),
                                         stop=(i == len(products) - 1))
                        job_full(ins, name)

                    x = job_open(pe, ("x_turn", l), c)
                    pe.wait_ge(S("x0_ready"), done + 1)
                    for j in range(QT):
                        ins = turn_over(x[:, P * j:P * j + P], xt_inv[:, j, :])
                    job_full(ins, ("x_turn", l))
                    for n in range(5):
                        evacuated_job(pe, ("xz", l, n - 1) if n else ("x_turn", l), c)
                        pairs(("z", l, n), (m1[:, :, 0:P], x_inv))
                        evacuated_job(pe, ("z", l, n), c)
                        if n:
                            evacuated_job(pe, ("zx", l, n - 1), c)
                        if n < 4:
                            pairs(("xz", l, n), (xt_inv, z_sb))
                        pairs(("zx", l, n), (z_sb, xt_inv))
                    pe.wait_ge(S("state_ready"), done)
                    for k in (2, 3):
                        evacuated_job(pe, ("sc", l, k), c)
                    evacuated_job(pe, ("v_turn_rw", l), c)
                    pairs(("rhs", l), (ar[:, :, 0:P], state), (m2[:, :, 0:P], v_tok_rw))
                    evacuated_job(pe, ("rhs", l), c)
                    evacuated_job(pe, ("zx", l, 4), c)
                    pairs(("u", l), (xt_inv, rhs_sb))
                    evacuated_job(pe, ("u", l), c)
                    pairs(("y", l), (state, ar[:, :, P:192]), (u_sb, m1[:, :, P:192]), (v_tok_rw, m2[:, :, P:192]),
                          width=C_RW)
                    evacuated_job(pe, ("b_turn", l), c)
                    evacuated_job(pe, ("k_turn_rw", l), c)
                    pairs(("rw_state", l), (b_tok, u_sb), (k_tok, v_tok_rw))

                evacuated_job(pe, ("y", l), chunks - 1)
                for j in range(QT):
                    x = job_open(pe, ("gn_mean", l, j))
                    job_full(MM(x, C("bdones"), P3[:, j, :], start=True, stop=True), ("gn_mean", l, j))
                for j in range(QT):
                    x = job_open(pe, ("gn_var", l, j))
                    pe.wait_ge(S("gn_sq"), 4 * l + j + 1)
                    job_full(MM(x, C("bdones"), R_[:, j, :], start=True, stop=True), ("gn_var", l, j))
                pe.wait_ge(split_lo, SPLITS["hg", l] + 4)
                for m in range(KT):
                    b = b_br + m
                    if m == 0:
                        pe.wait_ge(split_lo, SPLITS["rw", l] + 4)
                    x = job_open(pe, ("branch_rw", l, m))
                    job_full(project(b, tiles=(0, 1, 2, 3), rows=(4, 5, 6, 7), bank=x), ("branch_rw", l, m))
                    used(project(b, tiles=(8, 9, 10, 11), rows=(0, 1, 2, 3)))
                pe.wait_ge(split_lo, SPLITS["merged", l] + 4)
                x = job_open(pe, ("ln_mean", l))

                def add_up(m):
                    evacuated(pe, b_out + m)
                    return MM(x, C("ones"), xa[:, m, :], start=(m == 0), stop=(m == 7))

                for m in range(KT):
                    b = b_out + m
                    if m == 0:
                        project(b, tiles=(4, 5, 6, 7), rows=(0, 1, 2, 3), stop=False)
                        pe.wait_ge(split_lo, SPLITS["merged", l] + 8)
                        ins = project(b, tiles=(0, 1, 2, 3), rows=(4, 5, 6, 7), start=False, open_bank=False)
                    else:
                        ins = project(b, tiles=(4, 5, 6, 7, 0, 1, 2, 3))
                    used(ins)
                    if m:
                        add_up(m - 1)
                job_full(add_up(7), ("ln_mean", l))
                sum_squares(("ln", l), ("ln_var", l))

            sum_squares("pre0", "rms_pre0")
            pe.wait_ge(split_lo, SPLITS["lru_h"] + 8)
            with pe.Fori(0, 2 * RT // 4) as turn:
                for j in range(4):
                    used(project(LRU + j, turn=turn))
            pe.wait_ge(S("lru_w"), 16)
            gates = flat[:, 8 * T:8 * T + 4 * 14 * P].rearrange("p (g w n k) -> p g w n k", g=4, w=2, n=7)
            pe.wait_ge(S("conv_done"), RT)
            for g in range(4):
                for w in range(2):
                    for o in range(3):
                        name = ("lru_gate", g, 3 * w + o)
                        x = job_open(pe, name)
                        terms = [(n, i) for n, (to, i) in enumerate(BAND) if to == o]
                        for n, i in terms:
                            ins = MM(x, gates[:, g, w, n, :], X_C[:, 3 * g + i, :], start=(n == terms[0][0]),
                                     stop=(n == terms[-1][0]))
                        job_full(ins, name)
            pe.wait_ge(split_lo, SPLITS["lru_y"] + RT)
            for m in range(KT):
                u = LRU_OUT + m
                parts = {0: [(0, range(0, 8), range(0, 8)), (1, range(0, 4), range(8, 12))],
                         1: [(1, range(4, 8), range(0, 4)), (2, range(0, 8), range(4, 12))]}[m % 2]
                pe.wait_ge(proj_read[u % 2], u // 2)
                for i, (b, rows, tiles) in enumerate(parts):
                    ins = project(LRU_OUT + 3 * (m // 2) + b, tiles=tuple(tiles), rows=tuple(rows),
                                  bank=proj[u % 2][:, :], start=(i == 0), stop=(i == 1))
                    if (m % 2, i) == (0, 1):
                        ins.then_inc(S("lru_half"), 1)
                    else:
                        used(ins)
            sum_squares("post0", "rms_post0")

            sum_squares("pre1", "rms_pre1")
            pe.wait_ge(split_lo, SPLITS["ret_h"] + 8)

            def ret_blocks(h):
                b = RET + 12 * h
                with pe.Fori(0, 3) as turn:
                    for j in range(4):
                        used(project(b + j, turn=turn))

            def attend(h):
                q, k_tiles, v_tiles, _ = ret_tiles(h)
                pe.wait_ge(S("rotated"), 4 * (h + 1))
                for k in range(2):
                    x = job_open(pe, ("rk_turn", h, k))
                    for c in range(4):
                        cols = slice(P * c, P * c + P)
                        ins = turn_over(x[:, cols], k_tiles[:, k, cols])
                    job_full(ins, ("rk_turn", h, k))
                for v in range(4):
                    x = job_open(pe, ("rv_turn", h, v))
                    if v == 0:
                        evacuated(pe, RET + 12 * h + 6)
                        evacuated(pe, RET + 12 * h + 7)
                    for c in range(4):
                        cols = slice(P * c, P * c + P)
                        ins = turn_over(x[:, cols], v_tiles[:, v, cols])
                    job_full(ins, ("rv_turn", h, v))
                x = job_open(pe, ("r_score", h))
                for c in range(4):
                    cols = slice(P * c, P * c + P)
                    for k in range(2):
                        ins = MM(x[:, cols], k_tiles[:, k, cols], q[:, k, cols], start=(k == 0), stop=(k == 1))
                job_full(ins, ("r_score", h))
                outs = [job_open(pe, ("r_out", h, v)) for v in range(4)]
                evacuated_job(pe, ("r_score", h))
                pe.wait_ge(S("rq_ready"), 2 * (h + 1))
                for v in range(4):
                    evacuated_job(pe, ("rv_turn", h, v))
                for k in range(2):
                    evacuated_job(pe, ("rk_turn", h, k))
                for c in range(4):
                    cols = slice(P * c, P * c + P)
                    for v in range(4):
                        vs = slice(P * v, P * v + P)
                        ins = MM(outs[v][:, cols], r_vtok[:, c, vs], r_scores[:, cols], start=True, stop=(c == 0))
                        if c:
                            if v == 0:
                                for k in range(2):
                                    evacuated_job(pe, ("r_state", h, c - 1, k))
                            for k in range(2):
                                ins = MM(outs[v][:, cols], r_state[:, k, vs], r_qd[:, k, cols], start=False,
                                         stop=(k == 1))
                        if c == 3:
                            job_full(ins, ("r_out", h, v))
                    if c < 3:
                        for k in range(2):
                            x = job_open(pe, ("r_state", h, c, k))
                            job_full(MM(x, r_ktok[:, k, c, :], r_vtok[:, c, :], start=True, stop=True),
                                     ("r_state", h, c, k))
                x = job_open(pe, ("r_mean", h))
                for v in range(4):
                    evacuated_job(pe, ("r_out", h, v))
                    ins = MM(x, C("ones"), hg[:, 4 * h + v, :], start=(v == 0), stop=(v == 3))
                job_full(ins, ("r_mean", h))
                sum_squares(("ret", h), ("r_var", h), 4)

            ret_blocks(0)
            ret_blocks(1)
            attend(0)
            ret_blocks(2)
            attend(1)
            ret_blocks(3)
            attend(2)
            for m in range(KT):
                if m == 0:
                    pe.wait_ge(split_lo, SPLITS["ret_y"] + 8)
                used(project(RET_OUT + m))
            attend(3)
            pe.wait_ge(split_lo, SPLITS["ret_y"] + 16)
            for m in range(KT):
                used(project(RET_OUT + KT + m, tiles=(8, 9, 10, 11, 0, 1, 2, 3)))
            sum_squares("post1", "rms_post1")


def lay_out(inputs):
    a = {k: np.asarray(v) for k, v in inputs.items()}
    col = lambda v: v.reshape(-1, P).T
    x_t = np.ascontiguousarray(a["x"][0].T).reshape(KT, P, T)
    mats = {"w_in": a["w_in"], "v_down": np.concatenate([a["rw_v_down"]] * 4, 2), "b_hg": a["w_branch_hg"],
            "b_rw": a["w_branch_rw"], "w_out": a["w_out"], "lru_in": a["lru_w_in_2"], "lru_out": a["lru_w_out_2"],
            "ret_in": a["ret_w_in_2"], "ret_out": a["ret_w_out_2"]}
    _, pieces = block_plan()
    wall = np.stack([np.concatenate([mats[n][l, r:r + P, c:c + P] for n, l, r, c in b], 1) for b in pieces])
    v = {"c": col(a["c"][0]), "v0": col(a["rw_v0"][0])}
    for l in range(DEPTH):
        for name, key in (("b_ada", "b_ada"), ("lb", "hg_lower_bounds"), ("hg_g", "hg_norm_g"), ("w0", "rw_w0"),
                          ("a0", "rw_a0"), ("k_k", "rw_k_k"), ("k_a", "rw_k_a"), ("r_k", "rw_r_k"),
                          ("gn_g", "rw_gn_g"), ("gn_b", "rw_gn_b"), ("ln_g", "ln_g"), ("ln_b", "ln_b")):
            v[f"{name}{l}"] = col(a[key][l].reshape(-1))
        mu = col(a["rw_mu"][l])
        v[f"mu{l}"] = np.concatenate([mu[:, 16:17], mu[:, 0:16]], 1)
        v[f"pre{l}"], v[f"post{l}"] = col(a["norm_pre_2"][l]), col(a["norm_post_2"][l])
    v["conv_w"] = np.concatenate([col(a["lru_conv_w_2"][0, k]) for k in range(4)], 1)
    for name, key in (("conv_b", "lru_conv_b_2"), ("b_a", "lru_b_a_2"), ("b_x", "lru_b_x_2"), ("lam", "lru_lambda_2")):
        v[name] = col(a[key][0])
    vec = np.concatenate([v[n] for n, _ in VECTORS], 1)
    up = np.concatenate([a["rw_w_up"], a["rw_a_up"]], 1)
    const, tables = constants()
    gates = np.zeros((2, 4, 384, 384), np.float32)
    for n in range(16):
        g, o = n // 4, 96 * (n % 4)
        gates[0, g, o:o + 96, o:o + 96] = a["lru_w_a_2"][0, n]
        gates[1, g, o:o + 96, o:o + 96] = a["lru_w_x_2"][0, n]
    tiles = [gates[w, g, P * i:P * i + P, P * o:P * o + P] for g in range(4) for w in range(2) for o, i in BAND]
    return {"x_t": x_t, "wall": wall, "w_ada": a["w_ada"].reshape(DEPTH, KT, P, ADA), "vec": vec, "up": up,
            "v_up": a["rw_v_up"][0], "const": const, "tables": tables,
            "lru_gates": np.concatenate(tiles, 1).reshape(P, 4, 14 * P)}


def kernel(**inputs):
    import concourse.bacc as bacc
    from concourse.bass_utils import run_bass_kernel_spmd as run

    arrays = {k: np.ascontiguousarray(v) for k, v in lay_out(inputs).items()}
    nc = bacc.Bacc("TRN2", target_bir_lowering=False, num_devices=1)
    build(nc, {k: v.shape for k, v in arrays.items()})
    got = run(nc, [arrays], core_ids=[0]).results[0]["out"]
    return np.ascontiguousarray(got.reshape(D, T).T)[None]
```

```python
import math
from contextlib import ExitStack

import numpy as np
import concourse.bass as bass
from concourse import mybir

F32 = mybir.dt.float32
F32R = mybir.dt.float32r
I32 = mybir.dt.int32
ALU = mybir.AluOpType
ACT = mybir.ActivationFunctionType

P = 128
T = 512
D = 1024
KT = D // P
DEPTH = 2
HALF = 512
QT = HALF // P
ADA = 3 * D
RNN = 1536
RT = RNN // P
RET_HEADS = 4
C_RW = 64
RW_CHUNKS = T // C_RW
C_HG = 128
DN_ALPHA = (2 * DEPTH) ** 0.25
RW_DECAY = math.exp(-0.5)
RET_LOG = [math.log(1.0 - 2.0 ** (-5.0 - h)) for h in range(RET_HEADS)]


def block_plan():
    first, pieces = {}, []

    def full(name, layer, col, rows=D):
        return [(name, layer, P * k, col) for k in range(rows // P)]

    def add(phase, layer, blocks):
        first[phase, layer] = (len(pieces), len(blocks))
        pieces.extend(blocks)

    for l in range(DEPTH):
        rw = [full("w_in", l, 4096)]
        if l:
            rw += [full("v_down", 0, 0)]
        rw += [full("w_in", l, 2048 + P * m) for m in range(16)]
        add("rw", l, rw)
        add("hg", l, [full("w_in", l, P * m) for m in range(16)])
        add("gate", l, [full("w_in", l, 4224 + P * m) for m in range(16)])
        add("branch", l, [full("b_hg", l, P * m, HALF) + full("b_rw", l, P * m, HALF) for m in range(8)])
        add("out", l, [full("w_out", l, P * m) for m in range(8)])
    add("lru_in", 0, [full("lru_in", 0, P * m) for m in range(2 * RT)])
    tiles = [t for m in range(8) for t in full("lru_out", 0, P * m, RNN)]
    add("lru_out", 0, [tiles[8 * b:8 * b + 8] for b in range(len(tiles) // 8)])
    for h in range(RET_HEADS):
        cols = [256 * h, 256 * h + P, 1024 + 256 * h, 1024 + 256 * h + P]
        cols += [2048 + 512 * h + P * m for m in range(4)] + [4096 + 512 * h + P * m for m in range(4)]
        add("ret_in", h, [full("ret_in", 0, c) for c in cols])
    for half in range(2):
        add("ret_out", half, [[("ret_out", 0, D * half + P * k, P * m) for k in range(KT)] for m in range(8)])
    return first, pieces


VECTORS = [("c", 8)]
for _l in range(DEPTH):
    VECTORS += [(f"{n}{_l}", k) for n, k in (
        ("b_ada", 24), ("lb", 4), ("hg_g", 4), ("mu", 17), ("w0", 4), ("a0", 4), ("k_k", 4), ("k_a", 4),
        ("r_k", 4), ("gn_g", 4), ("gn_b", 4), ("ln_g", 8), ("ln_b", 8))]
VECTORS += [("v0", 4), ("pre0", 8), ("pre1", 8), ("post0", 8), ("post1", 8), ("conv_w", 4 * RT), ("conv_b", RT),
            ("b_a", RT), ("b_x", RT), ("lam", RT)]
CONSTANTS = [("ident", 128), ("ones", 128), ("bdones", 128), ("scan64", 512), ("scan128", 512),
             ("mask192", 192), ("level", 6 * 128), ("hgmask", 8 * 128), ("kdec", 4)]
FIRST_CONST = 3 * 128
TABLES = [("cos", 512), ("sin", 512), ("dmask", 512), ("qdec", 512)]


def columns(spec):
    at, out = 0, {}
    for name, n in spec:
        out[name] = (at, n)
        at += n
    return out, at


def constants():
    i = np.arange(P)
    s, t = i[:, None], i[None, :]
    head = (s // 64) == (t // 64)
    c = {"ident": s == t, "ones": np.ones((P, P)), "bdones": head}
    k = np.arange(T)
    c["scan64"] = np.broadcast_to(k % C_RW != 0, (P, T))
    c["scan128"] = np.broadcast_to(k % C_HG != 0, (P, T))
    c["mask192"] = np.concatenate([head & (s < t), (s % 64) <= np.arange(64)[None, :]], 1)
    low = lambda m: (s // (2 * m) == t // (2 * m)) & (s % (2 * m) >= m) & (t % (2 * m) < m)
    c["level"] = np.concatenate([low(1).T] + [low(m) for m in (2, 4, 8, 16, 32)], 1)
    c["hgmask"] = np.concatenate([s == t] + [low(m).T for m in (1, 2, 4, 8, 16, 32, 64)], 1)
    c["kdec"] = np.exp((P - 1.0 - i)[:, None] * np.array(RET_LOG)[None, :]) / 16.0
    tables = {}
    inv_freq = 10000.0 ** (-np.arange(0, 256, 2, dtype=np.float32) / np.float32(256))
    angle = (np.arange(T, dtype=np.float32)[None, :] * inv_freq.astype(np.float32)[:, None]).astype(np.float32)
    tables["cos"], tables["sin"] = np.cos(angle), np.sin(angle)
    diff = (t - s).astype(np.float64)
    tables["dmask"] = np.concatenate(
        [np.where(diff >= 0, np.exp(np.maximum(diff, 0) * g), 0.0) / 16.0 for g in RET_LOG], 1)
    tables["qdec"] = np.concatenate([np.broadcast_to(np.exp((i + 1.0) * g), (P, P)) for g in RET_LOG], 1)
    return (np.concatenate([np.asarray(c[n], np.float32) for n, _ in CONSTANTS], 1),
            np.concatenate([np.asarray(tables[n], np.float32) for n, _ in TABLES], 1))


BAND = [(0, 0), (0, 1), (1, 0), (1, 1), (1, 2), (2, 1), (2, 2)]


HG_CHAIN = 4


class Jobs:

    def __init__(self):
        self.table, self.used = {}, [0] * 6

    def add(self, name, bank):
        self.table[name] = (bank, self.used[bank], 0)
        self.used[bank] += 1

    def loop(self, names, turns):
        per = [sum(b == k for _, b in names) for k in range(6)]
        at = list(self.used)
        for name, bank in names:
            self.table[name] = (bank, at[bank], per[bank])
            at[bank] += 1
        self.used = [u + p * turns for u, p in zip(self.used, per)]

    def __call__(self, name, turn=0):
        bank, base, step = self.table[name]
        return bank, turn * step + base


def job_plan():
    jobs = Jobs()
    for l in range(DEPTH):
        jobs.add(("ada", l), 0)
        if l == 0:
            jobs.add("ada_gate", 0)
        for j in range(QT):
            jobs.add(("w_up", l, j), j)
        for j in range(QT):
            jobs.add(("a_up", l, j), 4 + j % 2)
        if l:
            for j in range(QT):
                jobs.add(("v_up", l, j), j)
        for name in ("kk_sum", "rk_sum"):
            for j in range(QT):
                jobs.add((name, l, j), j)
        jobs.loop([(("v_turn", l), 0)] + [(("level", l, n), 1 + n % 2) for n in range(8)]
                  + [(("k_turn", l), 3), (("hg_state", l), 4), (("hg_out", l), 5), (("hg_square", l), 0)], QT)
        def scores(s):
            return [(("sc", l, s, k), b) for k, b in enumerate((3, 4, 5, 3))]

        def chunk(s, last=False):
            names = [(("b_turn", l, s), 4), (("k_turn_rw", l, s), 5), (("v_turn_rw", l, s), 4), (("rhs", l, s), 3)]
            names += [] if last else scores(s)
            names += [(("u", l, s), 4), (("y", l, s), 5), (("rw_state", l, s), 3)]
            levels = [(name, l, s, n, half) for n in range(5) for name in ("z", "x") for half in range(2)]
            names += [(name, k % 3) for k, name in enumerate(levels)]
            return names + ([] if last else [(("x_turn", l, s), 2)])

        for name, bank in scores("P") + [(("x_turn", l, "P"), 2)]:
            jobs.add(name, bank)
        jobs.loop(chunk("A") + chunk("B"), RW_CHUNKS // 2 - 1)
        for name, bank in chunk("C") + chunk("D", last=True):
            jobs.add(name, bank)
        for j in range(QT):
            jobs.add(("gn_mean", l, j), j)
        for j in range(QT):
            jobs.add(("gn_var", l, j), j)
        for m in range(KT):
            jobs.add(("branch_rw", l, m), m % 2)
        jobs.add(("ln_mean", l), 2)
        jobs.add(("ln_var", l), 3)
    jobs.add("rms_pre0", 2)
    for g in range(4):
        for w in range(6):
            jobs.add(("lru_gate", g, w), w)
    jobs.add("rms_post0", 2)
    jobs.add("rms_pre1", 3)
    for h in range(RET_HEADS):
        for k in range(2):
            jobs.add(("rk_turn", h, k), 4 + k)
        for v in range(4):
            jobs.add(("rv_turn", h, v), v)
        jobs.add(("r_score", h), 4)
        for v in range(4):
            jobs.add(("r_out", h, v), v)
        for c in range(3):
            for k in range(2):
                jobs.add(("r_state", h, c, k), 4 + k)
        jobs.add(("r_mean", h), 4)
        jobs.add(("r_var", h), 5)
    jobs.add("rms_post1", 2)
    return jobs


class Chain:

    def __init__(self, eng, sem):
        self.eng, self.sem, self.n, self.turn, self.per = eng, sem, 0, None, 0

    def done(self, ins):
        ins.then_inc(self.sem, 1)
        self.n += 1
        self.eng.wait_ge(self.sem, self.n if self.turn is None else self.turn * self.per + self.n)

    def enter(self, turn, per):
        self.turn, self.per, self.start = turn, per, self.n

    def leave(self, turns):
        assert self.n - self.start == self.per, (self.n - self.start, self.per)
        self.n = self.start + self.per * turns
        self.turn = None


def build(nc, shapes):
    first, pieces = block_plan()
    jobs = job_plan()
    blocks = len(pieces)

    dram = {k: nc.dram_tensor(k, s, F32, kind="ExternalInput").ap() for k, s in shapes.items()}
    out = nc.dram_tensor("out", (KT, P, T), F32, kind="ExternalOutput").ap()
    gate_scr = nc.dram_tensor("gate_scr", (DEPTH, 16, P, T), F32).ap()
    x_scr = nc.dram_tensor("x_scr", (3, KT, P, T), F32).ap()
    v_scr = nc.dram_tensor("v_scr", (QT, P, T), F32).ap()

    with ExitStack() as ctx:
        def sb(name, shape, dt=F32):
            return ctx.enter_context(nc.sbuf_tensor(f"{name}_sb", shape, dt))

        def sem(name):
            return ctx.enter_context(nc.semaphore(name))

        act_hi, act_lo = sb("act_hi", [P, 12, T], F32R), sb("act_lo", [P, 12, T], F32R)
        w_raw = sb("w_raw", [P, 2, KT * P])
        w_hi, w_lo = sb("w_hi", [P, 2, KT, P], F32R), sb("w_lo", [P, 2, KT, P], F32R)
        slots = sb("slots", [P, 8, 4, T])
        area = sb("area", [P, 24, T])
        xa, hg = area[:, 0:8], area[:, 8:24]
        vec_at, vec_n = columns(VECTORS)
        const_at, const_n = columns(CONSTANTS)
        vec, const = sb("vec", [P, vec_n]), sb("const", [P, const_n])
        stage = sb("stage", [P, 2, 516])
        wa = sb("wa", [P, T])
        cond = sb("cond", [P, DEPTH, 24])
        derived = sb("derived", [P, 160])
        chunk_end = sb("chunk_end", [P, QT, T // C_RW])
        ST = [stage[:, i, 4:516] for i in range(2)]

        def V(name, k=None, n=1):
            at, size = vec_at[name]
            return vec[:, at:at + size] if k is None else vec[:, at + k:at + k + n]

        def C(name, lo=0, n=None):
            at, size = const_at[name]
            return const[:, at + lo:at + (size if n is None else lo + n)]

        derived_at, derived_first, used = {}, {}, 0
        for name, n in [("c", 8), ("lb_t", 12), ("cl", RT), ("cl_t", RT)] + [
                (f"{k}{l}", n) for l in range(DEPTH)
                for k, n in (("mu1", 17), ("omlb", 4), ("lbf", 4), ("ka1", 4))]:
            derived_at[name] = derived[:, used:used + n]
            derived_first[name] = used
            used += n
        assert used <= 160
        DV = derived_at

        proj = [ctx.enter_context(nc.psum_tensor(f"proj{i}", [P, T], F32)) for i in range(2)]
        aux = [ctx.enter_context(nc.psum_tensor(f"aux{i}", [P, T], F32)) for i in range(6)]

        raw_in = [sem(f"raw_in{i}") for i in range(2)]
        hi_ready, lo_ready, block_used = sem("hi_ready"), sem("lo_ready"), sem("block_used")
        proj_read = [sem(f"proj_read{i}") for i in range(2)]
        aux_full = [sem(f"aux_full{i}") for i in range(6)]
        aux_read = [sem(f"aux_read{i}") for i in range(6)]
        split_src, split_hi, split_lo = sem("split_src"), sem("split_hi"), sem("split_lo")
        sq_ready, sq_used = sem("sq_ready"), sem("sq_used")
        made = {}

        def S(name):
            if name not in made:
                made[name] = sem(name)
            return made[name]

        RW_LAST = [first["rw", l][0] + first["rw", l][1] - 1 for l in range(DEPTH)]
        SPLITS = {("h", 0): 0, ("hg", 0): 8, ("rw", 0): 12, ("merged", 0): 16, ("h", 1): 24, ("hg", 1): 32,
                  ("rw", 1): 36, ("merged", 1): 40, "lru_h": 48, "lru_y": 56, "ret_h": 68, "ret_y": 76}
        SQUARES = {("ln", 0): 0, ("ln", 1): 8, "pre0": 16, "post0": 24, "pre1": 32,
                   **{("ret", h): 40 + 4 * h for h in range(RET_HEADS)}, "post1": 56}
        R_, K_, V_, Z_, P1, P2, P3, P4 = (slots[:, i] for i in range(8))
        merged = slots[:, 0:2].rearrange("p a b t -> p (a b) t")
        ada_acc = slots[:, 2:4].rearrange("p a b t -> p (a b t)")[:, 0:ADA]
        ada_in = slots[:, 5:8].rearrange("p a b t -> p (a b t)").rearrange("p (s n) -> p s n", s=2)

        def wait(eng, semaphore, value):
            if not (isinstance(value, int) and value <= 0):
                eng.wait_ge(semaphore, value)

        def use_of(b):
            return b if b < first["lru_out", 0][0] else b - 4

        def projected(eng, b, turn=0, steps=4):
            eng.wait_ge(block_used, b + 1 + steps * turn)
            return proj[use_of(b) % 2][:, :]

        def read(ins, b):
            return ins.then_inc(proj_read[use_of(b) % 2], 1)

        def evacuated(eng, b):
            u = use_of(b)
            eng.wait_ge(proj_read[u % 2], u // 2 + 2)

        def job_open(eng, name, turn=0):
            bank, use = jobs(name, turn)
            wait(eng, aux_read[bank], use)
            return aux[bank][:, :]

        def job_full(ins, name):
            return ins.then_inc(aux_full[jobs(name)[0]], 1)

        def job_ready(eng, name, turn=0):
            bank, use = jobs(name, turn)
            eng.wait_ge(aux_full[bank], use + 1)
            return aux[bank][:, :]

        def job_read(ins, name):
            return ins.then_inc(aux_read[jobs(name)[0]], 1)

        def evacuated_job(eng, name, turn=0):
            bank, use = jobs(name, turn)
            eng.wait_ge(aux_read[bank], use + 1)

        def left(eng, u):
            eng.wait_ge(proj_read[u % 2], u // 2 + 2)

        def lru_out_ready(eng, m):
            if m % 2:
                eng.wait_ge(block_used, first["lru_out", 0][0] + 3 * (m // 2) + 3)
            else:
                eng.wait_ge(S("lru_half"), m // 2 + 1)

        def landed(eng):
            eng.wait_ge(S("vec_in"), 16)

        def derived_column(name):
            return derived_first[name]

        def in_chunks(ap, n):
            return ap.rearrange("p (c t) -> p c t", t=n)

        ring = [xa[:, i] for i in range(4)]
        v_tok, k_hg, decay, scores = xa[:, 4], xa[:, 5], xa[:, 6], xa[:, 7]

        flat = area[:, :, :].rearrange("p a t -> p (a t)")
        taken = [0]

        def carve(width):
            at = taken[0]
            taken[0] += QT * width
            return flat[:, at:at + QT * width].rearrange("p (j n) -> p j n", j=QT)

        m1, m2 = [carve(192), carve(192)], [carve(192), carve(192)]
        xt_inv = [carve(P), carve(P)]
        x_inv = carve(P)
        b_tok, k_tok, v_tok_rw = carve(P), carve(P), carve(P)
        z_sb, rhs_sb, u_sb, state = carve(P), carve(P), carve(P), carve(P)
        zeros_at = taken[0]
        ar = [carve(192), carve(192)]
        b_bd, k_bd, v_bd = carve(P), carve(P), carve(P)
        zeros = flat[:, zeros_at:taken[0]]
        assert 16 * T <= zeros_at and taken[0] <= 22 * T
        assert taken[0] <= 24 * T

        def rw_chunks(eng, chunk, last_pair=RW_CHUNKS - 2):
            with eng.Fori(0, RW_CHUNKS // 2 - 1) as turn:
                chunk(2 * turn, 0, "A", turn)
                chunk(2 * turn + 1, 1, "B", turn)
            chunk(last_pair, 0, "C", 0)
            chunk(last_pair + 1, 1, "D", 0)

        PAIRS = ((0, 1), (2, 3))
        HALF_PAIRS = (slice(0, 2), slice(2, 4))

        def chunk_at(c):
            return bass.ds(c * C_RW, C_RW)

        block = ctx.enter_context(nc.Block())

        @block.sync
        def _(sp):
            def load_block(b, turn=0):
                wait(sp, lo_ready, b - 1 + 2 * turn)
                sp.dma_start(w_raw[:, b % 2, :], dram["wall"][b + 2 * turn]).then_inc(raw_in[b % 2], 16)

            at = [0]

            def blocks_to(end):
                end = min(end, blocks)
                while at[0] < min(2, end):
                    load_block(at[0])
                    at[0] += 1
                n = (end - at[0]) // 2
                if n > 1:
                    start = at[0]
                    with sp.Fori(0, n) as turn:
                        for b in (start, start + 1):
                            load_block(b, turn)
                    at[0] += 2 * n
                while at[0] < end:
                    load_block(at[0])
                    at[0] += 1

            for i in range(2):
                sp.sem_inc(S(f"gate_out{i}"), 16)
            sp.dma_start(vec[:, :], dram["vec"]).then_inc(S("vec_in"), 16)
            sp.dma_start(const[:, 0:FIRST_CONST], dram["const"][:, 0:FIRST_CONST]).then_inc(S("const_in"), 16)
            sp.dma_start(xa[:, :, :], dram["x_t"].rearrange("k p t -> p k t")).then_inc(S("x_in"), 16)

            def load_ada(l, k):
                n = 8 * l + k
                wait(sp, S("ada_used"), n - 1)
                cols = slice(0, ADA if l else 2 * D)
                sp.dma_start(ada_in[:, k % 2, cols], dram["w_ada"][l, k][:, cols]).then_inc(S(f"ada_in{k % 2}"), 16)

            for k in range(KT):
                if k == 6:
                    blocks_to(2)
                load_ada(0, k)
            for l in range(DEPTH):
                b_rw, b_hg, b_gate = first["rw", l][0], first["hg", l][0], first["gate", l][0]
                b_br, b_out = first["branch", l][0], first["out", l][0]
                if l == 0:
                    blocks_to(2)
                    sp.dma_start(const[:, FIRST_CONST:], dram["const"][:, FIRST_CONST:]).then_inc(S("masks_in"), 16)
                    blocks_to(4)
                    sp.dma_start(hg.rearrange("p (k h) t -> p k (h t)", k=KT),
                                 dram["w_ada"][0].rearrange("k p n -> p k n")[:, :, 2 * D:]).then_inc(S("gate_cols"), 16)
                blocks_to(b_rw + 4)
                if l:
                    sp.wait_ge(S("x_done"), KT * l)
                    sp.dma_start(x_scr[0].rearrange("k p t -> p k t"), xa[:, :, :]).then_inc(S("x_saved"), 16)
                    sp.wait_ge(S("x_saved"), 16)
                sp.wait_ge(split_lo, SPLITS["h", l] + 8)
                sp.dma_start(xa[:, 0, :], dram["up"][l]).then_inc(S("up_in"), 16)
                if l:
                    sp.dma_start(xa[0:32, 2, :], dram["v_up"]).then_inc(S("up_in"), 16)
                    sp.wait_ge(S("v_out"), 16)
                    sp.dma_start(xa[:, 4:8, :], v_scr.rearrange("k p t -> p k t")).then_inc(S("v_in"), 16)
                blocks_to(b_hg + 3)
                if not l:
                    for b in (RW_LAST[0] - 5, RW_LAST[0] - 4):
                        evacuated(sp, b)
                    sp.dma_start(v_scr.rearrange("k p t -> p k t"), V_).then_inc(S("v_out"), 16)
                for m in range(16):
                    blocks_to(b_gate + m + 3)
                    evacuated(sp, b_gate + m)
                    sp.dma_start(gate_scr[l, m], ST[(b_gate + m) % 2]).then_inc(S(f"gate_out{(b_gate + m) % 2}"), 16)
                for m in range(KT):
                    blocks_to(b_br + m + 4)
                    if m == 0:
                        sp.wait_ge(S("state_ready"), (RW_CHUNKS + 1) * (l + 1))
                        for k in range(2):
                            sp.wait_ge(S(f"gate_out{k}"), 128 * (l + 1) + 16)
                    if m > 1:
                        sp.wait_ge(split_src, SPLITS["merged", l] + m - 1)
                    for k in range(2):
                        sp.dma_start(P1[:, 2 * (m % 2) + k, :], gate_scr[l, 8 * k + m])\
                            .then_inc(S(f"gate_in{m % 2}"), 16)
                    if m == 1:
                        evacuated_job(sp, ("y", l, "D"))
                        src = x_scr[0] if l else dram["x_t"]
                        sp.dma_start(xa[:, :, :], src.rearrange("k p t -> p k t")).then_inc(S("x_in"), 16)
                if not l:
                    sp.wait_ge(split_lo, SPLITS["rw", 0] + 4)
                    for k in range(KT):
                        load_ada(1, k)
                        blocks_to(b_out + 4 + k)
            lru = first["lru_in", 0][0]
            blocks_to(lru + 4)
            sp.wait_ge(S("x_done"), KT * 2)
            sp.dma_start(x_scr[1].rearrange("k p t -> p k t"), xa[:, :, :]).then_inc(S("x_saved"), 16)
            sp.dma_start(flat[:, 8 * T:8 * T + 4 * 14 * P], dram["lru_gates"].rearrange("p g n -> p (g n)"))\
                .then_inc(S("lru_w"), 16)
            blocks_to(first["lru_out", 0][0] + 3)
            sp.wait_ge(split_lo, SPLITS["lru_y"] + RT)
            sp.wait_ge(S("x_saved"), 32)
            sp.dma_start(xa[:, :, :], x_scr[1].rearrange("k p t -> p k t")).then_inc(S("x_in"), 16)
            ret = first["ret_in", 0][0]
            blocks_to(ret + 4)
            sp.wait_ge(S("x_done"), KT * 3)
            sp.dma_start(x_scr[2].rearrange("k p t -> p k t"), xa[:, :, :]).then_inc(S("x_saved"), 16)
            sp.wait_ge(S("x_saved"), 48)
            sp.wait_ge(split_lo, SPLITS["ret_h"] + 8)
            sp.dma_start(xa[:, 0:4, :].rearrange("p a t -> p (a t)"), dram["tables"]).then_inc(S("tables_in"), 16)
            blocks_to(first["ret_out", 1][0] + 3)
            sp.wait_ge(split_lo, SPLITS["ret_y"] + 16)
            sp.dma_start(xa[:, :, :], x_scr[2].rearrange("k p t -> p k t")).then_inc(S("x_in"), 16)
            blocks_to(blocks)
            for m in range(KT):
                sp.wait_ge(S("x_final"), m + 1)
                sp.dma_start(out[m], xa[:, m, :]).then_inc(S("out_done"), 16)
            sp.wait_ge(S("out_done"), 16 * KT)
            sp.wait_ge(S("x_saved"), 48)

        @block.gpsimd
        def _(pool):
            def low(b, turn=0):
                pool.wait_ge(hi_ready, b + 1 + 2 * turn)
                nc.gpsimd.tensor_tensor(w_lo[:, b % 2, :, :].rearrange("p k n -> p (k n)"), w_raw[:, b % 2, :],
                                        w_hi[:, b % 2, :, :].rearrange("p k n -> p (k n)").bitcast(F32),
                                        ALU.subtract).then_inc(lo_ready, 1)

            def low_blocks(start, end):
                n = (end - start) // 2
                with pool.Fori(0, n) as turn:
                    low(start, turn)
                    low(start + 1, turn)
                if start + 2 * n < end:
                    low(end - 1)

            at = 0
            for l in range(DEPTH):
                low_blocks(at, first["gate", l][0] + 14)
                at = first["gate", l][0] + 14
                pool.wait_ge(S("i_copied"), QT * (l + 1))
                pool.wait_ge(split_lo, SPLITS["hg", l] + 2)
                nc.gpsimd.memset(zeros, 0.0).then_inc(S("zeroed"), 1)
            low_blocks(at, blocks)

        LRU, LRU_OUT, RET, RET_OUT = (first[k, 0][0] for k in ("lru_in", "lru_out", "ret_in", "ret_out"))
        X_C = slots[:, 0:3].rearrange("p a b t -> p (a b) t")
        G_S = slots[:, 3:6].rearrange("p a b t -> p (a b) t")
        OUT = slots[:, 0:2].rearrange("p a b t -> p (a b) t")
        RS = slots[:, 7, 3, :]
        LRU_A, LRU_U = slots[:, 6], slots[:, 7]
        r_ktok = slots[:, 7, 0:2, :].rearrange("p k (c n) -> p k c n", n=P)
        r_vtok = slots[:, 6].rearrange("p a t -> p (a t)").rearrange("p (c n) -> p c n", n=512)
        r_scores = slots[:, 7, 2, :]
        r_qd = xa[:, 4:6]
        r_state = xa[:, 6:8]
        tables = dict(zip(("cos", "sin", "dmask", "qdec"), (xa[:, i] for i in range(4))))

        def ret_tiles(h):
            s = 3 * (h % 2)
            return slots[:, s, 0:2], slots[:, s, 2:4], slots[:, s + 1], slots[:, s + 2]

        def halves(ap, m):
            v = ap.rearrange("p (b h m) -> p b h m", h=2, m=m)
            return v[:, :, 0, :], v[:, :, 1, :]

        @block.scalar
        def _(act):
            chain = Chain(act, S("act_chain"))
            A = nc.scalar.activation

            def weights(b, turn=0):
                if b >= blocks:
                    return
                act.wait_ge(raw_in[b % 2], 16 * (b // 2 + 1) + 32 * turn)
                wait(act, block_used, b - 1 + 4 * turn)
                A(w_hi[:, b % 2, :, :].rearrange("p k n -> p (k n)"), w_raw[:, b % 2, :], ACT.Copy)\
                    .then_inc(hi_ready, 1)

            def high(n, slot, src, turn=0):
                act.wait_ge(split_src, n + 1 + turn)
                if not isinstance(turn, int):
                    landed(act)
                A(act_hi[:, slot, :], src, ACT.Copy).then_inc(split_hi, 1)

            def square(key, m, src):
                if m > 1:
                    act.wait_ge(sq_used, SQUARES[key] - list(SQUARES).index(key) + m - 1)
                A(ST[m % 2], src, ACT.Square).then_inc(sq_ready, 1)

            def inverse_root(dst, job, scale, eps, signal, turn=0):
                x = job_ready(act, job, turn)
                job_read(A(dst, x, ACT.Ln, scale=scale, bias=eps), job)
                evacuated_job(act, job, turn)
                A(dst, dst, ACT.Exp, scale=-0.5).then_inc(signal, 1)

            act.wait_ge(S("vec_in"), 16)
            A(DV["c"], V("c"), ACT.Sigmoid).then_inc(S("c_sig"), 1)
            act.wait_ge(S("setup_dve"), 1)
            chain.done(A(DV["lb_t"][:, 4:12], DV["lb_t"][:, 4:12], ACT.Exp))
            chain.done(A(DV["cl_t"], DV["cl_t"], ACT.Exp, scale=-1.0))
            A(DV["cl_t"], DV["cl_t"], ACT.Ln, bias=1.0).then_inc(S("setup_act"), 1)
            weights(0)
            weights(1)
            for l in range(DEPTH):
                b_rw, b_hg, b_gate = first["rw", l][0], first["hg", l][0], first["gate", l][0]
                b_br, b_out = first["branch", l][0], first["out", l][0]
                for m in range(KT):
                    high(SPLITS["h", l] + m, m, ST[m % 2])

                def scaled(b, k, turn=0):
                    weights(b + 2, turn)
                    x = projected(act, b, turn)
                    at = vec_at[f"mu{l}"][0] + k
                    landed(act)
                    A(ST[b % 2], x, ACT.Copy, scale=vec[:, bass.ds(at + 4 * turn, 1)]).then_inc(S("mu_scaled"), 1)

                scaled(b_rw, 0)
                evacuated(act, b_rw)
                A(wa[0:64, :], wa[0:64, :], ACT.Tanh).then_inc(S("tanh_done"), 1)
                b = b_rw + 1
                if l:
                    weights(b + 2)
                    act.wait_ge(S("x_saved"), 16)
                    read(A(xa[:, 1, :], projected(act, b), ACT.Copy), b)
                    b += 1
                with act.Fori(0, 4) as turn:
                    for j in range(4):
                        scaled(b + j, 1 + j, turn)
                for j in range(QT):
                    x = job_ready(act, ("w_up", l, j))
                    job_read(A(P1[:, j, :], x, ACT.Sigmoid, bias=V(f"w0{l}", j)), ("w_up", l, j))
                    x = job_ready(act, ("a_up", l, j))
                    job_read(A(P2[:, j, :], x, ACT.Sigmoid, bias=V(f"a0{l}", j)), ("a_up", l, j))
                if l:
                    for j in range(QT):
                        x = job_ready(act, ("v_up", l, j))
                        job_read(A(P3[:, j, :], x, ACT.Sigmoid, bias=V("v0", j)), ("v_up", l, j))
                evacuated(act, b_hg - 1)
                evacuated(act, b_hg - 2)
                A(P4, Z_, ACT.Sigmoid).then_inc(S("z_sig"), 1)
                if l == 0:
                    evacuated_job(act, "ada_gate")
                for j in range(QT):
                    act.wait_ge(S("kk0_ready"), 4 * l + j + 1)
                    A(xa[:, 4 + j, :], P4[:, j, :], ACT.Square).then_inc(S("kk_squares"), 1)

                def keep(m):
                    weights(b_hg + m + 2)
                    read(A(hg[:, m, :], projected(act, b_hg + m), ACT.Copy), b_hg + m)

                for m in range(4):
                    keep(m)
                for j in range(QT):
                    evacuated_job(act, ("kk_sum", l, j))
                chain.done(A(xa[:, 4:8, :], xa[:, 4:8, :], ACT.Ln, scale=2.0 ** 20))
                A(xa[:, 4:8, :], xa[:, 4:8, :], ACT.Exp, scale=-0.5, bias=10.0 * math.log(2.0))\
                    .then_inc(S("norm_ready"), 1)
                act.wait_ge(S("decay_ex"), l + 1)
                A(P1, P1, ACT.Exp, scale=-RW_DECAY).then_inc(S("decay_exp"), 1)
                for m in range(4, 8):
                    keep(m)
                act.wait_ge(S("bn_ready"), l + 1)
                A(P2, P3, ACT.Exp, scale=RW_DECAY).then_inc(S("decay_in"), 1)
                A(P3, P3, ACT.Exp, scale=-RW_DECAY).then_inc(S("decay_all"), 1)
                for m in range(8, 12):
                    keep(m)
                for m in range(12, 16):
                    b = b_hg + m
                    weights(b + 2)
                    A(ST[b % 2], projected(act, b), ACT.Sigmoid).then_inc(S("sig_staged"), 1)

                act.wait_ge(S("dve_prep"), l + 1)
                for k in (14, 15):
                    evacuated(act, b_hg + k)
                def forget_gate(turn):
                    landed(act)
                    A(decay, hg[:, 4 + turn, :], ACT.Sigmoid).then_inc(S("f_sig"), 1)
                    A(k_hg, hg[:, 4 + turn, :], ACT.Sigmoid, scale=-1.0).then_inc(S("f_sig"), 1)
                    landed(act)
                    A(ring[3], hg[:, 8 + turn, :], ACT.Copy).then_inc(S("i_copied"), 1)

                def hg_head(turn, last):
                    head = 4 * l + turn
                    act.wait_ge(S("f_mix"), 2 * head + 2)
                    A(decay, decay, ACT.Ln).then_inc(S("f_ln"), 1)
                    A(hg[:, 4 + turn, :], hg[:, 4 + turn, :], ACT.Ln).then_inc(S("f_ln"), 1)

                    def gate(g):
                        b = b_gate + g
                        weights(b + 2, turn)
                        x = projected(act, b, turn)
                        act.wait_ge(S(f"gate_out{b % 2}"), 16 * (8 * l + g // 2 + 1) + 32 * turn)
                        read(A(ST[b % 2], x, ACT.Copy), b)

                    def level(n):
                        act.wait_ge(S("diff_ready"), 7 * head + n)
                        r = ring[(n - 1) % 3]
                        lo, hi = halves(r, 1 << (n - 1))
                        A(lo, lo, ACT.Exp, scale=-1.0).then_inc(S("level_exp"), 1)
                        A(hi, hi, ACT.Exp).then_inc(S("level_exp"), 1)

                    gate(0)
                    job_read(A(v_tok, job_ready(act, ("v_turn", l), turn), ACT.Copy), ("v_turn", l))
                    level(1)
                    A(decay, hg[:, 4 + turn, :], ACT.Exp).then_inc(S("exp_ready"), 1)
                    gate(1)
                    for n in (2, 3, 4):
                        level(n)
                    gate(2)
                    for n in (5, 6, 7):
                        level(n)
                    act.wait_ge(S("tail_diff"), head + 1)
                    A(ring[1], ring[1], ACT.Exp, scale=-1.0).then_inc(S("tail_exp"), 1)
                    job_read(A(ring[2], job_ready(act, ("k_turn", l), turn), ACT.Copy), ("k_turn", l))
                    gate(3)
                    x = job_ready(act, ("hg_out", l), turn)
                    A(ring[3], x, ACT.Square).then_inc(S("hg_sq"), 1)
                    inverse_root(scores, ("hg_square", l), 1.0 / P, 1e-6, S("hg_rms"), turn)
                    if not last:
                        forget_gate(turn + 1)
                    high(SPLITS["hg", l], 8 + turn, hg[:, 12 + turn, :], turn)

                forget_gate(0)
                with act.Fori(0, QT - 1) as turn:
                    hg_head(turn, False)
                hg_head(QT - 1, True)

                def operands(c, odd):
                    landed(act)
                    for src, dst in ((K_, k_bd), (V_, v_bd)):
                        for q in (slice(0, 64), slice(64, 128)):
                            A(dst[q, :, q], src[q, :, chunk_at(c)], ACT.Copy).then_inc(S("chunk_act"), 1)
                    A(ar[odd][:, :, 128:192], R_[:, :, chunk_at(c)], ACT.Copy).then_inc(S("chunk_act"), 1)

                def chunk(c, odd, s, turn):
                    def take(dst, job):
                        x = job_ready(act, job, turn)
                        job_read(A(dst, in_chunks(x, P), ACT.Copy), job)

                    take(b_tok, ("b_turn", l, s))
                    take(k_tok, ("k_turn_rw", l, s))
                    take(v_tok_rw, ("v_turn_rw", l, s))
                    if s != "D":
                        operands(c + 1, 1 - odd)
                    take(rhs_sb, ("rhs", l, s))
                    take(u_sb, ("u", l, s))
                    x = job_ready(act, ("y", l, s), turn)
                    landed(act)
                    job_read(A(P3[:, :, chunk_at(c)], in_chunks(x[:, 0:QT * C_RW], C_RW), ACT.Copy), ("y", l, s))
                    if s != "D":
                        take(x_inv, ("x_turn", l, s))

                act.wait_ge(S("zeroed"), l + 1)
                operands(0, 0)
                job_read(A(x_inv, in_chunks(job_ready(act, ("x_turn", l, "P")), P), ACT.Copy), ("x_turn", l, "P"))
                rw_chunks(act, chunk)

                act.wait_ge(S("state_ready"), (RW_CHUNKS + 1) * (l + 1))
                for j in range(QT):
                    evacuated_job(act, ("gn_mean", l, j))
                    A(R_[:, j, :], P3[:, j, :], ACT.Square).then_inc(S("gn_sq"), 1)
                for j in range(QT):
                    x = job_ready(act, ("gn_var", l, j))
                    job_read(A(K_[:, j, :], x, ACT.Ln, scale=1.0 / 64, bias=64e-5), ("gn_var", l, j))
                for j in range(QT):
                    evacuated_job(act, ("gn_var", l, j))
                    A(K_[:, j, :], K_[:, j, :], ACT.Exp, scale=-0.5).then_inc(S("gn_rs"), 1)
                act.wait_ge(block_used, b_gate + 16)
                for j in range(QT):
                    high(SPLITS["rw", l] + j, j, P3[:, j, :])
                for m in range(KT):
                    weights(b_br + m + 2)
                    act.wait_ge(S(f"gate_in{m % 2}"), 32 * (4 * l + m // 2 + 1))
                    g = P1[:, 2 * (m % 2):2 * (m % 2) + 2, :]
                    A(g, g, ACT.Sigmoid).then_inc(S("gate_sig"), 1)
                    if m < 4:
                        high(SPLITS["merged", l] + m, 4 + m, merged[:, m, :])
                for m in range(4, KT):
                    high(SPLITS["merged", l] + m, m - 4, merged[:, m, :])
                for m in range(KT):
                    weights(b_out + m + 2)
                for m in range(KT):
                    if m < 7:
                        act.wait_ge(S("xc_ready"), 7 * l + m + 1)
                    else:
                        evacuated_job(act, ("ln_mean", l))
                    square(("ln", l), m, xa[:, m, :])
                inverse_root(merged[:, 0, :], ("ln_var", l), 1.0 / D, 1e-5, S("ln_rs"))

            def rms(key, job, tiles, ready):
                for m in range(KT):
                    ready(m)
                    square(key, m, tiles[:, m, :])
                inverse_root(RS, job, 1.0 / D, 1e-6, S("rms_rs"))

            rms("pre0", "rms_pre0", xa, lambda m: act.wait_ge(S("x_done"), KT + m + 1))
            for m in range(KT):
                high(SPLITS["lru_h"] + m, m, ST[m % 2])
            with act.Fori(0, RT // 4) as turn:
                for j in range(4):
                    b = LRU + j
                    weights(b + 2, turn)
                    x = projected(act, b, turn)
                    act.wait_ge(S("conv_done"), j + 1 + 4 * turn)
                    read(A(ST[b % 2], x, ACT.Copy), b)
            act.wait_ge(S("conv_done"), RT + 2)

            def lru_block(j):
                b = LRU + RT + j
                weights(b + 2)
                A(ST[b % 2], projected(act, b), ACT.Sigmoid).then_inc(S("sig_staged"), 1)

            def lru_rates(g):
                if g:
                    act.wait_ge(split_src, SPLITS["lru_y"] + 3 * g)
                else:
                    act.wait_ge(S("x_saved"), 32)
                for o in range(3):
                    x = job_ready(act, ("lru_gate", g, o))
                    job_read(A(LRU_A[:, o, :], x, ACT.Sigmoid, bias=V("b_a", 3 * g + o)), ("lru_gate", g, o))
                for o in range(3):
                    evacuated_job(act, ("lru_gate", g, o))
                    A(LRU_U[:, o, :], LRU_A[:, o, :], ACT.Tanh, scale=DV["cl_t"][:, 3 * g + o:3 * g + o + 1])\
                        .then_inc(S("lru_tanh"), 1)
                for o in range(3):
                    A(LRU_A[:, o, :], LRU_A[:, o, :], ACT.Exp, scale=DV["cl"][:, 3 * g + o:3 * g + o + 1])\
                        .then_inc(S("lru_exp"), 1)

            def lru_inputs(g):
                for o in range(3):
                    x = job_ready(act, ("lru_gate", g, 3 + o))
                    job_read(A(xa[:, o, :], x, ACT.Sigmoid, bias=V("b_x", 3 * g + o)), ("lru_gate", g, 3 + o))

            def lru_roots(g):
                for o in range(3):
                    act.wait_ge(S("lru_u"), 3 * g + o + 1)
                    A(LRU_U[:, o, :], LRU_U[:, o, :], ACT.Ln, scale=2.0 ** 60).then_inc(S("lru_ln"), 1)
                for o in range(3):
                    act.wait_ge(S("lru_ln"), 3 * g + o + 1)
                    A(LRU_U[:, o, :], LRU_U[:, o, :], ACT.Exp, scale=0.5, bias=-30.0 * math.log(2.0))\
                        .then_inc(S("lru_sqrt"), 1)

            for j in range(3):
                lru_block(j)
            for g in range(4):
                lru_rates(g)
                lru_inputs(g)
                lru_block((3, 6, 9, 10)[g])
                lru_roots(g)
                for j in ((4, 5), (7, 8), (), (11,))[g]:
                    lru_block(j)
            act.wait_ge(block_used, LRU + 2 * RT)
            for t in range(RT):
                high(SPLITS["lru_y"] + t, t, G_S[:, t, :])
            for b in range(LRU_OUT, RET):
                weights(b + 2)
            rms("post0", "rms_post0", OUT, lambda m: left(act, LRU_OUT + m))

            rms("pre1", "rms_pre1", xa, lambda m: act.wait_ge(S("x_done"), 2 * KT + m + 1))
            for m in range(KT):
                high(SPLITS["ret_h"] + m, m, ST[m % 2])

            def ret_blocks(h):
                q, k, v, _ = ret_tiles(h)
                if h > 1:
                    act.wait_ge(split_src, SPLITS["ret_y"] + 4 * (h - 1))
                for j in range(12):
                    b = RET + 12 * h + j
                    weights(b + 2)
                    x = projected(act, b)
                    if j < 8:
                        dst = (q, k, v[:, 0:2], v[:, 2:4])[j // 2][:, j % 2, :]
                        read(A(dst, x, ACT.Copy), b)
                    else:
                        A(ST[b % 2], x, ACT.Sigmoid).then_inc(S("sig_staged"), 1)

            act.wait_ge(S("masks_in"), 16)

            def attend(h):
                for k in range(2):
                    x = job_ready(act, ("rk_turn", h, k))
                    job_read(A(r_ktok[:, k], in_chunks(x, P), ACT.Copy, scale=C("kdec", h, 1)), ("rk_turn", h, k))
                for v in range(4):
                    x = job_ready(act, ("rv_turn", h, v))
                    job_read(A(r_vtok[:, :, v * P:(v + 1) * P], in_chunks(x, P), ACT.Copy), ("rv_turn", h, v))
                for v in range(4):
                    x = job_ready(act, ("r_out", h, v))
                    job_read(A(hg[:, 4 * h + v, :], x, ACT.Copy), ("r_out", h, v))
                for v in range(4):
                    if v < 3:
                        act.wait_ge(S("ret_c"), 3 * h + v + 1)
                    else:
                        evacuated_job(act, ("r_mean", h))
                    square(("ret", h), v, hg[:, 4 * h + v, :])
                inverse_root(RS, ("r_var", h), 1.0 / 512, 1e-5, S("rms_rs"))

            ret_blocks(0)
            ret_blocks(1)
            attend(0)
            ret_blocks(2)
            attend(1)
            ret_blocks(3)
            act.wait_ge(block_used, RET + 48)
            for i in range(8):
                high(SPLITS["ret_y"] + i, i, hg[:, i, :])
            attend(2)
            for i in range(4):
                high(SPLITS["ret_y"] + 8 + i, 8 + i, hg[:, 8 + i, :])
            for m in range(KT):
                weights(RET_OUT + m + 2)
            attend(3)
            for i in range(4):
                high(SPLITS["ret_y"] + 12 + i, i, hg[:, 12 + i, :])
            for m in range(KT):
                weights(RET_OUT + KT + m + 2)
            rms("post1", "rms_post1", OUT, lambda m: evacuated(act, RET_OUT + KT + m))

        @block.vector
        def _(dve):
            chain = Chain(dve, S("dve_chain"))
            TS, TT, STT = nc.vector.tensor_scalar, nc.vector.tensor_tensor, nc.vector.scalar_tensor_tensor

            def tt(out_ap, a, b, op):
                return TT(out_ap, a, b, op)

            def stt(out_ap, in0, scalar, in1, op0, op1):
                return STT(out=out_ap, in0=in0, scalar=scalar, in1=in1, op0=op0, op1=op1)

            def low(n, slot, src, turn=0):
                dve.wait_ge(split_hi, n + 1 + turn)
                tt(act_lo[:, slot, :], src, act_hi[:, slot, :].bitcast(F32), ALU.subtract).then_inc(split_lo, 1)

            def spread(ap, n):
                return ap.unsqueeze(1).to_broadcast([P, n, ap.shape[1]])

            for i in range(2):
                dve.sem_inc(proj_read[i], 1)
            dve.sem_inc(S("conv_done"), 2)
            chain.done(nc.vector.memset(stage[:, :, 0:4], 0.0))
            dve.wait_ge(S("vec_in"), 16)
            t = DV["lb_t"]
            chain.done(tt(t[:, 0:4], V("lb0"), V("lb1"), ALU.max))
            chain.done(tt(t[:, 4:8], V("lb0"), t[:, 0:4], ALU.subtract))
            chain.done(tt(t[:, 8:12], V("lb1"), t[:, 0:4], ALU.subtract))
            stt(DV["cl_t"], V("lam"), -1.0, V("lam"), ALU.mult, ALU.max).then_inc(S("setup_dve"), 1)
            for l in range(DEPTH):
                chain.done(TS(DV[f"mu1{l}"], V(f"mu{l}"), -1.0, 1.0, ALU.mult, ALU.add))
                chain.done(TS(DV[f"ka1{l}"], V(f"k_a{l}"), -1.0, 1.0, ALU.mult, ALU.add))
            dve.wait_ge(S("c_sig"), 1)
            chain.done(tt(DV["c"], DV["c"], V("c"), ALU.mult))

            def ada_step(l, k):
                n = 8 * l + k
                dve.wait_ge(S(f"ada_in{k % 2}"), 16 * (n // 2 + 1))
                wait(dve, S("ada_used"), n)
                acc, rows = (ada_acc, ada_in) if l else (ada_acc[:, 0:2 * D], ada_in[:, :, 0:2 * D])
                if k == 0:
                    ins = TS(acc, rows[:, 0], DV["c"][:, 0:1], None, ALU.mult)
                else:
                    ins = stt(acc, rows[:, k % 2], DV["c"][:, k:k + 1], acc, ALU.mult, ALU.add)
                ins.then_inc(S("ada_used"), 1)

            for k in range(KT):
                ada_step(0, k)
            dve.wait_ge(S("setup_act"), 1)
            chain.done(tt(t[:, 0:4], t[:, 4:8], t[:, 8:12], ALU.add))
            chain.done(nc.vector.reciprocal(t[:, 0:4], t[:, 0:4]))
            chain.done(tt(t[:, 4:8], t[:, 4:8], t[:, 0:4], ALU.mult))
            chain.done(tt(t[:, 8:12], t[:, 8:12], t[:, 0:4], ALU.mult))
            chain.done(tt(t[:, 8:12], t[:, 8:12], t[:, 4:8], ALU.add))
            chain.done(tt(t[:, 8:12], t[:, 8:12], t[:, 4:8], ALU.subtract))
            chain.done(tt(t[:, 4:8], t[:, 4:8], t[:, 4:8], ALU.subtract))
            for l in range(DEPTH):
                lb = t[:, 4 + 4 * l:8 + 4 * l]
                chain.done(TS(DV[f"omlb{l}"], lb, -1.0, 1.0, ALU.mult, ALU.add))
                chain.done(TS(DV[f"lbf{l}"], lb, 1e-30, None, ALU.max))
            chain.done(TS(DV["cl"], V("lam"), -1.0, 0.0, ALU.mult, ALU.max))
            chain.done(tt(DV["cl"], DV["cl"], DV["cl_t"], ALU.add))
            chain.done(TS(DV["cl"], DV["cl"], -8.0, None, ALU.mult))
            chain.done(TS(DV["cl_t"], DV["cl"], -1.0, None, ALU.mult))

            for l in range(DEPTH):
                b_rw, b_hg, b_gate = first["rw", l][0], first["hg", l][0], first["gate", l][0]
                b_br, b_out = first["branch", l][0], first["out", l][0]
                n = 24 if l else 16
                x = job_ready(dve, ("ada", l))
                job_read(tt(cond[:, l, 0:n], x[:, 0:n], V(f"b_ada{l}")[:, 0:n], ALU.add), ("ada", l))
                evacuated_job(dve, ("ada", l))
                chain.done(TS(cond[:, l, 8:n], cond[:, l, 8:n], 1.0, None, ALU.add))
                if l == 0:
                    dve.wait_ge(S("x_in"), 16)
                n = SPLITS["h", l]
                for m in range(KT):
                    if m > 1:
                        dve.wait_ge(split_lo, n + m - 1)
                    TS(ST[m % 2], xa[:, m, :], cond[:, l, 8 + m:9 + m], cond[:, l, m:m + 1], ALU.mult, ALU.add)\
                        .then_inc(split_src, 1)
                    if m:
                        low(n + m - 1, m - 1, ST[(m - 1) % 2])
                low(n + 7, 7, ST[1])

                def shifted(b, k, dst, turn=0):
                    dve.wait_ge(S("mu_scaled"), 17 * l + k + 1 + 4 * turn)
                    at = derived_column(f"mu1{l}") + k
                    read(stt(dst, proj[b % 2][:, :], derived[:, bass.ds(at + 4 * turn, 1)],
                             stage[:, b % 2, 3:515], ALU.mult, ALU.add), b)

                shifted(b_rw, 0, wa[:, :])
                b = b_rw + 1 + l
                if l:
                    dve.wait_ge(S("v_out"), 16)
                if l == 0:
                    nc.vector.memset(xa[:, 4:6, :], 0.0).then_inc(S("gate_rows"), 1)
                    dve.wait_ge(S("gate_cols"), 16)
                with dve.Fori(0, 4) as turn:
                    for j in range(4):
                        shifted(b + j, 1 + j, slots[:, turn, j, :], turn)
                        if l == 0 and j % 2:
                            k = 2 * turn + j // 2
                            dve.wait_ge(S("gate_rows"), k + 1)
                            stt(xa[:, 4:6, :], hg[:, bass.ds(2 * k, 2), :], derived[:, bass.ds(derived_column("c") + k, 1)], xa[:, 4:6, :],
                                ALU.mult, ALU.add).then_inc(S("gate_rows"), 1)
                if l == 0:
                    x = job_ready(dve, "ada_gate")
                    job_read(tt(cond[:, 0, 16:24], x[:, 0:8], V("b_ada0")[:, 16:24], ALU.add), "ada_gate")
                    evacuated_job(dve, "ada_gate")
                    chain.done(TS(cond[:, 0, 16:24], cond[:, 0, 16:24], 1.0, None, ALU.add))
                    dve.wait_ge(S("masks_in"), 16)
                for b in (b_hg - 2, b_hg - 1):
                    evacuated(dve, b)
                dve.wait_ge(S("z_sig"), l + 1)
                chain.done(tt(Z_, Z_, P4, ALU.mult))
                if l:
                    dve.wait_ge(S("v_in"), 16)
                    vf = xa[:, 4:8, :]
                    chain.done(tt(vf, vf, V_, ALU.subtract))
                    for j in range(QT):
                        evacuated_job(dve, ("v_up", l, j))
                    chain.done(tt(vf, vf, P3, ALU.mult))
                    chain.done(tt(V_, V_, vf, ALU.add))
                for j in range(QT):
                    TS(P4[:, j, :], K_[:, j, :], V(f"k_k{l}", j), None, ALU.mult).then_inc(S("kk0_ready"), 1)
                for j in range(QT):
                    evacuated_job(dve, ("w_up", l, j))
                    chain.done(nc.vector.tensor_tensor_scan(P3[:, j, :], C("scan64"), P1[:, j, :], 0.0,
                                                            ALU.mult, ALU.add))
                tt(P1, P3, P1, ALU.subtract).then_inc(S("decay_ex"), 1)
                for j in range(QT):
                    evacuated_job(dve, ("a_up", l, j))
                for j in range(QT):
                    chain.done(TS(xa[:, 3, :], P2[:, j, :], V(f"k_a{l}", j), DV[f"ka1{l}"][:, j:j + 1],
                                  ALU.mult, ALU.add))
                    chain.done(tt(K_[:, j, :], K_[:, j, :], xa[:, 3, :], ALU.mult))
                for j in range(QT):
                    stt(xa[:, j, :], R_[:, j, :], V(f"r_k{l}", j), K_[:, j, :], ALU.mult, ALU.mult)\
                        .then_inc(S("rk_ready"), 1)
                for j in range(QT):
                    x = job_ready(dve, ("kk_sum", l, j))
                    job_read(TS(xa[:, 4 + j, :], x, 1e-24, None, ALU.max), ("kk_sum", l, j))
                dve.wait_ge(S("norm_ready"), l + 1)
                chain.done(tt(P4, P4, xa[:, 4:8, :], ALU.mult))
                dve.wait_ge(S("decay_exp"), l + 1)
                chain.done(tt(P1, P1, P4, ALU.mult))
                stt(P4, P4, -1.0, P2, ALU.mult, ALU.mult).then_inc(S("bn_ready"), 1)
                dve.wait_ge(S("bn_ready"), l + 1)
                dve.wait_ge(S("decay_in"), l + 1)
                chain.done(tt(P4, P4, P2, ALU.mult))
                chain.done(tt(K_, K_, P2, ALU.mult))
                for j in range(QT):
                    x = job_ready(dve, ("rk_sum", l, j))
                    job_read(tt(P2[:, j, :], x, V_[:, j, :], ALU.mult), ("rk_sum", l, j))
                dve.wait_ge(S("decay_all"), l + 1)
                chain.done(nc.vector.tensor_copy(chunk_end[:, :, :], P3[:, :, C_RW - 1:T:C_RW]))
                tt(R_, R_, P3, ALU.mult).then_inc(S("dve_prep"), 1)
                for k in range(4):
                    b = b_hg + 12 + k
                    dve.wait_ge(S("sig_staged"), 4 * l + k + 1)
                    read(tt(hg[:, 12 + k, :], proj[b % 2][:, :], ST[b % 2], ALU.mult), b)

                with dve.Fori(0, QT) as turn:
                    chain.enter(turn, HG_CHAIN)
                    head = 4 * l + turn
                    b_row, q_row = hg[:, 4 + turn, :], hg[:, turn, :]
                    one = derived[:, bass.ds(derived_column(f"omlb{l}") + turn, 1)]
                    floor = derived[:, bass.ds(derived_column(f"lbf{l}") + turn, 1)]
                    dve.wait_ge(S("f_sig"), 2 * head + 2)
                    chain.done(TS(decay, decay, one, floor, ALU.mult, ALU.add))
                    TS(b_row, decay, 2.0 ** -50, None, ALU.max).then_inc(S("f_mix"), 1)
                    TS(decay, decay, 2.0 ** 50, 1.0, ALU.mult, ALU.min).then_inc(S("f_mix"), 1)
                    TS(k_hg, k_hg, one, None, ALU.mult).then_inc(S("k_scaled"), 1)
                    dve.wait_ge(S("f_ln"), 2 * head + 2)
                    chain.done(tt(decay, decay, b_row, ALU.add))
                    nc.vector.tensor_tensor_scan(b_row, C("scan128"), decay, 0.0, ALU.mult, ALU.add)\
                        .then_inc(S("b_ready"), 1)
                    dve.wait_ge(S("b_ready"), head + 1)
                    dve.wait_ge(S("k_scaled"), head + 1)

                    def diff(n):
                        if n > 3:
                            job_ready(dve, ("level", l, n - 3), turn)
                        m = 1 << (n - 1)
                        rows = b_row.rearrange("p (b t) -> p b t", t=2 * m)
                        mid = rows[:, :, m - 1:m].to_broadcast([P, T // (2 * m), 2 * m])
                        tt(ring[(n - 1) % 3].rearrange("p (b t) -> p b t", t=2 * m), rows, mid, ALU.subtract)\
                            .then_inc(S("diff_ready"), 1)

                    def fill(n):
                        m = 1 << (n - 1)
                        dve.wait_ge(S("level_exp"), 14 * head + 2 * n)
                        lo, hi = halves(ring[(n - 1) % 3], m)
                        tt(lo, lo, halves(k_hg, m)[0], ALU.mult).then_inc(S("qk_ready"), 1)
                        tt(hi, hi, halves(q_row, m)[1], ALU.mult).then_inc(S("qk_ready"), 1)

                    def pick(n):
                        if n == 0:
                            x = job_ready(dve, ("level", l, 0), turn)
                            job_read(tt(in_chunks(scores, P), in_chunks(x, P), spread(C("hgmask", 0, P), 4),
                                        ALU.mult), ("level", l, 0))
                            return
                        bank, use = jobs(("level", l, n), turn)
                        before, use_before = jobs(("level", l, n - 1), turn)
                        full, read_before = dve.snap(use + 1), dve.snap(use_before + 1)
                        landed(dve)
                        dve.wait_ge(aux_full[bank], full)
                        dve.wait_ge(aux_read[before], read_before)
                        dve.sem_inc(S("level_landed"), 1)
                        mask = spread(C("hgmask", P * n, P), 4).bitcast(I32)
                        job_read(nc.vector.copy_predicated(in_chunks(scores, P), mask,
                                                           in_chunks(aux[bank][:, :], P)), ("level", l, n))

                    diff(1), diff(2), fill(1), diff(3), fill(2), pick(0)
                    diff(4), pick(1), fill(3)
                    diff(5), pick(2), fill(4)
                    diff(6), pick(3), fill(5)
                    diff(7), pick(4), fill(6), fill(7)
                    pick(5)
                    b_chunks = in_chunks(b_row, P)
                    tt(in_chunks(ring[1], P), b_chunks, b_chunks[:, :, P - 1:P].to_broadcast([P, 4, P]),
                       ALU.subtract).then_inc(S("tail_diff"), 1)
                    pick(6)
                    dve.wait_ge(S("tail_exp"), head + 1)
                    tt(ring[1], ring[1], k_hg, ALU.mult).then_inc(S("k_decayed"), 1)
                    pick(7)
                    dve.wait_ge(S("exp_ready"), head + 1)
                    tt(ring[0], q_row, decay, ALU.mult).then_inc(S("q_decayed"), 1)
                    x = job_ready(dve, ("hg_state", l), turn)
                    chain.done(nc.vector.tensor_copy(k_hg[:, 0:P], x[:, 0:P]))
                    chain.done(stt(k_hg[:, P:2 * P], k_hg[:, 0:P], decay[:, 255:256], x[:, P:2 * P],
                                   ALU.mult, ALU.add))
                    job_read(stt(k_hg[:, 2 * P:3 * P], k_hg[:, P:2 * P], decay[:, 383:384], x[:, 2 * P:3 * P],
                                 ALU.mult, ALU.add), ("hg_state", l))
                    x = job_ready(dve, ("hg_out", l), turn)
                    dve.wait_ge(S("hg_rms"), head + 1)
                    gain = vec[:, bass.ds(vec_at[f"hg_g{l}"][0] + turn, 1)]
                    job_read(stt(ring[1], x, gain, scores, ALU.mult, ALU.mult), ("hg_out", l))
                    evacuated_job(dve, ("hg_out", l), turn)
                    tt(hg[:, 12 + turn, :], hg[:, 12 + turn, :], ring[1], ALU.mult).then_inc(split_src, 1)
                    low(SPLITS["hg", l], 8 + turn, hg[:, 12 + turn, :], turn)
                    chain.leave(QT)

                def operands(c, odd):
                    for src, dst in ((P1, ar[odd]), (P4, b_bd)):
                        for q in (slice(0, 64), slice(64, 128)):
                            nc.vector.tensor_copy(dst[q, :, q], src[q, :, chunk_at(c)]).then_inc(S("chunk_dve"), 1)

                def mask_scores(odd, s, turn, k):
                    x = job_ready(dve, ("sc", l, s, k), turn)
                    job_read(tt((m1, m2)[k // 2][odd][:, 2 * (k % 2):2 * (k % 2) + 2, :],
                                x[:, 0:384].rearrange("p (j n) -> p j n", n=192), spread(C("mask192"), 2),
                                ALU.mult), ("sc", l, s, k))

                def begin_inverse(odd, s, turn):
                    evacuated_job(dve, ("sc", l, s, 0), turn)
                    evacuated_job(dve, ("sc", l, s, 1), turn)
                    xt = xt_inv[odd]
                    tt(xt, m1[odd][:, :, 0:P], spread(C("level", 0, P), QT), ALU.mult).then_inc(S("pairs_picked"), 1)

                def end_begin(c, odd):
                    dve.wait_ge(S("pairs_picked"), RW_CHUNKS * l + c + 1)
                    tt(xt_inv[odd], xt_inv[odd], spread(C("ident"), QT), ALU.add).then_inc(S("x0_ready"), 1)

                def chunk(c, odd, s, turn):
                    xt = xt_inv[odd]
                    dve.wait_ge(S("x0_ready"), RW_CHUNKS * l + c + 1)
                    for n in range(5):
                        for half, js in enumerate(HALF_PAIRS):
                            x = job_ready(dve, ("z", l, s, n, half), turn)
                            job_read(tt(z_sb[:, js], in_chunks(x[:, 0:2 * P], P),
                                        spread(C("level", P * (n + 1), P), 2), ALU.mult), ("z", l, s, n, half))
                        if n == 4 and s != "D":
                            mask_scores(1 - odd, s, turn, 1)
                        for half, js in enumerate(HALF_PAIRS):
                            if n:
                                evacuated_job(dve, ("x", l, s, n - 1, half), turn)
                            x = job_ready(dve, ("x", l, s, n, half), turn)
                            if n < 4:
                                tt(x_inv[:, js], x_inv[:, js], in_chunks(x[:, 2 * P:4 * P], P), ALU.add)
                            job_read(tt(xt[:, js], xt[:, js], in_chunks(x[:, 0:2 * P], P), ALU.add),
                                     ("x", l, s, n, half))
                            if (n, half) == (4, 0) and s != "D":
                                begin_inverse(1 - odd, s, turn)
                        if n == 1 and s != "D":
                            job_ready(dve, ("b_turn", l, s), turn)
                            operands(c + 1, 1 - odd)
                        if n == 3 and s != "D":
                            mask_scores(1 - odd, s, turn, 0)
                    if s != "D":
                        end_begin(c + 1, 1 - odd)
                        mask_scores(1 - odd, s, turn, 2)
                        mask_scores(1 - odd, s, turn, 3)
                    at = (RW_CHUNKS + 1) * l + c + 1
                    x = job_ready(dve, ("rw_state", l, s), turn)
                    dve.wait_ge(S("state_ready"), at)
                    job_read(tt(state, state, in_chunks(x, P), ALU.add), ("rw_state", l, s))
                    evacuated_job(dve, ("rw_state", l, s), turn)
                    end = chunk_end[:, :, bass.ds(c, 1)].to_broadcast([P, QT, P])
                    tt(state, state, end, ALU.mult).then_inc(S("state_ready"), 1)

                dve.wait_ge(split_lo, SPLITS["hg", l] + 4)
                dve.wait_ge(S("zeroed"), l + 1)
                operands(0, 0)
                nc.vector.memset(state, 0.0).then_inc(S("state_ready"), 1)
                for k in range(4):
                    mask_scores(0, "P", 0, k)
                begin_inverse(0, "P", 0)
                end_begin(0, 0)
                rw_chunks(dve, chunk)

                for j in range(QT):
                    x = job_ready(dve, ("gn_mean", l, j))
                    job_read(stt(P3[:, j, :], x, -1.0 / 64, P3[:, j, :], ALU.mult, ALU.add), ("gn_mean", l, j))
                n = SPLITS["rw", l]
                for j in range(QT):
                    dve.wait_ge(S("gn_rs"), 4 * l + j + 1)
                    y = P3[:, j, :]
                    chain.done(tt(y, y, K_[:, j, :], ALU.mult))
                    chain.done(TS(y, y, V(f"gn_g{l}", j), V(f"gn_b{l}", j), ALU.mult, ALU.add))
                    chain.done(tt(y, y, P2[:, j, :], ALU.add))
                    tt(y, y, Z_[:, j, :], ALU.mult).then_inc(split_src, 1)
                    if j:
                        low(n + j - 1, j - 1, P3[:, j - 1, :])
                low(n + 3, 3, P3[:, 3, :])

                n = SPLITS["merged", l]
                for m in range(KT):
                    b = b_br + m
                    dve.wait_ge(S("gate_sig"), 8 * l + m + 1)
                    g = [P1[:, 2 * (m % 2) + k, :] for k in range(2)]
                    read(tt(g[0], g[0], projected(dve, b), ALU.mult), b)
                    x = job_ready(dve, ("branch_rw", l, m))
                    job_read(tt(g[1], g[1], x, ALU.mult), ("branch_rw", l, m))
                    evacuated(dve, b)
                    evacuated_job(dve, ("branch_rw", l, m))
                    tt(merged[:, m, :], g[0], g[1], ALU.add).then_inc(split_src, 1)
                    if 1 <= m <= 4:
                        low(n + m - 1, 4 + m - 1, merged[:, m - 1, :])
                for m in range(4, KT):
                    low(n + m, m - 4, merged[:, m, :])

                dve.wait_ge(S("x_in"), 32 + 16 * l)
                chain.done(TS(xa[:, :, :], xa[:, :, :], DN_ALPHA, None, ALU.mult))
                for m in range(KT):
                    b = b_out + m
                    read(stt(xa[:, m, :], projected(dve, b), cond[:, l, 16 + m:17 + m], xa[:, m, :],
                             ALU.mult, ALU.add), b)
                    if l == 0:
                        ada_step(1, m)
                x = job_ready(dve, ("ln_mean", l))
                for m in range(KT):
                    evacuated(dve, b_out + m)
                    ins = stt(xa[:, m, :], x, -1.0 / D, xa[:, m, :], ALU.mult, ALU.add)
                    job_read(ins, ("ln_mean", l)) if m == 7 else ins.then_inc(S("xc_ready"), 1)
                dve.wait_ge(S("ln_rs"), l + 1)
                for m in range(KT + 1):
                    if m < KT:
                        tt(xa[:, m, :], xa[:, m, :], merged[:, 0, :], ALU.mult).then_inc(S("ln_scaled"), 1)
                    if m:
                        dve.wait_ge(S("ln_scaled"), KT * l + m)
                        TS(xa[:, m - 1, :], xa[:, m - 1, :], V(f"ln_g{l}", m - 1), V(f"ln_b{l}", m - 1),
                           ALU.mult, ALU.add).then_inc(S("x_done"), 1)
                dve.wait_ge(S("x_done"), KT * (l + 1))

            def normed(n, pre, count):
                dve.wait_ge(S("rms_rs"), count)
                for m in range(KT):
                    if m > 1:
                        dve.wait_ge(split_lo, n + m - 1)
                    stt(ST[m % 2], xa[:, m, :], V(pre, m), RS, ALU.mult, ALU.mult).then_inc(split_src, 1)
                    if m:
                        low(n + m - 1, m - 1, ST[(m - 1) % 2])
                low(n + 7, 7, ST[1])

            def onto_x(n, post, count, x_in, done):
                dve.wait_ge(S("rms_rs"), count)
                dve.wait_ge(S("x_in"), x_in)
                for m in range(KT + 1):
                    if m < KT:
                        stt(OUT[:, m, :], OUT[:, m, :], V(post, m), RS, ALU.mult, ALU.mult).then_inc(S("out_scaled"), 1)
                    if m:
                        dve.wait_ge(S("out_scaled"), KT * n + m)
                        tt(xa[:, m - 1, :], xa[:, m - 1, :], OUT[:, m - 1, :], ALU.add).then_inc(done, 1)

            normed(SPLITS["lru_h"], "pre0", 1)
            with dve.Fori(0, RT // 4) as turn:
                chain.enter(turn, 12)
                for j in range(4):
                    b = LRU + j
                    dve.wait_ge(proj_read[b % 2], b // 2 + 2 + 2 * turn)
                    dst = X_C[:, 4 * turn + j, :]
                    w = [vec[:, bass.ds(vec_at["conv_w"][0] + RT * k + j + 4 * turn, 1)] for k in range(4)]
                    bias = vec[:, bass.ds(vec_at["conv_b"][0] + j + 4 * turn, 1)]
                    chain.done(TS(dst, stage[:, b % 2, 4:516], w[3], bias, ALU.mult, ALU.add))
                    for k in (2, 1):
                        chain.done(stt(dst, stage[:, b % 2, 1 + k:513 + k], w[k], dst, ALU.mult, ALU.add))
                    stt(dst, stage[:, b % 2, 1:513], w[0], dst, ALU.mult, ALU.add).then_inc(S("conv_done"), 1)
                chain.leave(RT // 4)

            def lru_block(j):
                b = LRU + RT + j
                dve.wait_ge(S("sig_staged"), 8 + j + 1)
                read(tt(G_S[:, j, :], proj[b % 2][:, :], ST[b % 2], ALU.mult), b)

            def lru_squares(g):
                for o in range(3):
                    dve.wait_ge(S("lru_exp"), 3 * g + o + 1)
                    a, u, a2 = LRU_A[:, o, :], LRU_U[:, o, :], xa[:, 4 + o, :]
                    chain.done(tt(a2, a, a, ALU.mult))
                    chain.done(stt(u, a2, 1.0, u, ALU.add, ALU.mult))
                    TS(u, u, 1e-37, None, ALU.max).then_inc(S("lru_u"), 1)

            def lru_scan(g, o):
                t = 3 * g + o
                a, u, i = LRU_A[:, o, :], LRU_U[:, o, :], xa[:, o, :]
                evacuated_job(dve, ("lru_gate", g, 3 + o))
                chain.done(tt(i, i, X_C[:, t, :], ALU.mult))
                dve.wait_ge(S("lru_sqrt"), t + 1)
                chain.done(tt(i, i, u, ALU.mult))
                chain.done(nc.vector.tensor_tensor_scan(u, a, i, 0.0, ALU.mult, ALU.add))
                evacuated(dve, LRU + RT + t)
                tt(G_S[:, t, :], u, G_S[:, t, :], ALU.mult).then_inc(split_src, 1)

            for j in range(3):
                lru_block(j)
            for g in range(4):
                lru_squares(g)
                lru_block((3, 6, 9, 10)[g])
                lru_scan(g, 0)
                if g < 2:
                    lru_block(3 * g + 4)
                if g == 3:
                    lru_block(11)
                    for t in range(0, 3):
                        low(SPLITS["lru_y"] + t, t, G_S[:, t, :])
                lru_scan(g, 1)
                if g < 2:
                    lru_block(3 * g + 5)
                elif g == 3:
                    for t in range(3, 6):
                        low(SPLITS["lru_y"] + t, t, G_S[:, t, :])
                lru_scan(g, 2)
            for t in range(6, RT):
                low(SPLITS["lru_y"] + t, t, G_S[:, t, :])
            for m in range(KT):
                u = LRU_OUT + m
                lru_out_ready(dve, m)
                nc.vector.tensor_copy(OUT[:, m, :], proj[u % 2][:, :]).then_inc(proj_read[u % 2], 1)
            for m in (6, 7):
                left(dve, LRU_OUT + m)
            onto_x(0, "post0", 2, 64, S("x_done"))
            dve.wait_ge(S("x_done"), 3 * KT)

            normed(SPLITS["ret_h"], "pre1", 3)

            def ret_blocks(h):
                q, k, _, gate = ret_tiles(h)
                b0 = RET + 12 * h
                if h == 0:
                    dve.wait_ge(S("tables_in"), 16)
                for n, x in enumerate((q, k)):
                    evacuated(dve, b0 + 2 * n)
                    evacuated(dve, b0 + 2 * n + 1)
                    chain.done(tt(r_qd, x, spread(tables["sin"], 2), ALU.mult))
                    chain.done(tt(x, x, spread(tables["cos"], 2), ALU.mult))
                    tt(x[:, 0, :], x[:, 0, :], r_qd[:, 1, :], ALU.subtract).then_inc(S("rotated"), 1)
                    tt(x[:, 1, :], x[:, 1, :], r_qd[:, 0, :], ALU.add).then_inc(S("rotated"), 1)
                    dve.wait_ge(S("rotated"), 4 * h + 2 * n + 2)
                for v in range(4):
                    b = b0 + 8 + v
                    dve.wait_ge(S("sig_staged"), 20 + 4 * h + v + 1)
                    read(tt(gate[:, v, :], proj[use_of(b) % 2][:, :], ST[b % 2], ALU.mult), b)

            def attend(h):
                q, _, _, gate = ret_tiles(h)
                dve.wait_ge(S("rotated"), 4 * (h + 1))
                for k in range(2):
                    tt(in_chunks(r_qd[:, k, :], P), in_chunks(q[:, k, :], P),
                       spread(tables["qdec"][:, P * h:P * h + P], 4), ALU.mult).then_inc(S("rq_ready"), 1)
                x = job_ready(dve, ("r_score", h))
                job_read(tt(in_chunks(r_scores, P), in_chunks(x, P), spread(tables["dmask"][:, P * h:P * h + P], 4),
                            ALU.mult), ("r_score", h))
                for c in range(3):
                    for k in range(2):
                        x = job_ready(dve, ("r_state", h, c, k))
                        if c == 0:
                            ins = nc.vector.tensor_copy(r_state[:, k, :], x)
                        else:
                            evacuated_job(dve, ("r_state", h, c - 1, k))
                            ins = stt(r_state[:, k, :], r_state[:, k, :], math.exp(P * RET_LOG[h]), x,
                                      ALU.mult, ALU.add)
                        job_read(ins, ("r_state", h, c, k))
                x = job_ready(dve, ("r_mean", h))
                for v in range(4):
                    y = hg[:, 4 * h + v, :]
                    ins = stt(y, x, -1.0 / 512, y, ALU.mult, ALU.add)
                    job_read(ins, ("r_mean", h)) if v == 3 else ins.then_inc(S("ret_c"), 1)
                dve.wait_ge(S("rms_rs"), 4 + h)
                for v in range(4):
                    y = hg[:, 4 * h + v, :]
                    chain.done(tt(y, y, RS, ALU.mult))
                    tt(y, y, gate[:, v, :], ALU.mult).then_inc(split_src, 1)

            ret_blocks(0)
            ret_blocks(1)
            attend(0)
            ret_blocks(2)
            attend(1)
            ret_blocks(3)
            for i in range(8):
                low(SPLITS["ret_y"] + i, i, hg[:, i, :])
            attend(2)
            for i in range(4):
                low(SPLITS["ret_y"] + 8 + i, 8 + i, hg[:, 8 + i, :])
            for m in range(KT):
                b = RET_OUT + m
                read(nc.vector.tensor_copy(OUT[:, m, :], projected(dve, b)), b)
            attend(3)
            for i in range(4):
                low(SPLITS["ret_y"] + 12 + i, i, hg[:, 12 + i, :])
            for m in range(KT):
                b = RET_OUT + KT + m
                evacuated(dve, RET_OUT + m)
                read(tt(OUT[:, m, :], OUT[:, m, :], projected(dve, b), ALU.add), b)
            for m in (6, 7):
                evacuated(dve, RET_OUT + KT + m)
            onto_x(1, "post1", 8, 80, S("x_final"))

        @block.tensor
        def _(pe):
            MM = nc.tensor.matmul

            def project(b, tiles=tuple(range(KT)), turn=0, bank=None, start=True, stop=True, open_bank=True,
                        rows=tuple(range(KT)), fresh=None):
                s = b % 2
                pe.wait_ge(lo_ready, b + 1 + 4 * turn)
                if bank is None:
                    u = use_of(b)
                    bank = proj[u % 2][:, :]
                    if open_bank:
                        pe.wait_ge(proj_read[u % 2], u // 2 + 1 + 2 * turn)
                terms = [(w, a, k, t) for k, t in zip(rows, tiles)
                         for w, a in ((w_hi, act_hi), (w_hi, act_lo), (w_lo, act_hi))]
                for i, (w, a, k, t) in enumerate(terms):
                    if fresh is not None and i % 3 == 0:
                        pe.wait_ge(split_lo, fresh + i // 3 + 1)
                    ins = MM(bank, w[:, s, k, :], a[:, t, :], start=(start and i == 0),
                             stop=(stop and i == len(terms) - 1))
                return ins

            def used(ins):
                ins.then_inc(block_used, 1)

            def turn_over(dst, src):
                return nc.tensor.transpose(dst, src, C("ident"))

            def sum_squares(key, job, tiles=KT):
                x = job_open(pe, job)
                for m in range(tiles):
                    pe.wait_ge(sq_ready, SQUARES[key] + m + 1)
                    ins = MM(x, C("ones"), ST[m % 2], start=(m == 0), stop=(m == tiles - 1))
                    job_full(ins, job) if m == tiles - 1 else ins.then_inc(sq_used, 1)

            pe.wait_ge(S("const_in"), 16)
            for l in range(DEPTH):
                b_rw, b_hg, b_gate = first["rw", l][0], first["hg", l][0], first["gate", l][0]
                b_br, b_out = first["branch", l][0], first["out", l][0]
                pe.wait_ge(S("ada_used"), 8 * (l + 1))
                x = job_open(pe, ("ada", l))
                for j in range(24 if l else 16):
                    ins = MM(x[:, j:j + 1], ada_acc[:, P * j:P * j + P], C("ones", 0, 1), start=True, stop=True)
                job_full(ins, ("ada", l))
                used(project(b_rw, fresh=SPLITS["h", l]))
                b = b_rw + 1
                if l:
                    used(project(b))
                    b += 1
                with pe.Fori(0, 4) as turn:
                    for j in range(4):
                        used(project(b + j, turn=turn))
                if l == 0:
                    pe.wait_ge(S("gate_rows"), KT + 1)
                    x = job_open(pe, "ada_gate")
                    for j in range(8):
                        ins = MM(x[:, j:j + 1], xa[:, 4 + j // 4, P * (j % 4):P * (j % 4) + P], C("ones", 0, 1),
                                 start=True, stop=True)
                    job_full(ins, "ada_gate")
                pe.wait_ge(S("tanh_done"), l + 1)
                pe.wait_ge(S("up_in"), 16 + 32 * l)
                for j in range(QT):
                    cols = slice(P * j, P * j + P)
                    for name, q in (("w_up", slice(0, 64)), ("a_up", slice(64, 128))):
                        x = job_open(pe, (name, l, j))
                        job_full(MM(x, xa[q, 0, cols], wa[q, :], start=True, stop=True), (name, l, j))
                if l:
                    evacuated(pe, b_rw + 1)
                    for j in range(QT):
                        x = job_open(pe, ("v_up", l, j))
                        job_full(MM(x, xa[0:32, 2, P * j:P * j + P], xa[0:32, 1, :], start=True, stop=True),
                                 ("v_up", l, j))
                for m in range(4):
                    used(project(b_hg + m))
                for j in range(QT):
                    x = job_open(pe, ("kk_sum", l, j))
                    pe.wait_ge(S("kk_squares"), 4 * l + j + 1)
                    job_full(MM(x, C("bdones"), xa[:, 4 + j, :], start=True, stop=True), ("kk_sum", l, j))
                for j in range(QT):
                    x = job_open(pe, ("rk_sum", l, j))
                    pe.wait_ge(S("rk_ready"), 4 * l + j + 1)
                    job_full(MM(x, C("bdones"), xa[:, j, :], start=True, stop=True), ("rk_sum", l, j))
                with pe.Fori(0, 3) as turn:
                    for j in range(4):
                        used(project(b_hg + 4 + j, turn=turn))

                with pe.Fori(0, QT) as turn:
                    head = 4 * l + turn

                    def level(n):
                        x = job_open(pe, ("level", l, n), turn)
                        if n == 0:
                            pe.wait_ge(S("k_scaled"), head + 1)
                        else:
                            pe.wait_ge(S("qk_ready"), 14 * head + 2 * n)
                        for c in range(4):
                            cols = slice(P * c, P * c + P)
                            if n == 0:
                                rhs = hg[:, turn, cols]
                                ins = MM(x[:, cols], k_hg[:, cols], rhs, start=True, stop=True)
                            else:
                                r = ring[(n - 1) % 3][:, cols]
                                ins = MM(x[:, cols], r, r, start=True, stop=True)
                        job_full(ins, ("level", l, n))

                    def gate(g, start, end):
                        tiles = tuple(range(start, end))
                        ins = project(b_gate + g, tiles=tiles, rows=tiles, turn=turn, start=(start == 0),
                                      stop=(end == KT), open_bank=(start == 0))
                        if end == KT:
                            used(ins)

                    gate(0, 0, 8)
                    x = job_open(pe, ("v_turn", l), turn)
                    pe.wait_ge(S("i_copied"), head + 1)
                    for c in range(4):
                        cols = slice(P * c, P * c + P)
                        ins = turn_over(x[:, cols], ring[3][:, cols])
                    job_full(ins, ("v_turn", l))
                    gate(1, 0, 8)
                    level(0)
                    gate(2, 0, 4)
                    level(1)
                    gate(2, 4, 6)
                    level(2)
                    gate(2, 6, 8)
                    level(3)
                    gate(3, 0, 2)
                    level(4)
                    level(5)
                    gate(3, 2, 4)
                    level(6)
                    level(7)
                    gate(3, 4, 6)
                    x = job_open(pe, ("k_turn", l), turn)
                    pe.wait_ge(S("k_decayed"), head + 1)
                    for c in range(3):
                        cols = slice(P * c, P * c + P)
                        turn_over(x[:, cols], ring[1][:, cols])
                    job_full(turn_over(x[:, 3 * P:], ring[1][:, 3 * P:]), ("k_turn", l))
                    gate(3, 6, 8)
                    x = job_open(pe, ("hg_state", l), turn)
                    evacuated_job(pe, ("k_turn", l), turn)
                    evacuated_job(pe, ("v_turn", l), turn)
                    for c in range(3):
                        cols = slice(P * c, P * c + P)
                        ins = MM(x[:, cols], ring[2][:, cols], v_tok[:, cols], start=True, stop=True)
                    job_full(ins, ("hg_state", l))
                    x = job_open(pe, ("hg_out", l), turn)
                    evacuated_job(pe, ("level", l, 7), turn)
                    for c in range(4):
                        cols = slice(P * c, P * c + P)
                        ins = MM(x[:, cols], v_tok[:, cols], scores[:, cols], start=True, stop=(c == 0))
                        if c == 1:
                            evacuated_job(pe, ("hg_state", l), turn)
                            pe.wait_ge(S("q_decayed"), head + 1)
                        if c:
                            ins = MM(x[:, cols], k_hg[:, P * (c - 1):P * c], ring[0][:, cols], start=False, stop=True)
                    job_full(ins, ("hg_out", l))
                    x = job_open(pe, ("hg_square", l), turn)
                    pe.wait_ge(S("hg_sq"), head + 1)
                    job_full(MM(x, C("ones"), ring[3], start=True, stop=True), ("hg_square", l))

                def score(c, odd, s, turn, k):
                    if k == 0:
                        pe.wait_ge(S("chunk_dve"), 4 * (RW_CHUNKS * l + c + 1))
                        pe.wait_ge(S("chunk_act"), 5 * (RW_CHUNKS * l + c + 1))
                    x = job_open(pe, ("sc", l, s, k), turn)
                    keys = (b_bd, k_bd)[k // 2]
                    for i in range(2):
                        j = 2 * (k % 2) + i
                        ins = MM(x[:, 192 * i:192 * i + 192], keys[:, j, :], ar[odd][:, j, :], start=True, stop=True)
                    job_full(ins, ("sc", l, s, k))

                def turn_pairs(name, src, turn):
                    x = job_open(pe, name, turn)
                    for j in range(QT):
                        ins = turn_over(x[:, P * j:P * j + P], src[:, j, :])
                    job_full(ins, name)

                def turn_inverse(c, odd, s, turn):
                    pe.wait_ge(S("x0_ready"), RW_CHUNKS * l + c + 1)
                    turn_pairs(("x_turn", l, s), xt_inv[odd], turn)

                def chunk(c, odd, s, turn):
                    def evac(name, *which):
                        evacuated_job(pe, (name, l, s, *which), turn)

                    def pairs(name, *products, width=P, heads=range(QT)):
                        x = job_open(pe, name, turn)
                        for j in heads:
                            for i, (a, b) in enumerate(products):
                                ins = MM(x[:, width * j:width * j + width], a[:, j, :], b[:, j, :], start=(i == 0),
                                         stop=(i == len(products) - 1))
                        if heads[-1] == QT - 1:
                            job_full(ins, name)

                    rhs = ("rhs", l, s), (ar[odd][:, :, 0:P], state), (m2[odd][:, :, 0:P], v_tok_rw)
                    xt = xt_inv[odd]

                    def z_half(n, half):
                        if n:
                            evac("x", n - 1, half)
                        x = job_open(pe, ("z", l, s, n, half), turn)
                        for i, j in enumerate(PAIRS[half]):
                            ins = MM(x[:, P * i:P * i + P], m1[odd][:, j, 0:P], x_inv[:, j, :], start=True, stop=True)
                        job_full(ins, ("z", l, s, n, half))

                    def x_half(n, half):
                        evac("z", n, half)
                        x = job_open(pe, ("x", l, s, n, half), turn)
                        for i, j in enumerate(PAIRS[half]):
                            ins = MM(x[:, P * i:P * i + P], z_sb[:, j, :], xt[:, j, :], start=True, stop=True)
                        if n < 4:
                            for i, j in enumerate(PAIRS[half]):
                                ins = MM(x[:, 2 * P + P * i:3 * P + P * i], xt[:, j, :], z_sb[:, j, :], start=True,
                                         stop=True)
                        job_full(ins, ("x", l, s, n, half))

                    if s == "A":
                        evacuated_job(pe, ("x_turn", l, "P"))
                        evacuated_job(pe, ("sc", l, "P", 3))
                    for n in range(5):
                        z_half(n, 0)
                        if n == 0:
                            turn_pairs(("b_turn", l, s), b_bd, turn)
                        elif n == 1:
                            turn_pairs(("v_turn_rw", l, s), v_bd, turn)
                        elif n == 2:
                            pe.wait_ge(S("state_ready"), (RW_CHUNKS + 1) * l + c + 1)
                            evac("v_turn_rw")
                            pairs(*rhs, heads=(0, 1))
                        elif s != "D":
                            score(c + 1, 1 - odd, s, turn, 0 if n == 3 else 2)
                        z_half(n, 1)
                        x_half(n, 0)
                        if n == 0:
                            turn_pairs(("k_turn_rw", l, s), k_bd, turn)
                        elif n == 2:
                            pairs(*rhs, heads=(2, 3))
                        elif n > 2 and s != "D":
                            score(c + 1, 1 - odd, s, turn, 1 if n == 3 else 3)
                        x_half(n, 1)
                    evac("rhs")
                    for half in range(2):
                        evac("x", 4, half)
                        pairs(("u", l, s), (xt, rhs_sb), heads=PAIRS[half])
                    evac("u")
                    pairs(("y", l, s), (state, ar[odd][:, :, P:192]), (u_sb, m1[odd][:, :, P:192]),
                          (v_tok_rw, m2[odd][:, :, P:192]), width=C_RW)
                    if s != "D":
                        turn_inverse(c + 1, 1 - odd, s, turn)
                    evac("b_turn")
                    evac("k_turn_rw")
                    pairs(("rw_state", l, s), (b_tok, u_sb), (k_tok, v_tok_rw))
                    if s != "D":
                        evac("x_turn")

                pe.wait_ge(S("zeroed"), l + 1)
                for k in range(4):
                    score(0, 0, "P", 0, k)
                turn_inverse(0, 0, "P", 0)
                rw_chunks(pe, chunk)

                evacuated_job(pe, ("y", l, "D"))
                for j in range(QT):
                    x = job_open(pe, ("gn_mean", l, j))
                    job_full(MM(x, C("bdones"), P3[:, j, :], start=True, stop=True), ("gn_mean", l, j))
                for j in range(QT):
                    x = job_open(pe, ("gn_var", l, j))
                    pe.wait_ge(S("gn_sq"), 4 * l + j + 1)
                    job_full(MM(x, C("bdones"), R_[:, j, :], start=True, stop=True), ("gn_var", l, j))
                pe.wait_ge(split_lo, SPLITS["hg", l] + 4)
                for m in range(2):
                    project(b_br + m, tiles=(8, 9, 10), rows=(0, 1, 2), stop=False)
                for m in range(KT):
                    x = job_open(pe, ("branch_rw", l, m))
                    job_full(project(b_br + m, tiles=(0, 1, 2, 3), rows=(4, 5, 6, 7), bank=x,
                                     fresh=None if m else SPLITS["rw", l]), ("branch_rw", l, m))
                    if m < 2:
                        used(project(b_br + m, tiles=(11,), rows=(3,), start=False, open_bank=False))
                    else:
                        used(project(b_br + m, tiles=(8, 9, 10, 11), rows=(0, 1, 2, 3)))
                x = job_open(pe, ("ln_mean", l))

                def add_up(m):
                    evacuated(pe, b_out + m)
                    return MM(x, C("ones"), xa[:, m, :], start=(m == 0), stop=(m == 7))

                for m in range(KT):
                    b = b_out + m
                    if m == 0:
                        ins = project(b, tiles=(4, 5, 6, 7, 0, 1, 2, 3), fresh=SPLITS["merged", l])
                    else:
                        ins = project(b, tiles=(4, 5, 6, 7, 0, 1, 2, 3))
                    used(ins)
                    if m:
                        add_up(m - 1)
                job_full(add_up(7), ("ln_mean", l))
                sum_squares(("ln", l), ("ln_var", l))

            sum_squares("pre0", "rms_pre0")
            for j in range(4):
                used(project(LRU + j, fresh=None if j else SPLITS["lru_h"]))
            with pe.Fori(0, RT // 4 - 1) as turn:
                for j in range(4, 8):
                    used(project(LRU + j, turn=turn))
            pe.wait_ge(S("lru_w"), 16)
            gates = flat[:, 8 * T:8 * T + 4 * 14 * P].rearrange("p (g w n k) -> p g w n k", g=4, w=2, n=7)
            pe.wait_ge(S("conv_done"), RT + 2)

            def lru_group(g):
                for w in range(2):
                    for o in range(3):
                        name = ("lru_gate", g, 3 * w + o)
                        x = job_open(pe, name)
                        terms = [(n, i) for n, (to, i) in enumerate(BAND) if to == o]
                        for n, i in terms:
                            ins = MM(x, gates[:, g, w, n, :], X_C[:, 3 * g + i, :], start=(n == terms[0][0]),
                                     stop=(n == terms[-1][0]))
                        job_full(ins, name)

            for j in range(3):
                used(project(LRU + RT + j))
            for g in range(4):
                lru_group(g)
                for j in ((3, 4, 5), (6, 7, 8), (9,), (10, 11))[g]:
                    used(project(LRU + RT + j))
            for m in range(KT):
                u = LRU_OUT + m
                parts = {0: [(0, range(0, 8), range(0, 8)), (1, range(0, 4), range(8, 12))],
                         1: [(1, range(4, 8), range(0, 4)), (2, range(0, 8), range(4, 12))]}[m % 2]
                pe.wait_ge(proj_read[u % 2], u // 2 + 1)
                for i, (b, rows, tiles) in enumerate(parts):
                    ins = project(LRU_OUT + 3 * (m // 2) + b, tiles=tuple(tiles), rows=tuple(rows),
                                  bank=proj[u % 2][:, :], start=(i == 0), stop=(i == 1),
                                  fresh=None if m else SPLITS["lru_y"] + (0, 8)[i])
                    if (m % 2, i) == (0, 1):
                        ins.then_inc(S("lru_half"), 1)
                    else:
                        used(ins)
            sum_squares("post0", "rms_post0")

            sum_squares("pre1", "rms_pre1")

            def ret_blocks(h):
                b = RET + 12 * h
                turns = 3
                if h == 0:
                    for j in range(4):
                        used(project(b + j, fresh=None if j else SPLITS["ret_h"]))
                    b, turns = b + 4, 2
                with pe.Fori(0, turns) as turn:
                    for j in range(4):
                        used(project(b + j, turn=turn))

            def attend(h):
                q, k_tiles, v_tiles, _ = ret_tiles(h)
                pe.wait_ge(S("rotated"), 4 * (h + 1))
                for k in range(2):
                    x = job_open(pe, ("rk_turn", h, k))
                    for c in range(4):
                        cols = slice(P * c, P * c + P)
                        ins = turn_over(x[:, cols], k_tiles[:, k, cols])
                    job_full(ins, ("rk_turn", h, k))
                for v in range(4):
                    x = job_open(pe, ("rv_turn", h, v))
                    if v == 0:
                        evacuated(pe, RET + 12 * h + 6)
                        evacuated(pe, RET + 12 * h + 7)
                    for c in range(4):
                        cols = slice(P * c, P * c + P)
                        ins = turn_over(x[:, cols], v_tiles[:, v, cols])
                    job_full(ins, ("rv_turn", h, v))
                x = job_open(pe, ("r_score", h))
                for c in range(4):
                    cols = slice(P * c, P * c + P)
                    for k in range(2):
                        ins = MM(x[:, cols], k_tiles[:, k, cols], q[:, k, cols], start=(k == 0), stop=(k == 1))
                job_full(ins, ("r_score", h))
                outs = [job_open(pe, ("r_out", h, v)) for v in range(4)]
                evacuated_job(pe, ("r_score", h))
                pe.wait_ge(S("rq_ready"), 2 * (h + 1))
                for v in range(4):
                    evacuated_job(pe, ("rv_turn", h, v))
                for k in range(2):
                    evacuated_job(pe, ("rk_turn", h, k))
                for c in range(4):
                    cols = slice(P * c, P * c + P)
                    for v in range(4):
                        vs = slice(P * v, P * v + P)
                        ins = MM(outs[v][:, cols], r_vtok[:, c, vs], r_scores[:, cols], start=True, stop=(c == 0))
                        if c:
                            if v == 0:
                                for k in range(2):
                                    evacuated_job(pe, ("r_state", h, c - 1, k))
                            for k in range(2):
                                ins = MM(outs[v][:, cols], r_state[:, k, vs], r_qd[:, k, cols], start=False,
                                         stop=(k == 1))
                        if c == 3:
                            job_full(ins, ("r_out", h, v))
                    if c < 3:
                        for k in range(2):
                            x = job_open(pe, ("r_state", h, c, k))
                            job_full(MM(x, r_ktok[:, k, c, :], r_vtok[:, c, :], start=True, stop=True),
                                     ("r_state", h, c, k))
                x = job_open(pe, ("r_mean", h))
                for v in range(4):
                    evacuated_job(pe, ("r_out", h, v))
                    ins = MM(x, C("ones"), hg[:, 4 * h + v, :], start=(v == 0), stop=(v == 3))
                job_full(ins, ("r_mean", h))
                sum_squares(("ret", h), ("r_var", h), 4)

            ret_blocks(0)
            ret_blocks(1)
            attend(0)
            ret_blocks(2)
            attend(1)
            ret_blocks(3)
            attend(2)
            for m in range(KT):
                if m == 0:
                    pe.wait_ge(split_lo, SPLITS["ret_y"] + 8)
                used(project(RET_OUT + m))
            attend(3)
            for m in range(KT):
                used(project(RET_OUT + KT + m, tiles=(8, 9, 10, 11, 0, 1, 2, 3),
                             fresh=None if m else SPLITS["ret_y"] + 8))
            sum_squares("post1", "rms_post1")


def lay_out(inputs):
    a = {k: np.asarray(v) for k, v in inputs.items()}
    col = lambda v: v.reshape(-1, P).T
    x_t = np.ascontiguousarray(a["x"][0].T).reshape(KT, P, T)
    mats = {"w_in": a["w_in"], "v_down": np.concatenate([a["rw_v_down"]] * 4, 2), "b_hg": a["w_branch_hg"],
            "b_rw": a["w_branch_rw"], "w_out": a["w_out"], "lru_in": a["lru_w_in_2"], "lru_out": a["lru_w_out_2"],
            "ret_in": a["ret_w_in_2"], "ret_out": a["ret_w_out_2"]}
    _, pieces = block_plan()
    wall = np.stack([np.concatenate([mats[n][l, r:r + P, c:c + P] for n, l, r, c in b], 1) for b in pieces])
    v = {"c": col(a["c"][0]), "v0": col(a["rw_v0"][0])}
    for l in range(DEPTH):
        for name, key in (("b_ada", "b_ada"), ("lb", "hg_lower_bounds"), ("hg_g", "hg_norm_g"), ("w0", "rw_w0"),
                          ("a0", "rw_a0"), ("k_k", "rw_k_k"), ("k_a", "rw_k_a"), ("r_k", "rw_r_k"),
                          ("gn_g", "rw_gn_g"), ("gn_b", "rw_gn_b"), ("ln_g", "ln_g"), ("ln_b", "ln_b")):
            v[f"{name}{l}"] = col(a[key][l].reshape(-1))
        mu = col(a["rw_mu"][l])
        v[f"mu{l}"] = np.concatenate([mu[:, 16:17], mu[:, 0:16]], 1)
        v[f"pre{l}"], v[f"post{l}"] = col(a["norm_pre_2"][l]), col(a["norm_post_2"][l])
    v["conv_w"] = np.concatenate([col(a["lru_conv_w_2"][0, k]) for k in range(4)], 1)
    for name, key in (("conv_b", "lru_conv_b_2"), ("b_a", "lru_b_a_2"), ("b_x", "lru_b_x_2"), ("lam", "lru_lambda_2")):
        v[name] = col(a[key][0])
    vec = np.concatenate([v[n] for n, _ in VECTORS], 1)
    up = np.concatenate([a["rw_w_up"], a["rw_a_up"]], 1)
    const, tables = constants()
    gates = np.zeros((2, 4, 384, 384), np.float32)
    for n in range(16):
        g, o = n // 4, 96 * (n % 4)
        gates[0, g, o:o + 96, o:o + 96] = a["lru_w_a_2"][0, n]
        gates[1, g, o:o + 96, o:o + 96] = a["lru_w_x_2"][0, n]
    tiles = [gates[w, g, P * i:P * i + P, P * o:P * o + P] for g in range(4) for w in range(2) for o, i in BAND]
    return {"x_t": x_t, "wall": wall, "w_ada": a["w_ada"].reshape(DEPTH, KT, P, ADA), "vec": vec, "up": up,
            "v_up": a["rw_v_up"][0], "const": const, "tables": tables,
            "lru_gates": np.concatenate(tiles, 1).reshape(P, 4, 14 * P)}


def kernel(**inputs):
    import concourse.bacc as bacc
    from concourse.bass_utils import run_bass_kernel_spmd as run

    arrays = {k: np.ascontiguousarray(v) for k, v in lay_out(inputs).items()}
    nc = bacc.Bacc("TRN2", target_bir_lowering=False, num_devices=1)
    build(nc, {k: v.shape for k, v in arrays.items()})
    got = run(nc, [arrays], core_ids=[0]).results[0]["out"]
    return np.ascontiguousarray(got.reshape(D, T).T)[None]
```
